# Optimizing a Trainium2 kernel written in Bass

```python
import jax, jax.numpy as jnp
from jax import lax
import numpy as np
import math

D_MODEL = 1024
BATCH = 1
SEQ = 512
DEPTH = 1

D_MIX = D_MODEL
HEAD_DIM = 64
ATTN_WIDTH = D_MIX // 2
CONV_WIDTH = D_MIX - ATTN_WIDTH
N_HEADS = ATTN_WIDTH // HEAD_DIM
N_KV_HEADS = 2
GQA_GROUP = N_HEADS // N_KV_HEADS
KV_WIDTH = N_KV_HEADS * HEAD_DIM
N_CONV_GROUPS = CONV_WIDTH // HEAD_DIM
WINDOW = 128
CONV_K = 3
IN_WIDTH = ATTN_WIDTH + 2 * KV_WIDTH + 3 * CONV_WIDTH
N_KEYS = 128
N_EXPERTS = N_KEYS * N_KEYS
PEER_HEADS = 8
PEER_TOPK = 16
D_KEY = 256
D_HALF = D_KEY // 2
PEER_CHUNK = 128
EPS = 1e-6
NEG = -1e30


def rms_norm(x, g):
    x32 = x.astype(jnp.float32)
    y = x32 * lax.rsqrt(jnp.mean(x32 * x32, axis=-1, keepdims=True) + EPS)
    return (y * g.astype(jnp.float32)).astype(x.dtype)

def head_rms_norm(x, g, n_groups):
    shp = x.shape
    xh = x.reshape(shp[:-1] + (n_groups, HEAD_DIM))
    y = rms_norm(xh, g.reshape(n_groups, HEAD_DIM))
    return y.reshape(shp)

def modulate(h, shift, scale):
    return h * (1 + scale[:, None, :]) + shift[:, None, :]

def sliding_window_sink_attention(q, k, v, sinks):
    bsz, s_len = q.shape[0], q.shape[1]
    nb = s_len // WINDOW
    qb = q.reshape(bsz, nb, WINDOW, N_KV_HEADS, GQA_GROUP, HEAD_DIM)
    kb = k.reshape(bsz, nb, WINDOW, N_KV_HEADS, HEAD_DIM)
    vb = v.reshape(bsz, nb, WINDOW, N_KV_HEADS, HEAD_DIM)

    def with_prev(t):
        prev = jnp.pad(t[:, :-1], ((0, 0), (1, 0), (0, 0), (0, 0), (0, 0)))
        return jnp.concatenate([prev, t], axis=2)

    kk, vv = with_prev(kb), with_prev(vb)
    s = jnp.einsum('bnqkgd,bnjkd->bnkgqj', qb, kk).astype(jnp.float32) * (HEAD_DIM ** -0.5)
    qi = jnp.arange(WINDOW)[:, None]
    kj = jnp.arange(2 * WINDOW)[None, :]
    diff = qi + WINDOW - kj
    rel_ok = (diff >= 0) & (diff < WINDOW)
    blk = jnp.arange(nb)[:, None, None]
    valid = rel_ok[None] & ((blk > 0) | (kj[None] >= WINDOW))
    s = jnp.where(valid[None, :, None, None], s, NEG)
    sink = sinks.astype(jnp.float32).reshape(N_KV_HEADS, GQA_GROUP)[None, None, :, :, None, None]
    m = jnp.maximum(jnp.max(s, axis=-1, keepdims=True), sink)
    e = jnp.exp(s - m)
    p = e / (jnp.sum(e, axis=-1, keepdims=True) + jnp.exp(sink - m))
    o = jnp.einsum('bnkgqj,bnjkd->bnqkgd', p.astype(v.dtype), vv)
    return o.reshape(bsz, s_len, ATTN_WIDTH)

def short_gated_conv(b_gate, c_gate, u, conv_w):
    z = c_gate * u
    zp = jnp.pad(z, ((0, 0), (CONV_K - 1, 0), (0, 0)))
    s_len = z.shape[1]
    conv = zp[:, 0:s_len] * conv_w[0] + zp[:, 1:s_len + 1] * conv_w[1] + zp[:, 2:s_len + 2] * conv_w[2]
    return b_gate * conv

def peer_layer(h, w_query, peer_keys1, peer_keys2, peer_u, peer_v):
    bsz, s_len, d = h.shape
    t = bsz * s_len
    hf = h.reshape(t, d)
    q = (hf @ w_query).reshape(t, PEER_HEADS, D_KEY)
    s1 = jnp.einsum('thd,hnd->thn', q[..., :D_HALF], peer_keys1).astype(jnp.float32)
    s2 = jnp.einsum('thd,hnd->thn', q[..., D_HALF:], peer_keys2).astype(jnp.float32)
    v1, i1 = lax.top_k(s1, PEER_TOPK)
    v2, i2 = lax.top_k(s2, PEER_TOPK)
    cand = (v1[..., :, None] + v2[..., None, :]).reshape(t, PEER_HEADS, PEER_TOPK * PEER_TOPK)
    sc, ci = lax.top_k(cand, PEER_TOPK)
    e1 = jnp.take_along_axis(i1, ci // PEER_TOPK, axis=-1)
    e2 = jnp.take_along_axis(i2, ci % PEER_TOPK, axis=-1)
    idx = e1 * N_KEYS + e2
    gates = jax.nn.softmax(sc, axis=-1).astype(h.dtype)

    nchunk = t // PEER_CHUNK
    hc = hf.reshape(nchunk, PEER_CHUNK, d)
    ic = idx.reshape(nchunk, PEER_CHUNK, PEER_HEADS, PEER_TOPK)
    gc = gates.reshape(nchunk, PEER_CHUNK, PEER_HEADS, PEER_TOPK)

    def chunk_fn(args):
        hx, ix, gx = args
        u = peer_u[ix]
        a = jax.nn.gelu(jnp.einsum('td,thkd->thk', hx, u), approximate=False)
        vsel = peer_v[ix]
        return jnp.einsum('thk,thkd->td', gx * a, vsel)

    out = lax.map(chunk_fn, (hc, ic, gc))
    return out.reshape(bsz, s_len, d)

def first_inputs(seed: int = 0) -> dict:
    key = jax.random.key(seed)
    ks = jax.random.split(key, 20)
    D = D_MODEL
    f32 = jnp.float32
    return {
        "x": jax.random.normal(ks[0], (BATCH, SEQ, D), f32),
        "c": jax.random.normal(ks[1], (BATCH, D), f32),
        "w_ada": jax.random.normal(ks[2], (D, 6 * D), f32) * D ** -0.5,
        "b_ada": jax.random.normal(ks[3], (6 * D,), f32) * 0.02,
        "norm1_g": 1.0 + 0.02 * jax.random.normal(ks[4], (D,), f32),
        "w_in": jax.random.normal(ks[5], (D, IN_WIDTH), f32) * D ** -0.5,
        "b_in": jax.random.normal(ks[6], (IN_WIDTH,), f32) * 0.02,
        "attn_sinks": jax.random.normal(ks[7], (N_HEADS,), f32) * 0.5,
        "conv_w": jax.random.normal(ks[8], (CONV_K, CONV_WIDTH), f32) * CONV_K ** -0.5,
        "attn_out_g": 1.0 + 0.02 * jax.random.normal(ks[9], (ATTN_WIDTH,), f32),
        "conv_out_g": 1.0 + 0.02 * jax.random.normal(ks[10], (CONV_WIDTH,), f32),
        "w_out": jax.random.normal(ks[11], (D_MIX, D), f32) * D_MIX ** -0.5,
        "b_out": jax.random.normal(ks[12], (D,), f32) * 0.02,
        "norm2_g": 1.0 + 0.02 * jax.random.normal(ks[13], (D,), f32),
        "w_query": jax.random.normal(ks[14], (D, PEER_HEADS * D_KEY), f32) * D ** -0.5,
        "peer_keys1": jax.random.normal(ks[15], (PEER_HEADS, N_KEYS, D_HALF), f32) * D_HALF ** -0.5,
        "peer_keys2": jax.random.normal(ks[16], (PEER_HEADS, N_KEYS, D_HALF), f32) * D_HALF ** -0.5,
        "peer_u": jax.random.normal(ks[17], (N_EXPERTS, D), f32) * D ** -0.5,
        "peer_v": jax.random.normal(ks[18], (N_EXPERTS, D), f32) * PEER_HEADS ** -0.5,
        "final_g": 1.0 + 0.02 * jax.random.normal(ks[19], (D,), f32),
    }

def first_block(x, c, w_ada, b_ada, norm1_g, w_in, b_in, attn_sinks, conv_w, attn_out_g,
              conv_out_g, w_out, b_out, norm2_g, w_query, peer_keys1, peer_keys2,
              peer_u, peer_v, final_g):
    bsz, s_len, _ = x.shape
    for _layer in range(DEPTH):
        ada = jax.nn.silu(c) @ w_ada + b_ada
        shift1, scale1, gate1, shift2, scale2, gate2 = jnp.split(ada, 6, axis=-1)

        h = modulate(rms_norm(x, norm1_g), shift1, scale1)
        proj = h @ w_in + b_in
        o1 = ATTN_WIDTH
        o2 = o1 + KV_WIDTH
        o3 = o2 + KV_WIDTH
        o4 = o3 + CONV_WIDTH
        o5 = o4 + CONV_WIDTH
        q = proj[..., :o1].reshape(bsz, s_len, N_HEADS, HEAD_DIM)
        k = proj[..., o1:o2].reshape(bsz, s_len, N_KV_HEADS, HEAD_DIM)
        v = proj[..., o2:o3].reshape(bsz, s_len, N_KV_HEADS, HEAD_DIM)
        b_gate = proj[..., o3:o4]
        c_gate = proj[..., o4:o5]
        u_conv = proj[..., o5:]
        attn = head_rms_norm(sliding_window_sink_attention(q, k, v, attn_sinks), attn_out_g, N_HEADS)
        conv = head_rms_norm(short_gated_conv(b_gate, c_gate, u_conv, conv_w), conv_out_g, N_CONV_GROUPS)
        mix = jnp.concatenate([attn, conv], axis=-1) @ w_out + b_out
        x = x + gate1[:, None, :] * mix

        h2 = modulate(rms_norm(x, norm2_g), shift2, scale2)
        x = x + gate2[:, None, :] * peer_layer(h2, w_query, peer_keys1, peer_keys2, peer_u, peer_v)
    return rms_norm(x, final_g)


GRID_W = 64
F32 = jnp.float32
HY_WIDTH = D_MODEL // 4
NA_HEAD_DIM = 64
NA_WIDTH = D_MODEL // 2
NA_HEADS = NA_WIDTH // NA_HEAD_DIM
POOL_WIDTH = D_MODEL // 4
POOL_WINDOWS = (2, 4, 8, 16)
POOL_GROUPS = len(POOL_WINDOWS)
POOL_GROUP_DIM = POOL_WIDTH // POOL_GROUPS
IN_WIDTH_2 = 3 * HY_WIDTH + 3 * NA_WIDTH + POOL_WIDTH
SHORT_CONV = 3
FILTER_EMB = 33
FILTER_BANDS = (FILTER_EMB - 1) // 2
FILTER_HIDDEN = 64
DECAY_FAST = 0.3
DECAY_SLOW = 1.5
DECAY_TARGET = 1e-2
NA_KH_MAX = 8
NA_KW = 16
N_EXPERTS_2 = 16
EC_CAPACITY = 2
EXPERT_FF = 2 * D_MODEL


def rms_norm_2(x, g):
    xf = x.astype(F32)
    y = xf * lax.rsqrt(jnp.mean(xf * xf, axis=-1, keepdims=True) + EPS)
    return (y * g.astype(F32)).astype(x.dtype)

def short_conv(u, w, b):
    up = jnp.pad(u, ((0, 0), (1, 1), (0, 0)))
    return up[:, :-2] * w[0] + up[:, 1:-1] * w[1] + up[:, 2:] * w[2] + b

def hyena_filter(L, w1, b1, w2, b2, w_out, freq):
    t = jnp.linspace(0.0, 1.0, L, dtype=F32)[:, None]
    ang = 2.0 * math.pi * jnp.arange(L, dtype=F32)[:, None] / L
    f = jnp.linspace(1e-4, FILTER_BANDS - 1, FILTER_BANDS, dtype=F32)[None, :]
    z = jnp.concatenate([t, jnp.cos(f * ang), -jnp.sin(f * ang)], axis=-1)
    fr = freq.astype(F32)
    h = jnp.sin(fr * (z @ w1.astype(F32) + b1.astype(F32)))
    h = jnp.sin(fr * (h @ w2.astype(F32) + b2.astype(F32)))
    h = h @ w_out.astype(F32)
    deltas = jnp.abs(jnp.linspace(math.log(DECAY_TARGET) / DECAY_FAST,
                                  math.log(DECAY_TARGET) / DECAY_SLOW, HY_WIDTH, dtype=F32))
    decay = jnp.exp(-t * deltas)
    h = h * jnp.concatenate([decay, decay], axis=-1)
    h_fwd, h_bwd = h[:, :HY_WIDTH], h[:, HY_WIDTH:]
    return jnp.concatenate([h_fwd, jnp.zeros((1, HY_WIDTH), F32), h_bwd[1:][::-1]], axis=0)

def hyena_mixer(u, sw, sb, filt, skip):
    u = short_conv(u, sw, sb)
    x0, x1, v = jnp.split(u, 3, axis=-1)
    z = (v * x1).astype(F32)
    L = z.shape[1]
    Z = jnp.fft.rfft(z, n=2 * L, axis=1)
    Hf = jnp.fft.rfft(filt, n=2 * L, axis=0)
    y = jnp.fft.irfft(Z * Hf[None], n=2 * L, axis=1)[:, :L]
    y = y + z * skip.astype(F32)
    return y.astype(u.dtype) * x0

def neighbourhood_attention(q, k, v, rpb):
    B, L, _ = q.shape
    rows = L // GRID_W
    kh = min(NA_KH_MAX, rows)
    shp = (B, rows, GRID_W, NA_HEADS, NA_HEAD_DIM)
    qg = (q * (NA_HEAD_DIM ** -0.5)).reshape(shp).transpose(1, 0, 2, 3, 4)
    kg = k.reshape(shp)
    vg = v.reshape(shp)
    cols = jnp.arange(GRID_W)
    col_start = jnp.clip(cols - NA_KW // 2, 0, GRID_W - NA_KW)
    col_idx = col_start[:, None] + jnp.arange(NA_KW)[None, :]
    dc_idx = col_idx - cols[:, None] + NA_KW - 1

    def one_row(args):
        q_row, r = args
        rs = jnp.clip(r - kh // 2, 0, rows - kh)
        k_nb = lax.dynamic_slice_in_dim(kg, rs, kh, axis=1)[:, :, col_idx]
        v_nb = lax.dynamic_slice_in_dim(vg, rs, kh, axis=1)[:, :, col_idx]
        s = jnp.einsum('bchd,bicjhd->bhcij', q_row, k_nb).astype(F32)
        dr_idx = rs + jnp.arange(kh) - r + NA_KH_MAX - 1
        bias = rpb[:, dr_idx][:, :, dc_idx].transpose(0, 2, 1, 3)
        s = s + bias.astype(F32)[None]
        p = jax.nn.softmax(s.reshape(B, NA_HEADS, GRID_W, kh * NA_KW), axis=-1)
        p = p.reshape(s.shape).astype(v_nb.dtype)
        return jnp.einsum('bhcij,bicjhd->bchd', p, v_nb)

    out = lax.map(one_row, (qg, jnp.arange(rows)))
    return out.transpose(1, 0, 2, 3, 4).reshape(B, L, NA_WIDTH)

def pool_mixer(u, pool_w, pool_scale):
    B, L, _ = u.shape
    ug = u.reshape(B, L, POOL_GROUPS, POOL_GROUP_DIM).astype(F32)
    S = jnp.concatenate([jnp.zeros((B, 1, POOL_GROUPS, POOL_GROUP_DIM), F32),
                         jnp.cumsum(ug, axis=1)], axis=1)
    t = jnp.arange(L)
    means = []
    for g, w in enumerate(POOL_WINDOWS):
        lo = jnp.clip(t - w // 2, 0, L)
        hi = jnp.clip(t + w // 2, 0, L)
        cnt = (hi - lo).astype(F32)[None, :, None]
        means.append((S[:, hi, g] - S[:, lo, g]) / cnt)
    pooled = jnp.stack(means, axis=2) - ug
    y = jnp.einsum('blgc,gcd->blgd', pooled, pool_w.astype(F32)).reshape(B, L, POOL_WIDTH)
    return (y * pool_scale.astype(F32)).astype(u.dtype)

def expert_choice_moe(h, w_router, w_gate, w_up, w_down):
    B, L, D = h.shape
    cap = EC_CAPACITY * L // N_EXPERTS_2
    aff = jax.nn.softmax(h.astype(F32) @ w_router.astype(F32), axis=-1)
    gate, idx = lax.top_k(aff.transpose(0, 2, 1), cap)
    xs = jax.vmap(lambda hb, ib: hb[ib])(h, idx)
    a = jnp.einsum('becd,edf->becf', xs, w_gate)
    b = jnp.einsum('becd,edf->becf', xs, w_up)
    y = jnp.einsum('becf,efd->becd', jax.nn.silu(a) * b, w_down)
    y = y * gate.astype(y.dtype)[..., None]
    return jax.vmap(lambda yb, ib: jnp.zeros((L, D), yb.dtype).at[ib.reshape(-1)].add(
        yb.reshape(-1, D)))(y, idx)

def second_inputs(seed: int = 0) -> dict:
    key = jax.random.key(seed)
    ks = jax.random.split(key, 24)
    n = lambda k, s, sc: jax.random.normal(k, s, F32) * sc
    gain = lambda k, s: 1.0 + 0.02 * jax.random.normal(k, s, F32)
    L_ = DEPTH
    return {
        'x': jax.random.normal(ks[0], (BATCH, SEQ, D_MODEL), F32),
        'norm1_g': gain(ks[1], (L_, D_MODEL)),
        'w_in': n(ks[2], (L_, D_MODEL, IN_WIDTH_2), D_MODEL ** -0.5),
        'hy_short_w': n(ks[3], (L_, SHORT_CONV, 3 * HY_WIDTH), SHORT_CONV ** -0.5),
        'hy_short_b': n(ks[4], (L_, 3 * HY_WIDTH), 0.02),
        'hy_f_w1': n(ks[5], (L_, FILTER_EMB, FILTER_HIDDEN), FILTER_EMB ** -0.5),
        'hy_f_b1': n(ks[6], (L_, FILTER_HIDDEN), 0.02),
        'hy_f_w2': n(ks[7], (L_, FILTER_HIDDEN, FILTER_HIDDEN), FILTER_HIDDEN ** -0.5),
        'hy_f_b2': n(ks[8], (L_, FILTER_HIDDEN), 0.02),
        'hy_f_wout': n(ks[9], (L_, FILTER_HIDDEN, 2 * HY_WIDTH), FILTER_HIDDEN ** -0.5),
        'hy_f_freq': gain(ks[10], (L_, FILTER_HIDDEN)),
        'hy_skip': n(ks[11], (L_, HY_WIDTH), 1.0),
        'na_rpb': n(ks[12], (L_, NA_HEADS, 2 * NA_KH_MAX - 1, 2 * NA_KW - 1), 0.02),
        'pool_w': n(ks[13], (L_, POOL_GROUPS, POOL_GROUP_DIM, POOL_GROUP_DIM), POOL_GROUP_DIM ** -0.5),
        'pool_scale': 1.0 + 0.1 * jax.random.normal(ks[14], (L_, POOL_WIDTH), F32),
        'mix_norm_g': gain(ks[15], (L_, D_MODEL)),
        'w_out': n(ks[16], (L_, D_MODEL, D_MODEL), D_MODEL ** -0.5),
        'norm2_g': gain(ks[17], (L_, D_MODEL)),
        'w_router': n(ks[18], (L_, D_MODEL, N_EXPERTS_2), D_MODEL ** -0.5),
        'w_gate': n(ks[19], (L_, N_EXPERTS_2, D_MODEL, EXPERT_FF), D_MODEL ** -0.5),
        'w_up': n(ks[20], (L_, N_EXPERTS_2, D_MODEL, EXPERT_FF), D_MODEL ** -0.5),
        'w_down': n(ks[21], (L_, N_EXPERTS_2, EXPERT_FF, D_MODEL), EXPERT_FF ** -0.5),
        'final_g': gain(ks[22], (D_MODEL,)),
    }

def second_block(x, norm1_g, w_in, hy_short_w, hy_short_b, hy_f_w1, hy_f_b1, hy_f_w2, hy_f_b2,
              hy_f_wout, hy_f_freq, hy_skip, na_rpb, pool_w, pool_scale, mix_norm_g, w_out,
              norm2_g, w_router, w_gate, w_up, w_down, final_g):
    L = x.shape[1]
    cuts = [3 * HY_WIDTH, 3 * HY_WIDTH + NA_WIDTH, 3 * HY_WIDTH + 2 * NA_WIDTH,
            3 * HY_WIDTH + 3 * NA_WIDTH]
    for i in range(DEPTH):
        h = rms_norm_2(x, norm1_g[i])
        proj = h @ w_in[i]
        hy_in, q, k, v, pool_in = jnp.split(proj, cuts, axis=-1)
        filt = hyena_filter(L, hy_f_w1[i], hy_f_b1[i], hy_f_w2[i], hy_f_b2[i],
                            hy_f_wout[i], hy_f_freq[i])
        y_hy = hyena_mixer(hy_in, hy_short_w[i], hy_short_b[i], filt, hy_skip[i])
        y_na = neighbourhood_attention(q, k, v, na_rpb[i])
        y_pool = pool_mixer(pool_in, pool_w[i], pool_scale[i])
        g = mix_norm_g[i]
        mixed = jnp.concatenate([
            rms_norm_2(y_hy, g[:HY_WIDTH]),
            rms_norm_2(y_na, g[HY_WIDTH:HY_WIDTH + NA_WIDTH]),
            rms_norm_2(y_pool, g[HY_WIDTH + NA_WIDTH:])], axis=-1)
        x = x + mixed @ w_out[i]
        x = x + expert_choice_moe(rms_norm_2(x, norm2_g[i]), w_router[i], w_gate[i],
                                  w_up[i], w_down[i])
    return rms_norm_2(x, final_g)


def setup_inputs(seed=0):
    out = dict(first_inputs(seed))
    for name, value in second_inputs(seed + 1).items():
        if name != "x":
            out[name + "_2"] = value
    return out


def reference(
    x, c, w_ada, b_ada, norm1_g, w_in, b_in, attn_sinks, conv_w, attn_out_g, conv_out_g, w_out,
    b_out, norm2_g, w_query, peer_keys1, peer_keys2, peer_u, peer_v, final_g, norm1_g_2, w_in_2,
    hy_short_w_2, hy_short_b_2, hy_f_w1_2, hy_f_b1_2, hy_f_w2_2, hy_f_b2_2, hy_f_wout_2,
    hy_f_freq_2, hy_skip_2, na_rpb_2, pool_w_2, pool_scale_2, mix_norm_g_2, w_out_2, norm2_g_2,
    w_router_2, w_gate_2, w_up_2, w_down_2, final_g_2,
):
    x = first_block(
        x, c, w_ada, b_ada, norm1_g, w_in, b_in, attn_sinks, conv_w, attn_out_g, conv_out_g,
        w_out, b_out, norm2_g, w_query, peer_keys1, peer_keys2, peer_u, peer_v, final_g,
    )
    return second_block(
        x, norm1_g_2, w_in_2, hy_short_w_2, hy_short_b_2, hy_f_w1_2, hy_f_b1_2, hy_f_w2_2,
        hy_f_b2_2, hy_f_wout_2, hy_f_freq_2, hy_skip_2, na_rpb_2, pool_w_2, pool_scale_2,
        mix_norm_g_2, w_out_2, norm2_g_2, w_router_2, w_gate_2, w_up_2, w_down_2, final_g_2,
    )


_drawn_inputs = setup_inputs


def setup_inputs(seed=0):
    import zlib

    import numpy as np

    out = dict(_drawn_inputs(seed))
    spreads = {}
    factors = {'attn_sinks': 64.0,
     'attn_out_g': 3.065,
     'conv_out_g': 3.553,
     'norm2_g': 2.739,
     'norm1_g_2': 2.71,
     'hy_short_b_2': 2.717,
     'hy_f_b1_2': 3.338,
     'hy_f_b2_2': 3.04,
     'hy_f_freq_2': 5.482,
     'na_rpb_2': 7.916,
     'mix_norm_g_2': 3.263,
     'norm2_g_2': 4.824,
     'final_g_2': 8.749}
    for name, (base, spread) in spreads.items():
        noise = np.random.default_rng([zlib.crc32(name.encode()), seed]).standard_normal(out[name].shape)
        drawn = base * np.exp(spread * noise) if base else spread * noise
        out[name] = __import__('jax').numpy.asarray(drawn.astype(out[name].dtype))
    for name, factor in factors.items():
        out[name] = (out[name] * factor).astype(out[name].dtype)
    return out
```

```python
from contextlib import ExitStack

import concourse.bass as bass
import numpy as np
from concourse import mybir

F32 = mybir.dt.float32
U32 = mybir.dt.uint32
I32 = mybir.dt.int32
ALU = mybir.AluOpType
ACT = mybir.ActivationFunctionType
AX = mybir.AxisListType

P = 128
T = 512
NT = T // P
D = 1024
KD = D // P
DH = 64
NH = 8
BANK = 512
EPS = 1e-6
NEG = -1e30
LOWEST = -3.0e38

NKEY = 128
PH = 8
PK = 16
NC = 2 * PH
ETILES = NKEY
GROUP = 8

NE = 16
CAP = 64
FF = 2048
NPAIR = NE // 2


class Steps:

    def __init__(self, eng, sem, base=0):
        self.eng, self.sem, self.base, self.n = eng, sem, base, 0

    def __call__(self, ins):
        ins.then_inc(self.sem, 1)
        self.n += 1
        self.eng.wait_ge(self.sem, self.base + self.n)


class Scope(ExitStack):

    def __init__(self, nc, name):
        super().__init__()
        self.nc, self.name, self.sems = nc, name, []
        self.callback(self.free_semaphores)

    def free_semaphores(self):
        for sem in self.sems:
            self.nc.gpsimd.sem_clear(sem)
            self.nc.release_semaphore(sem)

    def sb(self, name, shape, dt=F32):
        return self.enter_context(self.nc.sbuf_tensor(f"{self.name}_{name}", shape, dt))

    def ps(self, name, shape, dt=F32):
        return self.enter_context(self.nc.psum_tensor(f"{self.name}_{name}", shape, dt))

    def sem(self, name):
        self.sems.append(self.nc.alloc_semaphore(f"{self.name}_{name}"))
        return self.sems[-1]


def rows(vector_dram, n):
    return vector_dram.partition_broadcast(n)


def weight_tiles(w_dram):
    return w_dram.rearrange("(k p) n -> p k n", p=P)



def norm_phase(nc, name, ident, x, g_dram, width=D, groups=1, scale=None, shift=None,
               keep=None, to_t=None, t_chunk0=0, out_dram=None):
    gw = width // groups
    chunks = width // P
    with Scope(nc, name) as s:
        g_rows = s.sb("g_rows", [P, width])
        square = s.sb("square", [P, 2, width])
        h = s.sb("h", [P, NT, width]) if keep is None else keep
        mean = s.sb("mean", [P, NT * groups])
        root = s.sb("root", [P, NT * groups])
        rstd = s.sb("rstd", [P, NT * groups])
        per_bank = min(chunks, 4)
        n_banks = chunks // per_bank
        turned = s.ps("turned", [P, NT * n_banks, 4, P])
        g_loaded, squared, sq_summed, mean_ready, root_ready = (s.sem(n) for n in (
            "g_loaded", "squared", "sq_summed", "mean_ready", "root_ready"))
        dve_step, h_ready, turn_done, stored = (s.sem(n) for n in (
            "dve_step", "h_ready", "turn_done", "stored"))
        with nc.Block() as block:
            @block.sync
            def _(sp):
                sp.dma_start(g_rows[:], rows(g_dram, P)).then_inc(g_loaded, 16)
                if out_dram is not None:
                    for t in range(NT):
                        sp.wait_ge(h_ready, t + 1)
                        sp.dma_start(out_dram[t * P:(t + 1) * P, :], h[:, t, :]).then_inc(stored, 16)
                    sp.wait_ge(stored, 16 * NT)

            @block.scalar
            def _(act):
                for t in range(NT):
                    if t >= 2:
                        act.wait_ge(sq_summed, t - 1)
                    nc.scalar.activation(square[:, t % 2, :], x[:, t, :], ACT.Square).then_inc(squared, 1)
                act.wait_ge(mean_ready, 1)
                nc.scalar.activation(root[:], mean[:], ACT.Sqrt).then_inc(root_ready, 1)
                if to_t is not None:
                    for b in range(NT * n_banks):
                        t, half = b // n_banks, b % n_banks
                        act.wait_ge(turn_done, b + 1)
                        c0 = t_chunk0 + half * per_bank
                        nc.scalar.copy(to_t[:, c0:c0 + per_bank, t * P:(t + 1) * P],
                                       turned[:, b, 0:per_bank, :])

            @block.vector
            def _(dve):
                step = Steps(dve, dve_step)
                for t in range(NT):
                    dve.wait_ge(squared, t + 1)
                    ins = nc.vector.tensor_reduce(
                        mean[:, t * groups:(t + 1) * groups],
                        square[:, t % 2, :].rearrange("p (g w) -> p g w", g=groups), AX.X, ALU.add)
                    ins.then_inc(sq_summed, 1)
                dve.wait_ge(sq_summed, NT)
                nc.vector.tensor_scalar(mean[:], mean[:], 1.0 / gw, EPS, ALU.mult,
                                        ALU.add).then_inc(mean_ready, 1)
                dve.wait_ge(root_ready, 1)
                step(nc.vector.reciprocal(rstd[:], root[:]))
                dve.wait_ge(g_loaded, 16)
                for t in range(NT):
                    if groups == 1:
                        ins = nc.vector.scalar_tensor_tensor(
                            out=h[:, t, :], in0=x[:, t, :], scalar=rstd[:, t:t + 1], in1=g_rows[:],
                            op0=ALU.mult, op1=ALU.mult)
                    else:
                        r = rstd[:, t * groups:(t + 1) * groups].unsqueeze(2).to_broadcast([P, groups, gw])
                        step(nc.vector.tensor_tensor(
                            h[:, t, :].rearrange("p (g w) -> p g w", g=groups),
                            x[:, t, :].rearrange("p (g w) -> p g w", g=groups), r, ALU.mult))
                        ins = nc.vector.tensor_tensor(h[:, t, :], h[:, t, :], g_rows[:], ALU.mult)
                    if scale is not None:
                        step(ins)
                        step(nc.vector.scalar_tensor_tensor(out=h[:, t, :], in0=scale, scalar=1.0,
                                                            in1=h[:, t, :], op0=ALU.add, op1=ALU.mult))
                        ins = nc.vector.tensor_tensor(h[:, t, :], h[:, t, :], shift, ALU.add)
                    ins.then_inc(h_ready, 1)

            @block.tensor
            def _(pe):
                if to_t is None:
                    return
                for b in range(NT * n_banks):
                    t, half = b // n_banks, b % n_banks
                    pe.wait_ge(h_ready, t + 1)
                    for j in range(per_bank):
                        c = half * per_bank + j
                        last = nc.tensor.transpose(turned[:, b, j, :], h[:, t, c * P:(c + 1) * P], ident[:])
                    last.then_inc(turn_done, 1)



def product_phase(nc, name, chunks, n_slots, slot_width, extra_loads=()):
    outputs = [(n, o) for n, (_, outs) in enumerate(chunks) for o in outs]
    first = [sum(len(outs) for _, outs in chunks[:n]) for n in range(len(chunks) + 1)]
    with Scope(nc, name) as s:
        slots = s.sb("slots", [P, n_slots, KD, slot_width])
        banks = s.ps("banks", [P, 8, BANK])
        loaded = [s.sem(f"loaded{i}") for i in range(n_slots)]
        extra, product_done, act_taken, dve_taken, act_step, dve_step = (s.sem(n) for n in (
            "extra", "product_done", "act_taken", "dve_taken", "act_step", "dve_step"))
        landed = [0] * n_slots
        need = []
        for n, (loads, _) in enumerate(chunks):
            landed[n % n_slots] += 16 * len(loads(slots[:, n % n_slots]))
            need.append(landed[n % n_slots])
        with nc.Block() as block:
            @block.sync
            def _(sp):
                for to, src in extra_loads:
                    sp.dma_start(to, src).then_inc(extra, 16)
                for n, (loads, _) in enumerate(chunks):
                    if n >= n_slots:
                        sp.wait_ge(product_done, first[n - n_slots + 1])
                    for to, src in loads(slots[:, n % n_slots]):
                        sp.dma_start(to, src).then_inc(loaded[n % n_slots], 16)

            @block.tensor
            def _(pe):
                for o, (n, (m, width, operands, _)) in enumerate(outputs):
                    pe.wait_ge(loaded[n % n_slots], need[n])
                    if o >= 8:
                        pe.wait_ge(act_taken if o % 2 == 0 else dve_taken, (o - 8) // 2 + 1)
                    for k in range(KD):
                        lhsT, rhs = operands(slots[:, n % n_slots], k)
                        last = nc.tensor.matmul(banks[0:m, o % 8, 0:width], lhsT, rhs,
                                                start=(k == 0), stop=(k == KD - 1))
                    last.then_inc(product_done, 1)

            def takes(eng, nc_eng, parity, taken, step):
                eng.wait_ge(extra, 16 * len(extra_loads))
                for o, (n, (m, width, _, take)) in enumerate(outputs):
                    if o % 2 == parity:
                        eng.wait_ge(product_done, o + 1)
                        take(nc_eng, banks[0:m, o % 8, 0:width], step).then_inc(taken, 1)

            @block.scalar
            def _(act):
                takes(act, nc.scalar, 0, act_taken, Steps(act, act_step))

            @block.vector
            def _(dve):
                takes(dve, nc.vector, 1, dve_taken, Steps(dve, dve_step))


def copy_to(dst):
    def take(eng, bank, step):
        return eng.copy(dst, bank) if on_scalar(eng) else eng.tensor_copy(dst, bank)
    return take


def on_scalar(eng):
    return "activation" in dir(eng)


def add_column_to(dst, column):
    def take(eng, bank, step):
        if on_scalar(eng):
            return eng.activation(dst, bank, ACT.Identity, bias=column)
        return eng.tensor_scalar(dst, bank, column, None, ALU.add)
    return take



def attention_phase(nc, name, ident, units, q_of, k_of, v_of, bias_of, o_of, keys_max, sinks=None):
    n = len(units)
    chunks_max = keys_max // P
    with Scope(nc, name) as s:
        biased = s.sb("biased", [P, 2, keys_max])
        expd = s.sb("expd", [P, 2, keys_max])
        expd_t = s.sb("expd_t", [P, 2, chunks_max, P])
        top = s.sb("top", [P, n])
        minus_top = s.sb("minus_top", [P, n])
        total = s.sb("total", [P, n])
        sink_exp = s.sb("sink_exp", [P, n])
        total_inv = s.sb("total_inv", [P, n])
        score_ps = s.ps("score_ps", [P, 2, BANK])
        turn_ps = s.ps("turn_ps", [P, 2, 4, P])
        out_ps = s.ps("out_ps", [P, 2, BANK])
        scored, biased_ready, minus_ready, exp_ready, sink_ready, turned, turn_taken, weighed, out_taken = (
            s.sem(x) for x in ("scored", "biased_ready", "minus_ready", "exp_ready", "sink_ready",
                               "turned", "turn_taken", "weighed", "out_taken"))
        dve_step = s.sem("dve_step")
        with nc.Block() as block:
            @block.tensor
            def _(pe):
                for i in range(n + 2):
                    if i < n:
                        keys = k_of(*units[i])
                        if i >= 2:
                            pe.wait_ge(biased_ready, i - 1)
                        nc.tensor.matmul(score_ps[:, i % 2, 0:keys.shape[1]], q_of(*units[i]), keys,
                                         start=True, stop=True).then_inc(scored, 1)
                    if 1 <= i <= n:
                        j = i - 1
                        pe.wait_ge(exp_ready, j + 1)
                        if j >= 2:
                            pe.wait_ge(turn_taken, j - 1)
                        for c in range(k_of(*units[j]).shape[1] // P):
                            last = nc.tensor.transpose(turn_ps[:, j % 2, c, :],
                                                       expd[:, j % 2, c * P:(c + 1) * P], ident[:])
                        last.then_inc(turned, 1)
                    if i >= 2:
                        j = i - 2
                        pe.wait_ge(turn_taken, j + 1)
                        if j >= 2:
                            pe.wait_ge(out_taken, j - 1)
                        values = v_of(*units[j])
                        for c, v in enumerate(values):
                            last = nc.tensor.matmul(out_ps[:, j % 2, 0:DH], expd_t[:, j % 2, c, :], v,
                                                    start=(c == 0), stop=(c == len(values) - 1))
                        last.then_inc(weighed, 1)

            @block.scalar
            def _(act):
                for i in range(n + 1):
                    if i < n:
                        kw = k_of(*units[i]).shape[1]
                        act.wait_ge(minus_ready, i + 1)
                        if i >= 2:
                            act.wait_ge(turned, i - 1)
                        nc.scalar.activation(expd[:, i % 2, 0:kw], biased[:, i % 2, 0:kw], ACT.Exp,
                                             bias=minus_top[:, i:i + 1],
                                             accum_out=total[:, i:i + 1]).then_inc(exp_ready, 1)
                        if sinks is not None:
                            nc.scalar.activation(sink_exp[:, i:i + 1], sinks(*units[i]), ACT.Exp,
                                                 bias=minus_top[:, i:i + 1]).then_inc(sink_ready, 1)
                    if i >= 1:
                        j = i - 1
                        nch = k_of(*units[j]).shape[1] // P
                        act.wait_ge(turned, j + 1)
                        if j >= 2:
                            act.wait_ge(weighed, j - 1)
                        nc.scalar.copy(expd_t[:, j % 2, 0:nch, :],
                                       turn_ps[:, j % 2, 0:nch, :]).then_inc(turn_taken, 1)

            @block.vector
            def _(dve):
                step = Steps(dve, dve_step)
                for i in range(n + 2):
                    if i < n:
                        kw = k_of(*units[i]).shape[1]
                        dve.wait_ge(scored, i + 1)
                        if i >= 2:
                            dve.wait_ge(exp_ready, i - 1)
                        nc.vector.scalar_tensor_tensor(
                            out=biased[:, i % 2, 0:kw], in0=score_ps[:, i % 2, 0:kw], scalar=DH ** -0.5,
                            in1=bias_of(*units[i]), op0=ALU.mult, op1=ALU.add).then_inc(biased_ready, 1)
                        dve.wait_ge(biased_ready, i + 1)
                        step(nc.vector.reduce_max(top[:, i:i + 1], biased[:, i % 2, 0:kw], AX.X))
                        if sinks is not None:
                            step(nc.vector.tensor_tensor(top[:, i:i + 1], top[:, i:i + 1],
                                                         sinks(*units[i]), ALU.max))
                        nc.vector.tensor_scalar(minus_top[:, i:i + 1], top[:, i:i + 1], -1.0, None,
                                                ALU.mult).then_inc(minus_ready, 1)
                    if i >= 2:
                        j = i - 2
                        dve.wait_ge(exp_ready, j + 1)
                        if sinks is not None:
                            dve.wait_ge(sink_ready, j + 1)
                            step(nc.vector.tensor_tensor(total[:, j:j + 1], total[:, j:j + 1],
                                                         sink_exp[:, j:j + 1], ALU.add))
                        step(nc.vector.reciprocal(total_inv[:, j:j + 1], total[:, j:j + 1]))
                        dve.wait_ge(weighed, j + 1)
                        nc.vector.tensor_scalar(o_of(*units[j]), out_ps[:, j % 2, 0:DH],
                                                total_inv[:, j:j + 1], None,
                                                ALU.mult).then_inc(out_taken, 1)



def column_norm_phase(nc, name, jobs, ones_of, width):
    with Scope(nc, name) as s:
        n = len(jobs)
        most = max(len(j) for j in jobs)
        square = s.sb("square", [P, n, most, T])
        mean = s.sb("mean", [P, n, T])
        root = s.sb("root", [P, n, T])
        rstd = s.sb("rstd", [P, n, T])
        sum_ps = s.ps("sum_ps", [P, n, BANK])
        squared, summed, mean_ready, root_ready, dve_step = (s.sem(x) for x in (
            "squared", "summed", "mean_ready", "root_ready", "dve_step"))
        with nc.Block() as block:
            @block.scalar
            def _(act):
                for j, job in enumerate(jobs):
                    for m, (tile, _, _) in enumerate(job):
                        nc.scalar.activation(square[:, j, m, :], tile, ACT.Square).then_inc(squared, 1)
                for j in range(n):
                    act.wait_ge(mean_ready, j + 1)
                    nc.scalar.activation(root[:, j, :], mean[:, j, :], ACT.Sqrt).then_inc(root_ready, 1)

            @block.tensor
            def _(pe):
                done = 0
                for j, job in enumerate(jobs):
                    for m in range(len(job)):
                        done += 1
                        pe.wait_ge(squared, done)
                        last = nc.tensor.matmul(sum_ps[:, j, :], ones_of, square[:, j, m, :],
                                                start=(m == 0), stop=(m == len(job) - 1))
                    last.then_inc(summed, 1)

            @block.vector
            def _(dve):
                step = Steps(dve, dve_step)
                for j in range(n):
                    dve.wait_ge(summed, j + 1)
                    nc.vector.tensor_scalar(mean[:, j, :], sum_ps[:, j, :], 1.0 / width, EPS, ALU.mult,
                                            ALU.add).then_inc(mean_ready, 1)
                for j, job in enumerate(jobs):
                    dve.wait_ge(root_ready, j + 1)
                    step(nc.vector.reciprocal(rstd[:, j, :], root[:, j, :]))
                    for tile, gain, dst in job:
                        nc.vector.scalar_tensor_tensor(out=dst, in0=tile, scalar=gain,
                                                       in1=rstd[:, j, :], op0=ALU.mult, op1=ALU.mult)



def ada_phase(nc, A, ada):
    with Scope(nc, "ada") as s:
        c_col = s.sb("c_col", [P, KD])
        silu_col = s.sb("silu_col", [P, KD])
        silu_wide = s.sb("silu_wide", [P, KD, P])
        c_loaded, silu_ready = s.sem("c_loaded"), s.sem("silu_ready")
        with nc.Block() as block:
            @block.sync
            def _(sp):
                sp.dma_start(c_col[:], A["c_col"]).then_inc(c_loaded, 16)
                sp.dma_start(ada[:].rearrange("p i d -> p (i d)"), rows(A["b_ada"], P)).then_inc(c_loaded, 16)
                sp.wait_ge(c_loaded, 32)

            @block.scalar
            def _(act):
                act.wait_ge(c_loaded, 32)
                nc.scalar.activation(silu_col[:], c_col[:], ACT.Silu).then_inc(silu_ready, 1)
                act.wait_ge(silu_ready, 1)
                nc.scalar.copy(silu_wide[:], silu_col[:].unsqueeze(2).to_broadcast([P, KD, P]))

        flat = ada[:].rearrange("p i d -> p (i d)")
        w = weight_tiles(A["w_ada"])
        with Scope(nc, "adaw") as s:
            n_chunks = 6 * D // BANK
            slots = s.sb("slots", [P, 4, KD, BANK])
            banks = s.ps("banks", [P, 4, BANK])
            loaded = [s.sem(f"loaded{i}") for i in range(4)]
            product_done, taken = s.sem("product_done"), s.sem("taken")
            with nc.Block() as block:
                @block.sync
                def _(sp):
                    with sp.Fori(0, n_chunks // 4) as i:
                        for j in range(4):
                            sp.wait_ge(taken, i * 4)
                            sp.dma_start(slots[:, j], w[:, :, bass.ds(i * (4 * BANK) + j * BANK, BANK)]).then_inc(loaded[j], 16)

                @block.tensor
                def _(pe):
                    with pe.Fori(0, n_chunks // 4) as i:
                        for j in range(4):
                            pe.wait_ge(loaded[j], i * 16 + 16)
                            for k in range(KD):
                                last = nc.tensor.matmul(banks[:, j, :], silu_wide[:, k, :], slots[:, j, k, :],
                                                        start=(k == 0), stop=(k == KD - 1))
                            last.then_inc(product_done, 1)

                @block.vector
                def _(dve):
                    with dve.Fori(0, n_chunks // 4) as i:
                        for j in range(4):
                            dve.wait_ge(product_done, i * 4 + (j + 1))
                            part = flat[:, bass.ds(i * (4 * BANK) + j * BANK, BANK)]
                            nc.vector.tensor_tensor(part, banks[:, j, :], part, ALU.add).then_inc(taken, 1)


def first_projection(nc, A, h_t, feat, values):
    w = weight_tiles(A["w_in"])
    b = A["b_in"]
    AW, KVW, CW = 512, 128, 512
    o_k, o_v, o_b, o_c, o_u = AW, AW + KVW, AW + 2 * KVW, AW + 2 * KVW + CW, AW + 2 * KVW + 2 * CW
    with Scope(nc, "in1b") as s:
        bias = s.sb("bias", [P, 18])
        v_bias = s.sb("v_bias", [P, P])

        def feature(slot_col, f):
            return (P, T, lambda slot, k: (slot[:, k, slot_col:slot_col + P], h_t[:, k, :]),
                    add_column_to(feat[:, f, :], bias[:, f:f + 1]))

        def token(t):
            return (P, P, lambda slot, k: (h_t[:, k, t * P:(t + 1) * P], slot[:, k, 256:384]),
                    copy_to(values[:, t, :]))

        def plain(col):
            return lambda slot: [(slot[:, :, :], w[:, :, col:col + BANK])]

        def keys_values(slot):
            return ([(slot[:, :, 64 * i:64 * i + 64], w[:, :, o_k + 64 * (i // 2):o_k + 64 * (i // 2) + 64])
                     for i in range(4)] + [(slot[:, :, 256:384], w[:, :, o_v:o_v + P])])

        chunks = [(plain(0), [feature(P * j, j) for j in range(4)]),
                  (keys_values, [feature(0, 4), feature(P, 5)] + [token(t) for t in range(NT)])]
        for n, col in enumerate((o_b, o_c, o_u)):
            chunks.append((plain(col), [feature(P * j, 6 + 4 * n + j) for j in range(4)]))
        loads = [(bias[:, 0:4], A["b_in_col"][:, 0:4])]
        for i in range(4):
            half = slice(64 * (i % 2), 64 * (i % 2) + 64)
            loads.append((bias[half, 4 + i // 2:5 + i // 2],
                          b[o_k + 64 * (i // 2):o_k + 64 * (i // 2) + 64].rearrange("(p a) -> p a", a=1)))
        loads += [(bias[:, 6:18], A["b_in_col"][:, 6:18]), (v_bias[:], rows(b[o_v:o_v + P], P))]
        product_phase(nc, "in1", chunks, 4, BANK, loads)
        with nc.Block() as block:
            @block.vector
            def _(dve):
                nc.vector.tensor_tensor(values[:], values[:],
                                        v_bias[:].unsqueeze(1).to_broadcast([P, NT, P]), ALU.add)


def gated_conv_phase(nc, A, feat, conv_y):
    with Scope(nc, "conv") as s:
        z = s.sb("z", [P, 4, T + 2])
        taps = s.sb("taps", [P, 4, 3])
        acc = s.sb("acc", [P, 4, T])
        taps_loaded, dve_step = s.sem("taps_loaded"), s.sem("dve_step")
        with nc.Block() as block:
            @block.sync
            def _(sp):
                sp.dma_start(taps[:], A["conv_w_col"]).then_inc(taps_loaded, 16)

            @block.vector
            def _(dve):
                step = Steps(dve, dve_step)
                step(nc.vector.memset(z[:, :, 0:2], 0.0))
                step(nc.vector.tensor_tensor(z[:, :, 2:T + 2], feat[:, 10:14, :], feat[:, 14:18, :], ALU.mult))
                dve.wait_ge(taps_loaded, 16)
                for c in range(4):
                    step(nc.vector.tensor_scalar(acc[:, c, :], z[:, c, 0:T], taps[:, c, 0:1], None, ALU.mult))
                    for j in (1, 2):
                        step(nc.vector.scalar_tensor_tensor(
                            out=acc[:, c, :], in0=z[:, c, j:j + T], scalar=taps[:, c, j:j + 1],
                            in1=acc[:, c, :], op0=ALU.mult, op1=ALU.add))
                nc.vector.tensor_tensor(conv_y[:], acc[:], feat[:, 6:10, :], ALU.mult)


def out_projection(nc, name, w_dram, mix_t, x, bias_dram=None, gate=None):
    w = weight_tiles(w_dram)
    with Scope(nc, name) as s:
        b_rows = s.sb("b_rows", [P, D])
        part = s.sb("part", [P, 2, BANK])
        slots = s.sb("slots", [P, 2, KD, BANK])
        banks = s.ps("banks", [P, 8, BANK])
        loaded = [s.sem(f"loaded{i}") for i in range(2)]
        b_loaded, product_done, dve_step = s.sem("b_loaded"), s.sem("product_done"), s.sem("dve_step")
        with nc.Block() as block:
            @block.sync
            def _(sp):
                for n in range(2):
                    sp.dma_start(slots[:, n], w[:, :, n * BANK:(n + 1) * BANK]).then_inc(loaded[n], 16)
                if bias_dram is not None:
                    sp.dma_start(b_rows[:], rows(bias_dram, P)).then_inc(b_loaded, 16)

            @block.tensor
            def _(pe):
                for o in range(8):
                    n, t = o // NT, o % NT
                    pe.wait_ge(loaded[n], 16)
                    for k in range(KD):
                        last = nc.tensor.matmul(banks[:, o, :], mix_t[:, k, t * P:(t + 1) * P],
                                                slots[:, n, k, :], start=(k == 0), stop=(k == KD - 1))
                    last.then_inc(product_done, 1)

            @block.vector
            def _(dve):
                step = Steps(dve, dve_step)
                if bias_dram is not None:
                    dve.wait_ge(b_loaded, 16)
                for o in range(8):
                    n, t = o // NT, o % NT
                    cols = slice(n * BANK, (n + 1) * BANK)
                    dve.wait_ge(product_done, o + 1)
                    src = banks[:, o, :]
                    if gate is not None:
                        step(nc.vector.tensor_tensor(part[:, o % 2, :], src, b_rows[:, cols], ALU.add))
                        step(nc.vector.tensor_tensor(part[:, o % 2, :], part[:, o % 2, :], gate[:, cols], ALU.mult))
                        src = part[:, o % 2, :]
                    nc.vector.tensor_tensor(x[:, t, cols], src, x[:, t, cols], ALU.add)


def first_attention(nc, A, ident, feat, values, attn):
    with Scope(nc, "att1c") as s:
        mask = s.sb("mask", [P, 2 * P])
        sinks = s.sb("sinks", [P, NH])
        loaded = s.sem("loaded")
        with nc.Block() as block:
            @block.sync
            def _(sp):
                sp.dma_start(mask[:], A["window_mask"]).then_inc(loaded, 16)
                sp.dma_start(sinks[:], rows(A["attn_sinks"], P)).then_inc(loaded, 16)
                sp.wait_ge(loaded, 32)
        units = [(n, h) for n in range(NT) for h in range(NH)]

        def part(h):
            return slice(64 * (h % 2), 64 * (h % 2) + 64)

        attention_phase(
            nc, "att1", ident, units,
            q_of=lambda n, h: feat[part(h), h // 2, n * P:(n + 1) * P],
            k_of=lambda n, h: feat[part(h), 4 + h // 4, max(n - 1, 0) * P:(n + 1) * P],
            v_of=lambda n, h: [values[:, c, 64 * (h // 4):64 * (h // 4) + 64] for c in range(max(n - 1, 0), n + 1)],
            bias_of=lambda n, h: mask[:, P:2 * P] if n == 0 else mask[:],
            o_of=lambda n, h: attn[:, n, DH * h:DH * h + DH],
            keys_max=2 * P, sinks=lambda n, h: sinks[:, h:h + 1])



def query_projection(nc, A, h_t, query_t):
    w = weight_tiles(A["w_query"])

    def feature(slot_col, f):
        return (P, T, lambda slot, k: (slot[:, k, slot_col:slot_col + P], h_t[:, k, :]), copy_to(query_t[:, f, :]))

    chunks = [((lambda slot, n=n: [(slot[:, :, :], w[:, :, n * BANK:(n + 1) * BANK])]),
               [feature(P * j, 4 * n + j) for j in range(4)]) for n in range(4)]
    product_phase(nc, "qp", chunks, 4, BANK)


def peer_choice_phase(nc, A, query_t, choice):
    with Scope(nc, "pick") as s:
        keys_t = s.sb("keys_t", [P, NC, NKEY])
        score = s.sb("score", [P, 2, NC, NKEY])
        val = s.sb("val", [P, NC, PK])
        idx = s.sb("idx", [P, NC, PK], U32)
        idx_f = s.sb("idx_f", [P, NC, PK])
        cand = s.sb("cand", [P, PH, PK, PK])
        best = s.sb("best", [P, PH, PK])
        place = s.sb("place", [P, PH, PK], U32)
        place_part = s.sb("place_part", [P, PH, PK], U32)
        place_f = s.sb("place_f", [P, PH, PK])
        hot = s.sb("hot", [P, PH * PK, PK])
        iota16 = s.sb("iota16", [P, PK])
        shifted = s.sb("shifted", [P, PH, PK])
        expd = s.sb("expd", [P, PH, PK])
        total = s.sb("total", [P, PH])
        total_inv = s.sb("total_inv", [P, PH])
        score_ps = s.ps("score_ps", [P, 8, 4, NKEY])
        loaded, scored, copied, used, dve_step, shift_ready, exp_ready = (s.sem(x) for x in (
            "loaded", "scored", "copied", "used", "dve_step", "shift_ready", "exp_ready"))
        with nc.Block() as block:
            @block.sync
            def _(sp):
                for half in range(2):
                    sp.dma_start(keys_t[:, half::2, :], A[f"keys_t{half + 1}"]).then_inc(loaded, 16)
                sp.dma_start(iota16[:], rows(A["iota"][0:PK], P)).then_inc(loaded, 16)

            @block.tensor
            def _(pe):
                pe.wait_ge(loaded, 48)
                for t in range(NT):
                    for b in range(4):
                        g = 4 * t + b
                        if g >= 8:
                            pe.wait_ge(copied, g - 7)
                        for j in range(4):
                            last = nc.tensor.matmul(score_ps[:, g % 8, j, :],
                                                    query_t[:, 4 * b + j, t * P:(t + 1) * P],
                                                    keys_t[:, 4 * b + j, :], start=True, stop=True)
                        last.then_inc(scored, 1)

            @block.scalar
            def _(act):
                def copy_scores(t):
                    if t >= 2:
                        act.wait_ge(used, t - 1)
                    for b in range(4):
                        act.wait_ge(scored, 4 * t + b + 1)
                        nc.scalar.copy(score[:, t % 2, 4 * b:4 * b + 4, :],
                                       score_ps[:, (4 * t + b) % 8, :, :]).then_inc(copied, 1)
                copy_scores(0)
                for t in range(NT):
                    if t + 1 < NT:
                        copy_scores(t + 1)
                    act.wait_ge(shift_ready, t + 1)
                    nc.scalar.activation(expd[:], shifted[:], ACT.Exp).then_inc(exp_ready, 1)

            @block.vector
            def _(dve):
                step = Steps(dve, dve_step)
                dve.wait_ge(loaded, 48)

                def best16(v, i, data):
                    step(nc.vector.max(v[:, 0:8], data))
                    step(nc.vector.max_index(i[:, 0:8], v[:, 0:8], data))
                    step(nc.vector.match_replace(data, v[:, 0:8], data, LOWEST))
                    step(nc.vector.max(v[:, 8:16], data))
                    step(nc.vector.max_index(i[:, 8:16], v[:, 8:16], data))

                for t in range(NT):
                    dve.wait_ge(copied, 4 * t + 4)
                    for c in range(NC):
                        best16(val[:, c, :], idx[:, c, :], score[:, t % 2, c, :])
                    nc.vector.tensor_copy(idx_f[:], idx[:]).then_inc(used, 1)
                    dve.wait_ge(used, t + 1)
                    step(nc.vector.tensor_tensor(
                        cand[:], val[:, 0::2, :].unsqueeze(3).to_broadcast([P, PH, PK, PK]),
                        val[:, 1::2, :].unsqueeze(2).to_broadcast([P, PH, PK, PK]), ALU.add))
                    for h in range(PH):
                        best16(best[:, h, :], place[:, h, :], cand[:, h, :, :].rearrange("p i j -> p (i j)"))
                    for i, (op, by) in enumerate(((ALU.logical_shift_right, 4), (ALU.bitwise_and, 15))):
                        step(nc.vector.tensor_scalar(place_part[:], place[:], by, None, op))
                        step(nc.vector.tensor_copy(place_f[:], place_part[:]))
                        step(nc.vector.tensor_tensor(
                            hot[:], place_f[:].rearrange("p h k -> p (h k)").unsqueeze(2).to_broadcast([P, PH * PK, PK]),
                            iota16[:].unsqueeze(1).to_broadcast([P, PH * PK, PK]), ALU.is_equal))
                        hot4 = hot[:].rearrange("p (h k) i -> p h k i", h=PH)
                        for h in range(PH):
                            last = nc.vector.tensor_tensor(
                                hot4[:, h], hot4[:, h],
                                idx_f[:, 2 * h + i, :].unsqueeze(1).to_broadcast([P, PK, PK]), ALU.mult)
                            if h < PH - 1:
                                step(last)
                        step(last)
                        step(nc.vector.tensor_reduce(choice[:, i, t, :], hot[:], AX.X, ALU.add))
                    if t >= 1:
                        dve.wait_ge(exp_ready, t)
                    nc.vector.tensor_tensor(shifted[:], best[:], best[:, :, 0:1].to_broadcast([P, PH, PK]),
                                            ALU.subtract).then_inc(shift_ready, 1)
                    dve.wait_ge(exp_ready, t + 1)
                    step(nc.vector.tensor_reduce(total[:], expd[:], AX.X, ALU.add))
                    step(nc.vector.reciprocal(total_inv[:], total[:]))
                    step(nc.vector.tensor_tensor(
                        choice[:, 2, t, :].rearrange("p (h k) -> p h k", h=PH), expd[:],
                        total_inv[:].unsqueeze(2).to_broadcast([P, PH, PK]), ALU.mult))


def peer_weight_phase(nc, A, ident, choice, weight_dram):
    SET = 8
    with Scope(nc, "wt") as s:
        choice_t = s.sb("choice_t", [P, 3, T])
        iota = s.sb("iota", [P, NKEY])
        now = s.sb("now", [P, 2, 2, SET])
        hot1 = s.sb("hot1", [P, 2, SET, NKEY])
        hot2 = s.sb("hot2", [P, 2, SET, NKEY])
        stage = s.sb("stage", [P, 2, NKEY, P])
        iota_loaded, turned, taken = s.sem("iota_loaded"), s.sem("turned"), s.sem("taken")
        with ExitStack() as inner:
            turn_ps = inner.enter_context(nc.psum_tensor("wt_turn_ps", [P, 3, NT, P], F32))
            with nc.Block() as block:
                @block.sync
                def _(sp):
                    sp.dma_start(iota[:], rows(A["iota"], P)).then_inc(iota_loaded, 16)
                    sp.wait_ge(iota_loaded, 16)

                @block.tensor
                def _(pe):
                    for i in range(3):
                        for t in range(NT):
                            last = nc.tensor.transpose(turn_ps[:, i, t, :], choice[:, i, t, :], ident[:])
                        last.then_inc(turned, 1)

                @block.vector
                def _(dve):
                    for i in range(3):
                        dve.wait_ge(turned, i + 1)
                        nc.vector.tensor_copy(choice_t[:, i, :], turn_ps[:, i, :, :].rearrange("p t q -> p (t q)"))

        banks = s.ps("banks", [P, 4, 4, NKEY])
        now_ready, hot1_ready, hot2_ready = (s.sem(x) for x in ("now_ready", "hot1_ready", "hot2_ready"))
        product_done = [s.sem(f"product_done{b}") for b in range(2)]
        staged = [s.sem(f"staged{b}") for b in range(2)]
        stored = [s.sem(f"stored{b}") for b in range(2)]
        rounds = P // (2 * SET)
        with nc.Block() as block:
            @block.vector
            def _(dve):
                for t in range(NT):
                    with dve.Fori(0, rounds) as i:
                        for b in range(2):
                            token = i * (2 * SET) + (t * P + b * SET)
                            dve.wait_ge(product_done[b], i * 2 + 2 * rounds * t)
                            nc.vector.tensor_copy(now[:, b, 0, :], choice_t[:, 0, bass.ds(token, SET)]).then_inc(now_ready, 1)
                            nc.vector.tensor_tensor(
                                hot2[:, b], iota[:].unsqueeze(1).to_broadcast([P, SET, NKEY]),
                                choice_t[:, 1, bass.ds(token, SET)].unsqueeze(2).to_broadcast([P, SET, NKEY]),
                                ALU.is_equal).then_inc(hot2_ready, 1)
                            nc.vector.tensor_copy(now[:, b, 1, :], choice_t[:, 2, bass.ds(token, SET)]).then_inc(now_ready, 1)
                            dve.wait_ge(now_ready, i * 4 + (4 * rounds * t + 2 * b + 2))
                            for j in range(SET):
                                last = nc.vector.tensor_scalar(hot1[:, b, j, :], iota[:], now[:, b, 0, j:j + 1],
                                                               now[:, b, 1, j:j + 1], ALU.is_equal, ALU.mult)
                            last.then_inc(hot1_ready, 1)

            @block.tensor
            def _(pe):
                for t in range(NT):
                    with pe.Fori(0, rounds) as i:
                        for b in range(2):
                            pe.wait_ge(hot1_ready, i * 2 + (2 * rounds * t + b + 1))
                            pe.wait_ge(hot2_ready, i * 2 + (2 * rounds * t + b + 1))
                            pe.wait_ge(staged[b], i * 2 + 2 * rounds * t)
                            for j in range(SET):
                                last = nc.tensor.matmul(banks[:, 2 * b + j // 4, j % 4, :], hot2[:, b, j, :],
                                                        hot1[:, b, j, :], start=True, stop=True)
                                if j % 4 == 3:
                                    last.then_inc(product_done[b], 1)

            @block.scalar
            def _(act):
                for t in range(NT):
                    if t >= 2:
                        act.wait_ge(stored[t % 2], 16)
                    with act.Fori(0, rounds) as i:
                        for q in range(4):
                            act.wait_ge(product_done[q // 2], i * 2 + (2 * rounds * t + q % 2 + 1))
                            nc.scalar.copy(stage[:, t % 2, :, bass.ds(i * (2 * SET) + 4 * q, 4)],
                                           banks[:, q].rearrange("p t e -> p e t")).then_inc(staged[q // 2], 1)

            @block.sync
            def _(sp):
                out = weight_dram.rearrange("a b t -> b a t")
                for t in range(NT):
                    for b in range(2):
                        sp.wait_ge(staged[b], 2 * rounds * (t + 1))
                    sp.dma_start(out[:, :, t * P:(t + 1) * P], stage[:, t % 2]).then_inc(stored[t % 2], 16)
                for b in range(2):
                    sp.wait_ge(stored[b], 16 * NT // 2)


def peer_dense_phase(nc, A, h_t, weight_dram, x, gate):
    US, WS = 4, 4
    with Scope(nc, "peer") as s:
        acc = s.sb("acc", [P, NT, D])
        u = s.sb("u", [P, US, KD, P])
        wt = s.sb("wt", [P, WS, T])
        v = s.sb("v", [P, GROUP, D])
        gelu = s.sb("gelu", [P, 2, T])
        coef = s.sb("coef", [P, GROUP, T])
        act_ps = s.ps("act_ps", [P, 4, BANK])
        sum_ps = s.ps("sum_ps", [P, 4, BANK])
        u_loaded = [s.sem(f"u_loaded{i}") for i in range(US)]
        w_loaded = [s.sem(f"w_loaded{i}") for i in range(WS)]
        v_loaded = [s.sem(f"v_loaded{i}") for i in range(GROUP)]
        dotted, gelu_ready, coef_ready, summed, added, dve_step = (s.sem(x) for x in (
            "dotted", "gelu_ready", "coef_ready", "summed", "added", "dve_step"))
        n_groups = ETILES // GROUP
        with nc.Block() as block:
            @block.sync
            def _(sp):
                def load_tile(g, j):
                    tile = g * GROUP + j
                    sp.wait_ge(dotted, g * GROUP + max(j - US + 1, 0))
                    sp.dma_start(u[:, j % US], A["u_tiles"][bass.ds(tile, 1)].rearrange(
                        "a p k e -> p (a k) e")).then_inc(u_loaded[j % US], 16)
                    sp.wait_ge(coef_ready, g * GROUP + max(j - WS + 1, 0))
                    sp.dma_start(wt[:, j % WS], weight_dram[bass.ds(tile, 1)].rearrange(
                        "a b t -> b (a t)")).then_inc(w_loaded[j % WS], 16)

                with sp.Fori(0, n_groups) as g:
                    for j in range(US):
                        load_tile(g, j)
                    sp.wait_ge(summed, g * 8)
                    for j in range(GROUP):
                        if US + j < GROUP:
                            load_tile(g, US + j)
                        sp.dma_start(v[:, j], A["peer_v"][bass.ds((g * GROUP + j) * P, P), :]).then_inc(v_loaded[j], 16)

            @block.tensor
            def _(pe):
                with pe.Fori(0, n_groups) as g:
                    for j in range(GROUP):
                        pe.wait_ge(u_loaded[j % US], g * (16 * (GROUP // US)) + (j // US + 1) * 16)
                        pe.wait_ge(gelu_ready, g * GROUP + max(j - 3, 0))
                        for k in range(KD):
                            last = nc.tensor.matmul(act_ps[:, j % 4, :], u[:, j % US, k, :], h_t[:, k, :],
                                                    start=(k == 0), stop=(k == KD - 1))
                        last.then_inc(dotted, 1)
                    for o in range(8):
                        t, half = o // 2, o % 2
                        pe.wait_ge(added, g * 8 + max(o - 3, 0))
                        for j in range(GROUP):
                            if o == 0:
                                pe.wait_ge(coef_ready, g * GROUP + (j + 1))
                                pe.wait_ge(v_loaded[j], g * 16 + 16)
                            last = nc.tensor.matmul(sum_ps[:, o % 4, :], coef[:, j, t * P:(t + 1) * P],
                                                    v[:, j, half * BANK:(half + 1) * BANK],
                                                    start=(j == 0), stop=(j == GROUP - 1))
                        last.then_inc(summed, 1)

            @block.scalar
            def _(act):
                with act.Fori(0, n_groups) as g:
                    for j in range(GROUP):
                        act.wait_ge(dotted, g * GROUP + (j + 1))
                        act.wait_ge(coef_ready, g * GROUP + max(j - 1, 0))
                        nc.scalar.activation(gelu[:, j % 2, :], act_ps[:, j % 4, :], ACT.Gelu).then_inc(gelu_ready, 1)

            @block.vector
            def _(dve):
                step = Steps(dve, dve_step)
                step(nc.vector.memset(acc[:], 0.0))
                with dve.Fori(0, n_groups) as g:
                    for j in range(GROUP):
                        dve.wait_ge(gelu_ready, g * GROUP + (j + 1))
                        dve.wait_ge(w_loaded[j % WS], g * (16 * (GROUP // WS)) + (j // WS + 1) * 16)
                        dve.wait_ge(summed, g * 8)
                        nc.vector.tensor_tensor(coef[:, j, :], gelu[:, j % 2, :], wt[:, j % WS], ALU.mult).then_inc(coef_ready, 1)
                    for o in range(8):
                        t, half = o // 2, o % 2
                        part = acc[:, t, half * BANK:(half + 1) * BANK]
                        dve.wait_ge(summed, g * 8 + (o + 1))
                        nc.vector.tensor_tensor(part, sum_ps[:, o % 4, :], part, ALU.add).then_inc(added, 1)
                dve.wait_ge(added, 8 * n_groups)
                for t in range(NT):
                    step(nc.vector.tensor_tensor(acc[:, t, :], acc[:, t, :], gate, ALU.mult))
                    nc.vector.tensor_tensor(x[:, t, :], acc[:, t, :], x[:, t, :], ALU.add)



HY, NA, PW = 256, 512, 256
FH = 64
FE = 33
TWO_PI = 2.0 * np.pi
ROUND = 1.5 * 2.0 ** 23
PI_1 = 6.28125
PI_2 = float((np.array([TWO_PI - PI_1], np.float32).view(np.uint32) & np.uint32(0xFFFFF000)).view(np.float32)[0])
PI_3 = float(np.float32(TWO_PI - PI_1 - PI_2))
PI_LOW = 3.1415925


def second_projection(nc, A, h_t, feat, values):
    w = weight_tiles(A["w_in_2"][0])

    def feature(slot_col, f):
        return (P, T, lambda slot, k: (slot[:, k, slot_col:slot_col + P], h_t[:, k, :]), copy_to(feat[:, f, :]))

    def token(t):
        return (P, NA, lambda slot, k: (h_t[:, k, t * P:(t + 1) * P], slot[:, k, :]), copy_to(values[:, t, :]))

    def cols(at, width):
        return lambda slot: [(slot[:, :, 0:width], w[:, :, at:at + width])]

    chunks, at, f = [], 0, 0
    for width in (512, 256, 512, 512):
        chunks.append((cols(at, width), [feature(P * j, f + j) for j in range(width // P)]))
        at, f = at + width, f + width // P
    chunks.append((cols(at, NA), [token(t) for t in range(NT)]))
    chunks.append((cols(at + NA, PW), [feature(P * j, f + j) for j in range(PW // P)]))
    product_phase(nc, "in2", chunks, 4, BANK)


def filter_phase(nc, A, even, odd):
    with Scope(nc, "filt") as s:
        pos_t = s.sb("pos_t", [FE, T])
        w1 = s.sb("w1", [FE, FH])
        w2 = s.sb("w2", [FH, FH])
        w_out = s.sb("w_out", [FH, 2 * HY])
        cols = s.sb("cols", [FH, 3])
        decay = s.sb("decay", [P, NT, 2 * HY])
        arg = s.sb("arg", [FH, T])
        turns = s.sb("turns", [FH, T])
        hid = s.sb("hid", [FH, 2, T])
        taps = s.sb("taps", [P, NT, 2 * HY])
        hid_ps = s.ps("hid_ps", [FH, 2, BANK])
        tap_ps = s.ps("tap_ps", [P, NT, BANK])
        loaded, hid_done, arg_ready, sine_ready, taps_done, dve_step = (s.sem(x) for x in (
            "loaded", "hid_done", "arg_ready", "sine_ready", "taps_done", "dve_step"))
        with nc.Block() as block:
            @block.sync
            def _(sp):
                for to, src in ((pos_t[:], A["pos_t"]), (w1[:], A["hy_f_w1_2"][0]), (w2[:], A["hy_f_w2_2"][0]),
                                (w_out[:], A["hy_f_wout_2"][0]),
                                (cols[:, 0:1], A["hy_f_b1_2"].rearrange("a n -> n a")),
                                (cols[:, 1:2], A["hy_f_b2_2"].rearrange("a n -> n a")),
                                (cols[:, 2:3], A["hy_f_freq_2"].rearrange("a n -> n a")),
                                (decay[:], A["decay"].rearrange("(t p) c -> p t c", p=P))):
                    sp.dma_start(to, src).then_inc(loaded, 16)

            @block.tensor
            def _(pe):
                pe.wait_ge(loaded, 16 * 8)
                nc.tensor.matmul(hid_ps[:, 0, :], w1[:], pos_t[:], start=True, stop=True).then_inc(hid_done, 1)
                pe.wait_ge(sine_ready, 1)
                nc.tensor.matmul(hid_ps[:, 1, :], w2[:], hid[:, 0, :], start=True, stop=True).then_inc(hid_done, 1)
                pe.wait_ge(sine_ready, 2)
                for t in range(NT):
                    nc.tensor.matmul(tap_ps[:, t, :], hid[:, 1, t * P:(t + 1) * P], w_out[:],
                                     start=True, stop=True).then_inc(taps_done, 1)

            @block.scalar
            def _(act):
                for i in range(2):
                    act.wait_ge(arg_ready, i + 1)
                    nc.scalar.activation(hid[:, i, :], arg[:], ACT.Sin).then_inc(sine_ready, 1)

            @block.vector
            def _(dve):
                step = Steps(dve, dve_step)
                dve.wait_ge(loaded, 16 * 8)
                for i in range(2):
                    dve.wait_ge(hid_done, i + 1)
                    step(nc.vector.tensor_scalar(arg[:], hid_ps[:, i, :], cols[:, i:i + 1], cols[:, 2:3],
                                                 ALU.add, ALU.mult))
                    step(nc.vector.tensor_scalar(turns[:], arg[:], 1.0 / TWO_PI, ROUND, ALU.mult, ALU.add))
                    step(nc.vector.tensor_scalar(turns[:], turns[:], ROUND, None, ALU.subtract))
                    for part in (PI_1, PI_2, PI_3):
                        step(nc.vector.scalar_tensor_tensor(out=arg[:], in0=turns[:], scalar=-part, in1=arg[:],
                                                            op0=ALU.mult, op1=ALU.add))
                    nc.vector.tensor_scalar(arg[:], arg[:], PI_LOW, -PI_LOW, ALU.min, ALU.max).then_inc(arg_ready, 1)
                    dve.wait_ge(sine_ready, i + 1)
                for t in range(NT):
                    dve.wait_ge(taps_done, t + 1)
                    step(nc.vector.tensor_tensor(taps[:, t, :], tap_ps[:, t, :], decay[:, t, :], ALU.mult))
                nc.vector.tensor_tensor(even[:], taps[:, :, 0:HY], taps[:, :, HY:], ALU.add)
                nc.vector.tensor_tensor(odd[:], taps[:, :, 0:HY], taps[:, :, HY:], ALU.subtract)


def hyena_phase(nc, A, ident, feat, even, odd, hy_y):
    with Scope(nc, "hyen") as s:
        short = s.sb("short", [P, 6, T])
        taps = s.sb("taps", [P, 6, 3])
        short_bias = s.sb("short_bias", [P, 6])
        skip = s.sb("skip", [P, 2])
        z = s.sb("z", [P, 2, T])
        with_cos = s.sb("with_cos", [P, NT, 2 * HY])
        with_sin = s.sb("with_sin", [P, NT, 2 * HY])
        cos = s.sb("cos", [P, NT, T])
        sin = s.sb("sin", [P, NT, T])
        cos_t = s.sb("cos_t", [P, NT, T])
        sin_t = s.sb("sin_t", [P, NT, T])
        spec_cos = s.sb("spec_cos", [P, NT, 2 * HY])
        spec_sin = s.sb("spec_sin", [P, NT, 2 * HY])
        out_cos = s.sb("out_cos", [P, NT, HY])
        out_sin = s.sb("out_sin", [P, NT, HY])
        part = s.sb("part", [P, NT, HY])
        banks = s.ps("banks", [P, 8, BANK])
        taps_loaded, dft_loaded, z_ready, turned, input_ready, spec_done, spec_taken, out_ready, y_done, dve_step = (
            s.sem(x) for x in ("taps_loaded", "dft_loaded", "z_ready", "turned", "input_ready", "spec_done",
                               "spec_taken", "out_ready", "y_done", "dve_step"))
        with nc.Block() as block:
            @block.sync
            def _(sp):
                sp.dma_start(taps[:], A["hy_short_w_col"]).then_inc(taps_loaded, 16)
                sp.dma_start(short_bias[:], A["hy_short_b_col"]).then_inc(taps_loaded, 16)
                sp.dma_start(skip[:], A["hy_skip_col"]).then_inc(taps_loaded, 16)
                for to, name in ((cos, "dft_cos"), (sin, "dft_sin"), (cos_t, "dft_cos_t"), (sin_t, "dft_sin_t")):
                    sp.dma_start(to[:], A[name].rearrange("(t p) f -> p t f", p=P)).then_inc(dft_loaded, 16)

            @block.tensor
            def _(pe):
                pe.wait_ge(z_ready, 1)
                for c in range(2):
                    for t in range(NT):
                        last = nc.tensor.transpose(banks[:, c, t * P:(t + 1) * P], z[:, c, t * P:(t + 1) * P], ident[:])
                    last.then_inc(turned, 1)
                pe.wait_ge(dft_loaded, 64)
                pe.wait_ge(input_ready, 3)
                for f in range(NT):
                    for i, (table, data) in enumerate(((cos, with_cos), (sin, with_sin))):
                        for t in range(NT):
                            last = nc.tensor.matmul(banks[:, 2 * f + i, :], table[:, t, f * P:(f + 1) * P],
                                                    data[:, t, :], start=(t == 0), stop=(t == NT - 1))
                        last.then_inc(spec_done, 1)
                pe.wait_ge(out_ready, 1)
                for c in range(2):
                    for i, (table, data) in enumerate(((cos_t, out_cos), (sin_t, out_sin))):
                        for f in range(NT):
                            last = nc.tensor.matmul(banks[:, c, :], data[:, f, c * P:(c + 1) * P], table[:, f, :],
                                                    start=(i == 0 and f == 0), stop=(i == 1 and f == NT - 1))
                    last.then_inc(y_done, 1)

            @block.scalar
            def _(act):
                nc.scalar.copy(with_cos[:, :, HY:], even[:]).then_inc(input_ready, 1)
                nc.scalar.copy(with_sin[:, :, HY:], odd[:]).then_inc(input_ready, 1)
                for g in range(8):
                    act.wait_ge(spec_done, g + 1)
                    dst = (spec_cos, spec_sin)[g % 2]
                    nc.scalar.copy(dst[:, g // 2, :], banks[:, g, :]).then_inc(spec_taken, 1)

            @block.vector
            def _(dve):
                step = Steps(dve, dve_step)
                dve.wait_ge(taps_loaded, 48)
                for f in range(6):
                    step(nc.vector.tensor_scalar(short[:, f, :], feat[:, f, :], taps[:, f, 1:2], short_bias[:, f:f + 1],
                                                 ALU.mult, ALU.add))
                    step(nc.vector.scalar_tensor_tensor(out=short[:, f, 1:T], in0=feat[:, f, 0:T - 1],
                                                        scalar=taps[:, f, 0:1], in1=short[:, f, 1:T],
                                                        op0=ALU.mult, op1=ALU.add))
                    step(nc.vector.scalar_tensor_tensor(out=short[:, f, 0:T - 1], in0=feat[:, f, 1:T],
                                                        scalar=taps[:, f, 2:3], in1=short[:, f, 0:T - 1],
                                                        op0=ALU.mult, op1=ALU.add))
                nc.vector.tensor_tensor(z[:], short[:, 4:6, :], short[:, 2:4, :], ALU.mult).then_inc(z_ready, 1)
                dve.wait_ge(turned, 2)
                for to in (with_cos, with_sin):
                    for c in range(2):
                        last = nc.vector.tensor_copy(to[:, :, c * P:(c + 1) * P],
                                                     banks[:, c, :].rearrange("p (t q) -> p t q", q=P))
                        if c == 0 or to is with_cos:
                            step(last)
                last.then_inc(input_ready, 1)
                dve.wait_ge(z_ready, 1)
                for c in range(2):
                    step(nc.vector.tensor_scalar(z[:, c, :], z[:, c, :], skip[:, c:c + 1], None, ALU.mult))
                dve.wait_ge(spec_taken, 8)
                zc, ec = spec_cos[:, :, 0:HY], spec_cos[:, :, HY:]
                zs, es = spec_sin[:, :, 0:HY], spec_sin[:, :, HY:]
                step(nc.vector.tensor_tensor(out_cos[:], zc, ec, ALU.mult))
                step(nc.vector.tensor_tensor(part[:], zs, es, ALU.mult))
                step(nc.vector.tensor_tensor(out_cos[:], out_cos[:], part[:], ALU.subtract))
                step(nc.vector.tensor_tensor(out_sin[:], zc, es, ALU.mult))
                step(nc.vector.tensor_tensor(part[:], zs, ec, ALU.mult))
                nc.vector.tensor_tensor(out_sin[:], out_sin[:], part[:], ALU.add).then_inc(out_ready, 1)
                for c in range(2):
                    dve.wait_ge(y_done, c + 1)
                    step(nc.vector.scalar_tensor_tensor(out=hy_y[:, c, :], in0=banks[:, c, :], scalar=2.0 / (2 * T),
                                                        in1=z[:, c, :], op0=ALU.mult, op1=ALU.add))
                    nc.vector.tensor_tensor(hy_y[:, c, :], hy_y[:, c, :], short[:, c, :], ALU.mult)


def pool_phase(nc, A, feat, pool_y):
    PAD = 8
    W = T + 2 * PAD
    with Scope(nc, "pool") as s:
        sums = s.sb("sums", [P, 5, 2, W])
        inv = s.sb("inv", [P, 2, T])
        mat = s.sb("mat", [P, 2, P])
        scale = s.sb("scale", [P, 2])
        pooled = s.sb("pooled", [P, 2, T])
        banks = s.ps("banks", [P, 2, BANK])
        zeroed, loaded, pooled_ready, product_done, dve_step = (s.sem(x) for x in (
            "zeroed", "loaded", "pooled_ready", "product_done", "dve_step"))
        with nc.Block() as block:
            @block.sync
            def _(sp):
                for g in range(4):
                    half = slice(64 * (g % 2), 64 * (g % 2) + 64)
                    sp.dma_start(inv[half, g // 2, :], rows(A["pool_inv"][g], 64)).then_inc(loaded, 16)
                sp.dma_start(scale[:], A["pool_scale_col"]).then_inc(loaded, 16)
                sp.wait_ge(zeroed, 1)
                for g in range(4):
                    half = slice(64 * (g % 2), 64 * (g % 2) + 64)
                    sp.dma_start(mat[half, g // 2, half], A["pool_w_2"][0, g]).then_inc(loaded, 16)

            @block.vector
            def _(dve):
                step = Steps(dve, dve_step)
                nc.vector.memset(mat[:], 0.0).then_inc(zeroed, 1)
                step(nc.vector.memset(sums[:], 0.0))
                step(nc.vector.tensor_copy(sums[:, 0, :, PAD:PAD + T], feat[:, 14:16, :]))
                step(nc.vector.tensor_tensor(sums[:, 1, :, 1:W - 1], sums[:, 0, :, 0:W - 2], sums[:, 0, :, 1:W - 1], ALU.add))
                for i, (lo, by) in enumerate(((2, 1), (4, 2), (8, 4))):
                    step(nc.vector.tensor_tensor(sums[:, i + 2, :, lo:W - lo], sums[:, i + 1, :, lo - by:W - lo - by],
                                                 sums[:, i + 1, :, lo + by:W - lo + by], ALU.add))
                dve.wait_ge(loaded, 16 * 9)
                for g in range(4):
                    half = slice(64 * (g % 2), 64 * (g % 2) + 64)
                    step(nc.vector.tensor_tensor(pooled[half, g // 2, :], sums[half, g + 1, g // 2, PAD:PAD + T],
                                                 inv[half, g // 2, :], ALU.mult))
                nc.vector.tensor_tensor(pooled[:], pooled[:], feat[:, 14:16, :], ALU.subtract).then_inc(pooled_ready, 1)
                for c in range(2):
                    dve.wait_ge(product_done, c + 1)
                    nc.vector.tensor_scalar(pool_y[:, c, :], banks[:, c, :], scale[:, c:c + 1], None, ALU.mult)

            @block.tensor
            def _(pe):
                pe.wait_ge(loaded, 16 * 9)
                pe.wait_ge(pooled_ready, 1)
                for c in range(2):
                    nc.tensor.matmul(banks[:, c, :], mat[:, c, :], pooled[:, c, :],
                                     start=True, stop=True).then_inc(product_done, 1)


def bias_table_phase(nc, A, table):
    DR, DC, GW = 15, 31, 64
    with Scope(nc, "bias") as s:
        pick = s.sb("pick", [DC + 1, GW, P])
        bias = s.sb("bias", [DC + 1, NH * DR])
        banks = s.ps("banks", [P, 4, BANK])
        one, loaded, product_done, act_taken, dve_taken = (s.sem(x) for x in (
            "one", "loaded", "product_done", "act_taken", "dve_taken"))
        n = GW // 4
        with nc.Block() as block:
            @block.sync
            def _(sp):
                sp.dma_start(pick[:], A["bias_pick"]).then_inc(loaded, 16)
                sp.wait_ge(one, 1)
                sp.dma_start(bias[0:DC, :], A["rpb_t"]).then_inc(loaded, 16)

            @block.tensor
            def _(pe):
                pe.wait_ge(loaded, 32)
                for g in range(n):
                    if g >= 4:
                        pe.wait_ge(act_taken, g - 3)
                        pe.wait_ge(dve_taken, g - 3)
                    for j in range(4):
                        last = nc.tensor.matmul(banks[:, g % 4, j * NH * DR:(j + 1) * NH * DR],
                                                pick[:, 4 * g + j, :], bias[:], start=True, stop=True)
                    last.then_inc(product_done, 1)

            def move(copy, half, row, g):
                src = banks[half, g % 4, 0:4 * NH * DR].rearrange("p (j h r) -> p h r j", j=4, h=NH)
                dst = table[half, :, :].rearrange("p h (r j) -> p h r j", j=GW)
                return copy(dst[:, :, row:row + DR, 4 * g:4 * g + 4], src)

            @block.scalar
            def _(act):
                for g in range(n):
                    act.wait_ge(product_done, g + 1)
                    move(nc.scalar.copy, slice(0, 64), 0, g).then_inc(act_taken, 1)

            @block.vector
            def _(dve):
                nc.vector.memset(bias[:], 1.0).then_inc(one, 1)
                for g in range(n):
                    dve.wait_ge(product_done, g + 1)
                    move(nc.vector.tensor_copy, slice(64, 128), 1, g).then_inc(dve_taken, 1)


def second_attention(nc, A, ident, feat, values, table, attn):
    units = [(t, h) for t in range(NT) for h in range(NH)]

    def part(h):
        return slice(64 * (h % 2), 64 * (h % 2) + 64)

    attention_phase(
        nc, "att2", ident, units,
        q_of=lambda t, h: feat[part(h), 6 + h // 2, t * P:(t + 1) * P],
        k_of=lambda t, h: feat[part(h), 10 + h // 2, :],
        v_of=lambda t, h: [values[:, c, DH * h:DH * h + DH] for c in range(NT)],
        bias_of=lambda t, h: table[:, h, (7 - 2 * t) * 64:(7 - 2 * t) * 64 + T],
        o_of=lambda t, h: attn[:, t, DH * h:DH * h + DH], keys_max=T)



def router_phase(nc, A, ident, h_t, h_dram, gate_dram, token_dram, xs_t, token_f, gate):
    with Scope(nc, "rout") as s:
        w = s.sb("w", [P, KD, NE])
        top = s.sb("top", [P, NT])
        logit = s.sb("logit", [P, NT, NE])
        expd = s.sb("expd", [P, NT, NE])
        total = s.sb("total", [P, NT])
        total_inv = s.sb("total_inv", [P, NT])
        aff = s.sb("aff", [P, NT, NE])
        aff_t = s.sb("aff_t", [NE, T])
        val = s.sb("val", [NE, CAP])
        idx = s.sb("idx", [NE, CAP], U32)
        idx_f = s.sb("idx_f", [NE, CAP])
        token_u = s.sb("token_u", [P, NPAIR], U32)
        xs = s.sb("xs", [P, NPAIR, D])
        logit_ps = s.ps("logit_ps", [P, NT, NE])
        aff_ps = s.ps("aff_ps", [NE, T])
        turn_ps = s.ps("turn_ps", [P, 4, 4, P])
        (w_loaded, logits_done, shift_ready, exp_ready, aff_ready, turned, best_ready, listed, relisted,
         token_ready, xs_turned, xs_taken, dve_step) = (s.sem(x) for x in (
             "w_loaded", "logits_done", "shift_ready", "exp_ready", "aff_ready", "turned", "best_ready", "listed",
             "relisted", "token_ready", "xs_turned", "xs_taken", "dve_step"))
        gathered = [s.sem(f"gathered{i}") for i in range(NPAIR)]
        with nc.Block() as block:
            @block.sync
            def _(sp):
                sp.dma_start(w[:], weight_tiles(A["w_router_2"][0])).then_inc(w_loaded, 16)
                sp.wait_ge(best_ready, 1)
                sp.dma_start(gate_dram, val[:]).then_inc(listed, 16)
                sp.dma_start(token_dram, idx_f[:]).then_inc(listed, 16)
                sp.wait_ge(listed, 32)
                sp.dma_start(gate[:], gate_dram.rearrange("(i e) s -> (e s) i", e=2),
                             allow_slow_non_contiguous=True).then_inc(relisted, 16)
                sp.dma_start(token_f[:], token_dram.rearrange("(i e) s -> (e s) i", e=2),
                             allow_slow_non_contiguous=True).then_inc(relisted, 16)
                sp.wait_ge(relisted, 32)

            @block.tensor
            def _(pe):
                pe.wait_ge(w_loaded, 16)
                for t in range(NT):
                    for k in range(KD):
                        last = nc.tensor.matmul(logit_ps[:, t, :], h_t[:, k, t * P:(t + 1) * P], w[:, k, :],
                                                start=(k == 0), stop=(k == KD - 1))
                last.then_inc(logits_done, 1)
                pe.wait_ge(aff_ready, 1)
                for t in range(NT):
                    last = nc.tensor.transpose(aff_ps[:, t * P:(t + 1) * P], aff[:, t, :], ident[:])
                last.then_inc(turned, 1)
                for g in range(2 * NPAIR):
                    i, half = g // 2, g % 2
                    pe.wait_ge(gathered[i], 16)
                    if g >= 4:
                        pe.wait_ge(xs_taken, g - 3)
                    for j in range(4):
                        c = 4 * half + j
                        last = nc.tensor.transpose(turn_ps[:, g % 4, j, :], xs[:, i, c * P:(c + 1) * P], ident[:])
                    last.then_inc(xs_turned, 1)

            @block.scalar
            def _(act):
                act.wait_ge(shift_ready, 1)
                nc.scalar.activation(expd[:], logit[:], ACT.Exp).then_inc(exp_ready, 1)
                for g in range(2 * NPAIR):
                    act.wait_ge(xs_turned, g + 1)
                    nc.scalar.copy(xs_t[:, g // 2, 4 * (g % 2):4 * (g % 2) + 4, :],
                                   turn_ps[:, g % 4, :, :]).then_inc(xs_taken, 1)

            @block.gpsimd
            def _(pool):
                pool.wait_ge(token_ready, 1)
                for i in range(NPAIR):
                    nc.gpsimd.indirect_dma_start(
                        out=xs[:, i, :], out_offset=None, in_=h_dram,
                        in_offset=bass.IndirectOffsetOnAxis(ap=token_u[:, i:i + 1], axis=0)).then_inc(gathered[i], 16)

            @block.vector
            def _(dve):
                step = Steps(dve, dve_step)
                dve.wait_ge(logits_done, 1)
                step(nc.vector.tensor_reduce(top[:], logit_ps[:], AX.X, ALU.max))
                nc.vector.tensor_tensor(logit[:], logit_ps[:], top[:].unsqueeze(2).to_broadcast([P, NT, NE]),
                                        ALU.subtract).then_inc(shift_ready, 1)
                dve.wait_ge(exp_ready, 1)
                step(nc.vector.tensor_reduce(total[:], expd[:], AX.X, ALU.add))
                step(nc.vector.reciprocal(total_inv[:], total[:]))
                nc.vector.tensor_tensor(aff[:], expd[:], total_inv[:].unsqueeze(2).to_broadcast([P, NT, NE]),
                                        ALU.mult).then_inc(aff_ready, 1)
                dve.wait_ge(turned, 1)
                step(nc.vector.tensor_copy(aff_t[:], aff_ps[:]))
                for r in range(CAP // 8):
                    eight = slice(8 * r, 8 * r + 8)
                    step(nc.vector.max(val[:, eight], aff_t[:]))
                    step(nc.vector.max_index(idx[:, eight], val[:, eight], aff_t[:]))
                    if r < CAP // 8 - 1:
                        step(nc.vector.match_replace(aff_t[:], val[:, eight], aff_t[:], -1.0))
                nc.vector.tensor_copy(idx_f[:], idx[:]).then_inc(best_ready, 1)
                dve.wait_ge(relisted, 32)
                nc.vector.tensor_copy(token_u[:], token_f[:]).then_inc(token_ready, 1)


def moe_phase(nc, A, ident, xs_t, token_f, gate, x):
    NS = 6
    NCH = FF // BANK
    KF = FF // P
    with Scope(nc, "moe") as s:
        slots = s.sb("slots", [P, NS, KD * BANK])
        xs = s.sb("xs", [P, 2, KD, CAP])
        silu = s.sb("silu", [CAP, 2, BANK])
        hid = s.sb("hid", [P, 2, BANK])
        hid_t = s.sb("hid_t", [P, KF, CAP])
        y = s.sb("y", [P, D])
        spread = s.sb("spread", [P, T])
        iota = s.sb("iota", [P, T])
        up_ps = s.ps("up_ps", [P, 2, 2, BANK])
        turn_ps = s.ps("turn_ps", [P, 2, BANK])
        y_ps = s.ps("y_ps", [CAP, 2, BANK])
        iota_loaded, silu_ready, turned, turn_taken, spread_ready, spread_done, added = (
            s.sem(x_) for x_ in ("iota_loaded", "silu_ready", "turned", "turn_taken", "spread_ready",
                                 "spread_done", "added"))
        y_taken = [s.sem(f"y_taken{i}") for i in range(2)]
        loaded = [s.sem(f"loaded{i}") for i in range(NS)]
        used = [s.sem(f"used{i}") for i in range(NS)]
        hid_ready = [s.sem(f"hid_ready{i}") for i in range(2)]
        xs_ready = [s.sem(f"xs_ready{i}") for i in range(2)]
        order = [(m, n) for n in range(NCH) for m in ("gate", "up")] + [("down", n) for n in range(NCH)]
        at = {c: i for i, c in enumerate(order)}
        assert len(order) == 2 * NS

        def up_slot(c):
            return slots[:, at[c] % NS, :].rearrange("p (k n) -> p k n", k=KD)

        def down_slot(c):
            return slots[:, at[c] % NS, :].rearrange("p (k n) -> p k n", n=D)

        def uses(i, e, c):
            return i * 4 + (2 * e + at[c] // NS)

        with nc.Block() as block:
            @block.sync
            def _(sp):
                sp.dma_start(iota[:], rows(A["iota512"], P)).then_inc(iota_loaded, 16)
                with sp.Fori(0, NPAIR) as i:
                    for e in range(2):
                        for c in order:
                            m, n = c
                            sp.wait_ge(used[at[c] % NS], uses(i, e, c))
                            w = A[f"w_{m}_2"][0, bass.ds(i * 2 + e, 1)]
                            if m == "down":
                                src = w[:, n * BANK:(n + 1) * BANK, :].rearrange("a (k p) n -> p (a k) n", p=P)
                                dst = down_slot(c)
                            else:
                                src = w.rearrange("a (k p) n -> p (a k) n", p=P)[:, :, n * BANK:(n + 1) * BANK]
                                dst = up_slot(c)
                            sp.dma_start(dst, src).then_inc(loaded[at[c] % NS], 16)

            @block.gpsimd
            def _(pool):
                with pool.Fori(0, NPAIR) as i:
                    for e in range(2):
                        pool.wait_ge(y_taken[e], i)
                        nc.gpsimd.tensor_copy(
                            xs[:, e], xs_t[:, bass.ds(i, 1), :, CAP * e:CAP * e + CAP].rearrange(
                                "p a k s -> p (a k) s")).then_inc(xs_ready[e], 1)

            @block.tensor
            def _(pe):
                def transposes(i, e, n):
                    pe.wait_ge(hid_ready[n % 2], i * 4 + (2 * e + n // 2 + 1))
                    pe.wait_ge(turn_taken, i * 8 + (4 * e + max(n - 1, 0)))
                    for j in range(4):
                        last = nc.tensor.transpose(turn_ps[:, n % 2, j * P:(j + 1) * P],
                                                   hid[:, n % 2, j * P:(j + 1) * P], ident[:])
                    last.then_inc(turned, 1)

                with pe.Fori(0, NPAIR) as i:
                    for e in range(2):
                        pe.wait_ge(xs_ready[e], i + 1)
                        if e == 0:
                            pe.wait_ge(added, i * 8)
                        for n in range(NCH):
                            for g, m in enumerate(("gate", "up")):
                                c = (m, n)
                                pe.wait_ge(loaded[at[c] % NS], uses(i, e, c) * 16 + 16)
                                pe.wait_ge(hid_ready[n % 2], i * 4 + (2 * e + n // 2))
                                for k in range(KD):
                                    last = nc.tensor.matmul(up_ps[0:CAP, n % 2, g, :], xs[:, e, k, :],
                                                            up_slot(c)[:, k, :], start=(k == 0), stop=(k == KD - 1))
                                last.then_inc(used[at[c] % NS], 1)
                            if n >= 1:
                                transposes(i, e, n - 1)
                        transposes(i, e, NCH - 1)
                        pe.wait_ge(y_taken[1 - e], i + e)
                        for n in range(NCH):
                            c = ("down", n)
                            pe.wait_ge(loaded[at[c] % NS], uses(i, e, c) * 16 + 16)
                            pe.wait_ge(turn_taken, i * 8 + (4 * e + n + 1))
                            for j in range(4):
                                k = 4 * n + j
                                for half in range(2):
                                    last = nc.tensor.matmul(y_ps[:, half, :], hid_t[:, k, :],
                                                            down_slot(c)[:, j, half * BANK:(half + 1) * BANK],
                                                            start=(k == 0), stop=(k == KF - 1))
                            last.then_inc(used[at[c] % NS], 1)
                    pe.wait_ge(spread_ready, i + 1)
                    pe.wait_ge(y_taken[1], i + 1)
                    for o in range(8):
                        t, half = o // 2, o % 2
                        pe.wait_ge(added, i * 8 + max(o - 3, 0))
                        nc.tensor.matmul(up_ps[:, (o // 2) % 2, o % 2, :], spread[:, t * P:(t + 1) * P],
                                         y[:, half * BANK:(half + 1) * BANK], start=True,
                                         stop=True).then_inc(spread_done, 1)

            @block.scalar
            def _(act):
                with act.Fori(0, NPAIR) as i:
                    for e in range(2):
                        for n in range(NCH + 1):
                            if n < NCH:
                                c = ("gate", n)
                                act.wait_ge(used[at[c] % NS], uses(i, e, c) + 1)
                                act.wait_ge(hid_ready[n % 2], i * 4 + (2 * e + n // 2))
                                nc.scalar.activation(silu[:, n % 2, :], up_ps[0:CAP, n % 2, 0, :],
                                                     ACT.Silu).then_inc(silu_ready, 1)
                            if n >= 1:
                                act.wait_ge(turned, i * 8 + (4 * e + n))
                                nc.scalar.copy(hid_t[:, 4 * n - 4:4 * n, :],
                                               turn_ps[:, (n - 1) % 2, :].rearrange(
                                                   "p (j s) -> p j s", j=4)[:, :, 0:CAP]).then_inc(turn_taken, 1)
                        c = ("down", NCH - 1)
                        act.wait_ge(used[at[c] % NS], uses(i, e, c) + 1)
                        if e == 0:
                            act.wait_ge(spread_done, i * 8)
                        nc.scalar.copy(y[CAP * e:CAP * e + CAP, :],
                                       y_ps[:].rearrange("p a n -> p (a n)")).then_inc(y_taken[e], 1)

            @block.vector
            def _(dve):
                dve.wait_ge(iota_loaded, 16)
                nc.vector.memset(hid[CAP:P], 0.0)
                with dve.Fori(0, NPAIR) as i:
                    dve.wait_ge(spread_done, i * 8)
                    nc.vector.tensor_scalar(spread[:], iota[:], token_f[:, bass.ds(i, 1)], gate[:, bass.ds(i, 1)],
                                            ALU.is_equal, ALU.mult).then_inc(spread_ready, 1)
                    for e in range(2):
                        for n in range(NCH):
                            c = ("up", n)
                            dve.wait_ge(used[at[c] % NS], uses(i, e, c) + 1)
                            dve.wait_ge(silu_ready, i * 8 + (4 * e + n + 1))
                            dve.wait_ge(turned, i * 8 + (4 * e + max(n - 1, 0)))
                            nc.vector.tensor_tensor(hid[0:CAP, n % 2, :], silu[:, n % 2, :], up_ps[0:CAP, n % 2, 1, :],
                                                    ALU.mult).then_inc(hid_ready[n % 2], 1)
                    for o in range(8):
                        t, half = o // 2, o % 2
                        part = x[:, t, half * BANK:(half + 1) * BANK]
                        dve.wait_ge(spread_done, i * 8 + (o + 1))
                        nc.vector.tensor_tensor(part, up_ps[:, (o // 2) % 2, o % 2, :], part, ALU.add).then_inc(added, 1)



def program(nc, A, out, taps=None):
    taps = taps or {}

    def tap(name, buf):
        if name in taps:
            with Scope(nc, "tap" + name) as s:
                done = s.sem("done")
                with nc.Block() as block:
                    @block.sync
                    def _(sp):
                        sp.dma_start(taps[name], buf[:]).then_inc(done, 16)
                        sp.wait_ge(done, 16)

    h_dram = nc.dram_tensor("h_rows", (T, D), F32, kind="Internal").ap()
    weight_dram = nc.dram_tensor("expert_weights", (NKEY, NKEY, T), F32, kind="Internal").ap()
    gate_dram = nc.dram_tensor("gate_list", (NE, CAP), F32, kind="Internal").ap()
    token_dram = nc.dram_tensor("token_list", (NE, CAP), F32, kind="Internal").ap()

    with Scope(nc, "all") as g:
        x = g.sb("x", [P, NT, D])
        ident = g.sb("ident", [P, P])
        halves = g.sb("halves", [P, P])
        ones = g.sb("ones", [P, P])
        loaded = g.sem("loaded")
        with nc.Block() as block:
            @block.sync
            def _(sp):
                sp.dma_start(ident[:], A["ident"]).then_inc(loaded, 16)
                sp.dma_start(halves[:], A["halves"]).then_inc(loaded, 16)
                sp.dma_start(x[:], A["x"][0].rearrange("(t p) d -> p t d", p=P)).then_inc(loaded, 16)
                sp.wait_ge(loaded, 48)

            @block.vector
            def _(dve):
                nc.vector.memset(ones[:], 1.0)

        with Scope(nc, "one") as b1:
            gate2 = b1.sb("gate2", [P, D])
            h_t = b1.sb("h_t", [P, KD, T])
            with Scope(nc, "adas") as b0:
                ada = b0.sb("ada", [P, 6, D])
                shift1, scale1, gate1, shift2, scale2 = (ada[:, i, :] for i in range(5))
                ada_phase(nc, A, ada)
                tap("ada", ada)
                with nc.Block() as block:
                    @block.scalar
                    def _(act):
                        nc.scalar.copy(gate2[:], ada[:, 5, :])
                norm_phase(nc, "n1", ident, x, A["norm1_g"], scale=scale1, shift=shift1, to_t=h_t)
                tap("h_t", h_t)
                with Scope(nc, "mix") as m:
                    mix_t = m.sb("mix_t", [P, KD, T])
                    with Scope(nc, "mixin") as mi:
                        feat = mi.sb("feat", [P, 18, T])
                        values = mi.sb("values", [P, NT, P])
                        first_projection(nc, A, h_t, feat, values)
                        tap("feat", feat)
                        with Scope(nc, "cv") as c:
                            conv_y = c.sb("conv_y", [P, 4, T])
                            gain = c.sb("gain", [P, 4])
                            load_columns(nc, "cg", gain, A["conv_out_g_col"])
                            gated_conv_phase(nc, A, feat, conv_y)
                            column_norm_phase(nc, "cn", [[(conv_y[:, i, :], gain[:, i:i + 1], mix_t[:, 4 + i, :])]
                                                         for i in range(4)], halves[:], DH)
                        with Scope(nc, "a1") as a:
                            attn = a.sb("attn", [P, NT, NH * DH])
                            first_attention(nc, A, ident, feat, values, attn)
                            tap("attn", attn)
                            norm_phase(nc, "an", ident, attn, A["attn_out_g"], width=NH * DH, groups=NH, to_t=mix_t)
                    tap("mix_t", mix_t)
                    out_projection(nc, "out1", A["w_out"], mix_t, x, A["b_out"], gate1)
                tap("x1", x)
                norm_phase(nc, "n2", ident, x, A["norm2_g"], scale=scale2, shift=shift2, to_t=h_t)
            with Scope(nc, "pe") as p:
                choice = p.sb("choice", [P, 3, NT, P])
                with Scope(nc, "q") as q:
                    query_t = q.sb("query_t", [P, NC, T])
                    query_projection(nc, A, h_t, query_t)
                    peer_choice_phase(nc, A, query_t, choice)
                tap("choice", choice)
                peer_weight_phase(nc, A, ident, choice, weight_dram)
            peer_dense_phase(nc, A, h_t, weight_dram, x, gate2[:])
            norm_phase(nc, "nf", ident, x, A["final_g"], keep=x)
            tap("x2", x)

        h_t = g.sb("h_t2", [P, KD, T])
        norm_phase(nc, "n3", ident, x, A["norm1_g_2"][0], to_t=h_t)
        with Scope(nc, "two") as b2:
            mix_t = b2.sb("mix_t", [P, KD, T])
            gain = b2.sb("gain", [P, KD])
            load_columns(nc, "mg", gain, A["mix_norm_g_col"])
            feat = b2.sb("feat", [P, 16, T])
            values = b2.sb("values", [P, NT, NA])
            second_projection(nc, A, h_t, feat, values)
            tap("feat2", feat)
            with Scope(nc, "hy") as hy:
                hy_y = hy.sb("hy_y", [P, 2, T])
                pool_y = hy.sb("pool_y", [P, 2, T])
                pool_phase(nc, A, feat, pool_y)
                tap("pool_y", pool_y)
                with Scope(nc, "ev") as ev:
                    even, odd = ev.sb("even", [P, NT, HY]), ev.sb("odd", [P, NT, HY])
                    filter_phase(nc, A, even, odd)
                    tap("even", even)
                    hyena_phase(nc, A, ident, feat, even, odd, hy_y)
                    tap("hy_y", hy_y)
                column_norm_phase(nc, "hn", [
                    [(y[:, i, :], gain[:, c + i:c + i + 1], mix_t[:, c + i, :]) for i in range(2)]
                    for y, c in ((hy_y, 0), (pool_y, 6))], ones[:], HY)
            with Scope(nc, "a2") as a:
                attn = a.sb("attn", [P, NT, NA])
                with Scope(nc, "bt") as bt:
                    table = bt.sb("table", [P, NH, 16 * 64])
                    bias_table_phase(nc, A, table)
                    second_attention(nc, A, ident, feat, values, table, attn)
                tap("attn2", attn)
                norm_phase(nc, "an2", ident, attn, A["mix_norm_g_2"][0, HY:HY + NA], width=NA, to_t=mix_t, t_chunk0=2)
            tap("mix_t2", mix_t)
            out_projection(nc, "out2", A["w_out_2"][0], mix_t, x)
        tap("x3", x)
        norm_phase(nc, "n4", ident, x, A["norm2_g_2"][0], to_t=h_t, out_dram=h_dram)
        xs_t = g.sb("xs_t", [P, NPAIR, KD, P])
        token_f, gate = g.sb("token_f", [P, NPAIR]), g.sb("gate", [P, NPAIR])
        router_phase(nc, A, ident, h_t, h_dram, gate_dram, token_dram, xs_t, token_f, gate)
        tap("token_f", token_f)
        tap("gate", gate)
        moe_phase(nc, A, ident, xs_t, token_f, gate, x)
        tap("x4", x)
        norm_phase(nc, "no", ident, x, A["final_g_2"], out_dram=out[0])


def load_columns(nc, name, dst, columns_dram):
    with Scope(nc, name) as s:
        loaded = s.sem("loaded")
        with nc.Block() as block:
            @block.sync
            def _(sp):
                sp.dma_start(dst[:], columns_dram).then_inc(loaded, 16)
                sp.wait_ge(loaded, 16)



def shape_tables():
    f = np.float32
    c = {}
    c["ident"] = np.eye(P, dtype=f)
    half = np.arange(P) // 64
    c["halves"] = (half[:, None] == half[None, :]).astype(f)
    c["iota"] = np.arange(NKEY).astype(f)
    c["iota512"] = np.arange(T).astype(f)
    q, k = np.arange(P)[:, None], np.arange(2 * P)[None, :]
    diff = q + P - k
    c["window_mask"] = np.where((diff >= 0) & (diff < P), 0.0, NEG).astype(f)
    bands = (FE - 1) // 2
    t = np.linspace(0.0, 1.0, T, dtype=f)[:, None].astype(np.float64)
    ang = (f(TWO_PI) * np.arange(T, dtype=f)[:, None] / f(T)).astype(f)
    band = np.linspace(1e-4, bands - 1, bands, dtype=f)[None, :]
    turn = (band * ang).astype(f).astype(np.float64)
    c["pos_t"] = np.ascontiguousarray(np.concatenate([t, np.cos(turn), -np.sin(turn)], -1).T.astype(f))
    lo, hi = np.log(1e-2) / 0.3, np.log(1e-2) / 1.5
    decay = np.exp(-t * np.abs(np.linspace(lo, hi, HY, dtype=f)).astype(np.float64))
    back = decay.copy()
    back[0] = 0.0
    c["decay"] = np.concatenate([decay, back], -1).astype(f)
    turn = np.pi * ((2 * np.arange(T)[None, :] + 1) * np.arange(T)[:, None] % (4 * T)) / (2 * T)
    c["dft_cos"], c["dft_sin"] = np.cos(turn).astype(f), np.sin(turn).astype(f)
    c["dft_cos_t"] = np.ascontiguousarray(c["dft_cos"].T)
    c["dft_sin_t"] = np.ascontiguousarray(c["dft_sin"].T)
    at = np.arange(T)
    c["pool_inv"] = np.stack([1.0 / (np.clip(at + w // 2, 0, T) - np.clip(at - w // 2, 0, T))
                              for w in (2, 4, 8, 16)]).astype(f)
    j, col = np.arange(64)[:, None], (np.arange(P) % 64)[None, :]
    start = np.clip(col - 8, 0, 48)
    inside = (j >= start) & (j < start + 16)
    pick = np.zeros((32, 64, P), f)
    for dc in range(31):
        pick[dc] = inside & (j - col + 15 == dc)
    pick[31] = np.where(inside, 0.0, NEG)
    c["bias_pick"] = pick
    return c


PLAIN = ["x", "w_ada", "b_ada", "norm1_g", "w_in", "b_in", "attn_sinks", "attn_out_g", "w_out",
         "b_out", "norm2_g", "w_query", "peer_v", "final_g", "norm1_g_2", "w_in_2", "hy_f_w1_2",
         "hy_f_b1_2", "hy_f_w2_2", "hy_f_b2_2", "hy_f_wout_2", "hy_f_freq_2", "pool_w_2",
         "mix_norm_g_2", "w_out_2", "norm2_g_2", "w_router_2", "w_gate_2", "w_up_2", "w_down_2",
         "final_g_2"]


def laid_out(inputs):
    a = {n: np.ascontiguousarray(inputs[n]) for n in PLAIN}
    u = np.asarray(inputs["peer_u"]).reshape(ETILES, P, KD, P)
    a["u_tiles"] = np.ascontiguousarray(u.transpose(0, 3, 2, 1))
    for i in (1, 2):
        a[f"keys_t{i}"] = np.ascontiguousarray(np.asarray(inputs[f"peer_keys{i}"]).transpose(2, 0, 1))
    a["rpb_t"] = np.ascontiguousarray(np.asarray(inputs["na_rpb_2"])[0].transpose(2, 0, 1).reshape(31, NH * 15))
    for n, name in (("c", "c"), ("b_in", "b_in"), ("conv_w", "conv_w"), ("conv_out_g", "conv_out_g"),
                    ("hy_short_w", "hy_short_w_2"), ("hy_short_b", "hy_short_b_2"), ("hy_skip", "hy_skip_2"),
                    ("pool_scale", "pool_scale_2"), ("mix_norm_g", "mix_norm_g_2")):
        v = np.asarray(inputs[name])
        v = v.reshape(v.shape[-2:] if n in ("conv_w", "hy_short_w") else (1, -1))
        v = v.reshape(v.shape[0], -1, P).transpose(2, 1, 0)
        a[f"{n}_col"] = np.ascontiguousarray(v if v.shape[2] > 1 else v[:, :, 0])
    a.update(shape_tables())
    return a


def kernel(**inputs):
    import concourse.bacc as bacc
    from concourse.bass_utils import run_bass_kernel_spmd

    nc = bacc.Bacc("TRN2", target_bir_lowering=False, num_devices=1)
    arrays = {f"in_{n}": a for n, a in laid_out(inputs).items()}
    aps = {n[3:]: nc.dram_tensor(n, a.shape, mybir.dt.from_np(a.dtype), kind="ExternalInput").ap()
           for n, a in arrays.items()}
    out = nc.dram_tensor("out", (1, T, D), F32, kind="ExternalOutput").ap()
    program(nc, aps, out)
    r = run_bass_kernel_spmd(nc, [arrays], core_ids=[0])
    return r.results[0]["out"]
```

```python
from contextlib import ExitStack

import concourse.bass as bass
import numpy as np
from concourse import mybir

F32 = mybir.dt.float32
U32 = mybir.dt.uint32
F32R = mybir.dt.float32r
ALU = mybir.AluOpType
ACT = mybir.ActivationFunctionType
AX = mybir.AxisListType

P = 128
T = 512
NT = T // P
D = 1024
KD = D // P
DH = 64
NH = 8
BANK = 512
EPS = 1e-6
NEG = -1e30
LOWEST = -3.0e38

NKEY = 128
PH = 8
PK = 16
NC = 2 * PH
ETILES = NKEY

NE = 16
CAP = 64
FF = 2048
NPAIR = NE // 2


class Steps:

    def __init__(self, eng, sem, base=0):
        self.eng, self.sem, self.base, self.n = eng, sem, base, 0

    def __call__(self, ins):
        ins.then_inc(self.sem, 1)
        self.n += 1
        self.eng.wait_ge(self.sem, self.base + self.n)


class Scope(ExitStack):

    def __init__(self, nc, name):
        super().__init__()
        self.nc, self.name, self.sems = nc, name, []
        self.callback(self.free_semaphores)

    def free_semaphores(self):
        for sem in self.sems:
            self.nc.gpsimd.sem_clear(sem)
            self.nc.release_semaphore(sem)

    def sb(self, name, shape, dt=F32):
        return self.enter_context(self.nc.sbuf_tensor(f"{self.name}_{name}", shape, dt))

    def ps(self, name, shape, dt=F32):
        return self.enter_context(self.nc.psum_tensor(f"{self.name}_{name}", shape, dt))

    def sem(self, name):
        self.sems.append(self.nc.alloc_semaphore(f"{self.name}_{name}"))
        return self.sems[-1]


def split_hi(eng, part, src):
    return eng.copy(part, src)


def split_lo(eng, part_lo, src, part_hi):
    return eng.tensor_tensor(part_lo, src, part_hi.bitcast(F32), ALU.subtract)


def rows(vector_dram, n):
    return vector_dram.partition_broadcast(n)


def weight_tiles(w_dram):
    return w_dram.rearrange("(k p) n -> p k n", p=P)



def norm_phase(nc, name, ident, x, g_dram, width=D, groups=1, scale=None, shift=None,
               keep=None, to_t=None, t_chunk0=0, out_dram=None):
    gw = width // groups
    chunks = width // P
    with Scope(nc, name) as s:
        g_rows = s.sb("g_rows", [P, width])
        gain = s.sb("gain", [P, width]) if scale is not None else None
        square = s.sb("square", [P, 2, width])
        h = s.sb("h", [P, NT, width]) if keep is None else keep
        mean = s.sb("mean", [P, NT * groups])
        root = s.sb("root", [P, NT * groups])
        rstd = s.sb("rstd", [P, NT * groups])
        per_bank = min(chunks, 4)
        n_banks = chunks // per_bank
        turned = s.ps("turned", [P, NT * n_banks, 4, P])
        g_loaded, squared, sq_summed, mean_ready, root_ready = (s.sem(n) for n in (
            "g_loaded", "squared", "sq_summed", "mean_ready", "root_ready"))
        dve_step, h_ready, turn_done, hi_ready, stored = (s.sem(n) for n in (
            "dve_step", "h_ready", "turn_done", "hi_ready", "stored"))

        def part_of(b, hl):
            c0 = t_chunk0 + (b % n_banks) * per_bank
            t = b // n_banks
            return to_t[:, hl, c0:c0 + per_bank, t * P:(t + 1) * P]

        with nc.Block() as block:
            @block.sync
            def _(sp):
                sp.dma_start(g_rows[:], rows(g_dram, P)).then_inc(g_loaded, 16)
                if out_dram is not None:
                    for t in range(NT):
                        sp.wait_ge(h_ready, t + 1)
                        sp.dma_start(out_dram[t * P:(t + 1) * P, :], h[:, t, :]).then_inc(stored, 16)
                    sp.wait_ge(stored, 16 * NT)

            @block.scalar
            def _(act):
                for t in range(NT):
                    if t >= 2:
                        act.wait_ge(squared if groups == 1 else sq_summed, t - 1)
                    nc.scalar.activation(square[:, t % 2, :], x[:, t, :], ACT.Square,
                                         accum_out=mean[:, t:t + 1] if groups == 1 else None).then_inc(squared, 1)
                act.wait_ge(mean_ready, 1)
                nc.scalar.activation(root[:], mean[:], ACT.Sqrt).then_inc(root_ready, 1)
                if to_t is not None:
                    for b in range(NT * n_banks):
                        act.wait_ge(turn_done, b + 1)
                        split_hi(nc.scalar, part_of(b, 0), turned[:, b, 0:per_bank, :]).then_inc(hi_ready, 1)

            @block.vector
            def _(dve):
                step = Steps(dve, dve_step)
                g = g_rows
                if scale is not None:
                    dve.wait_ge(g_loaded, 16)
                    step(nc.vector.scalar_tensor_tensor(out=gain[:], in0=scale, scalar=1.0, in1=g_rows[:],
                                                        op0=ALU.add, op1=ALU.mult))
                    g = gain
                if groups == 1:
                    dve.wait_ge(squared, NT)
                else:
                    for t in range(NT):
                        dve.wait_ge(squared, t + 1)
                        nc.vector.tensor_reduce(
                            mean[:, t * groups:(t + 1) * groups],
                            square[:, t % 2, :].rearrange("p (g w) -> p g w", g=groups), AX.X,
                            ALU.add).then_inc(sq_summed, 1)
                    dve.wait_ge(sq_summed, NT)
                nc.vector.tensor_scalar(mean[:], mean[:], 1.0 / gw, EPS, ALU.mult,
                                        ALU.add).then_inc(mean_ready, 1)
                dve.wait_ge(root_ready, 1)
                step(nc.vector.reciprocal(rstd[:], root[:]))
                dve.wait_ge(g_loaded, 16)

                def rest(t):
                    for b in range(t * n_banks, (t + 1) * n_banks) if to_t is not None else ():
                        dve.wait_ge(hi_ready, b + 1)
                        split_lo(nc.vector, part_of(b, 1), turned[:, b, 0:per_bank, :], part_of(b, 0))

                for t in range(NT):
                    if groups == 1:
                        ins = nc.vector.scalar_tensor_tensor(
                            out=h[:, t, :], in0=x[:, t, :], scalar=rstd[:, t:t + 1], in1=g[:],
                            op0=ALU.mult, op1=ALU.mult)
                    else:
                        r = rstd[:, t * groups:(t + 1) * groups].unsqueeze(2).to_broadcast([P, groups, gw])
                        step(nc.vector.tensor_tensor(
                            h[:, t, :].rearrange("p (g w) -> p g w", g=groups),
                            x[:, t, :].rearrange("p (g w) -> p g w", g=groups), r, ALU.mult))
                        ins = nc.vector.tensor_tensor(h[:, t, :], h[:, t, :], g_rows[:], ALU.mult)
                    if scale is not None:
                        step(ins)
                        ins = nc.vector.tensor_tensor(h[:, t, :], h[:, t, :], shift, ALU.add)
                    ins.then_inc(h_ready, 1)
                    if t >= 1:
                        rest(t - 1)
                rest(NT - 1)

            @block.tensor
            def _(pe):
                if to_t is None:
                    return
                for b in range(NT * n_banks):
                    t, half = b // n_banks, b % n_banks
                    pe.wait_ge(h_ready, t + 1)
                    for j in range(per_bank):
                        c = half * per_bank + j
                        last = nc.tensor.transpose(turned[:, b, j, :], h[:, t, c * P:(c + 1) * P], ident[:])
                    last.then_inc(turn_done, 1)



def product_phase(nc, name, chunks, width, extra_loads=()):
    RAW, SPLIT, PARTS = 6, 6, 4
    TILES = KD // PARTS
    pieces = [(n, h) for n in range(len(chunks)) for h in range(PARTS)]
    last_of = [PARTS * n + PARTS for n in range(len(chunks))]
    with Scope(nc, name) as s:
        raw = s.sb("raw", [P, RAW, TILES, width])
        split = s.sb("split", [P, SPLIT, 2, TILES, width], F32R)
        banks = s.ps("banks", [P, 8, BANK])
        loaded = [s.sem(f"loaded{i}") for i in range(RAW)]
        extra, hi_ready, lo_ready, piece_done, act_taken, dve_taken, act_step, dve_step = (s.sem(n) for n in (
            "extra", "hi_ready", "lo_ready", "piece_done", "act_taken", "dve_taken", "act_step", "dve_step"))
        landed, need = [0] * RAW, []
        for p, (n, h) in enumerate(pieces):
            landed[p % RAW] += 16 * len(chunks[n][0](raw[:, p % RAW], slice(0, TILES)))
            need.append(landed[p % RAW])
        taken_by = [[sum(o[3] == on_act for _, outs, _ in chunks[:n + 1] for o in outs) for n in range(len(chunks))]
                    for on_act in (False, True)]
        with nc.Block() as block:
            @block.sync
            def _(sp):
                for p, (n, h) in enumerate(pieces):
                    if p >= RAW:
                        sp.wait_ge(lo_ready, p - RAW + 1)
                    for to, src in chunks[n][0](raw[:, p % RAW], slice(h * TILES, (h + 1) * TILES)):
                        sp.dma_start(to, src).then_inc(loaded[p % RAW], 16)
                    if p == 0:
                        for to, src in extra_loads:
                            sp.dma_start(to, src).then_inc(extra, 16)

            @block.tensor
            def _(pe):
                for p, (n, h) in enumerate(pieces):
                    pe.wait_ge(lo_ready, p + 1)
                    if h == 0 and n >= 2:
                        for sem, on_act in ((dve_taken, False), (act_taken, True)):
                            if taken_by[on_act][n - 2]:
                                pe.wait_ge(sem, taken_by[on_act][n - 2])
                    w = split[:, p % SPLIT]
                    for o, (m, cols, operands, _, _) in enumerate(chunks[n][1]):
                        for k in range(TILES):
                            for i, (w_part, part) in enumerate(((0, 0), (0, 1), (1, 0))):
                                a, b = operands(w[:, w_part, k], part, h * TILES + k)
                                last = nc.tensor.matmul(
                                    banks[0:m, 4 * (n % 2) + o, 0:cols], a, b,
                                    start=(h == 0 and k == 0 and i == 0),
                                    stop=(h == PARTS - 1 and k == TILES - 1 and i == 2))
                    last.then_inc(piece_done, 1)

            def run(eng, nc_eng, on_act, taken, step, split_piece):
                def takes(n):
                    if n == 0:
                        eng.wait_ge(extra, 16 * len(extra_loads))
                    eng.wait_ge(piece_done, last_of[n])
                    for o, (m, cols, _, by_act, take) in enumerate(chunks[n][1]):
                        if by_act == on_act:
                            take(nc_eng, banks[0:m, 4 * (n % 2) + o, 0:cols], step).then_inc(taken, 1)

                for p, (n, h) in enumerate(pieces):
                    split_piece(p)
                    if h == PARTS - 1 and n >= 1:
                        takes(n - 1)
                takes(len(chunks) - 1)

            @block.scalar
            def _(act):
                def split_piece(p):
                    act.wait_ge(loaded[p % RAW], need[p])
                    if p >= SPLIT:
                        act.wait_ge(piece_done, p - SPLIT + 1)
                    cols = chunks[pieces[p][0]][2]
                    split_hi(nc.scalar, split[:, p % SPLIT, 0, :, cols], raw[:, p % RAW, :, cols]).then_inc(hi_ready, 1)

                run(act, nc.scalar, True, act_taken, Steps(act, act_step), split_piece)

            @block.vector
            def _(dve):
                def split_piece(p):
                    dve.wait_ge(hi_ready, p + 1)
                    cols = chunks[pieces[p][0]][2]
                    split_lo(nc.vector, split[:, p % SPLIT, 1, :, cols], raw[:, p % RAW, :, cols],
                             split[:, p % SPLIT, 0, :, cols]).then_inc(lo_ready, 1)

                run(dve, nc.vector, False, dve_taken, Steps(dve, dve_step), split_piece)


def copy_to(dst):
    def take(eng, bank, step):
        return eng.copy(dst, bank) if on_scalar(eng) else eng.tensor_copy(dst, bank)
    return take


def on_scalar(eng):
    return "activation" in dir(eng)


def add_column_to(dst, column):
    def take(eng, bank, step):
        if on_scalar(eng):
            return eng.activation(dst, bank, ACT.Identity, bias=column)
        return eng.tensor_scalar(dst, bank, column, None, ALU.add)
    return take



def attention_phase(nc, name, ident, units, q_of, k_of, v_of, bias_of, o_of, keys_max, sinks=None):
    n = len(units)
    chunks_max = keys_max // P
    with Scope(nc, name) as s:
        biased = s.sb("biased", [P, 2, keys_max])
        expd = s.sb("expd", [P, 2, keys_max])
        expd_t = s.sb("expd_t", [P, 2, chunks_max, P])
        top = s.sb("top", [P, n])
        minus_top = s.sb("minus_top", [P, n])
        total = s.sb("total", [P, n])
        sink_exp = s.sb("sink_exp", [P, n])
        total_inv = s.sb("total_inv", [P, n])
        score_ps = s.ps("score_ps", [P, 2, BANK])
        turn_ps = s.ps("turn_ps", [P, 2, 4, P])
        out_ps = s.ps("out_ps", [P, 2, BANK])
        scored, biased_ready, minus_ready, exp_ready, sink_ready, turned, turn_taken, weighed, out_taken = (
            s.sem(x) for x in ("scored", "biased_ready", "minus_ready", "exp_ready", "sink_ready",
                               "turned", "turn_taken", "weighed", "out_taken"))
        dve_step = s.sem("dve_step")
        with nc.Block() as block:
            @block.tensor
            def _(pe):
                for i in range(n + 2):
                    if i < n:
                        keys = k_of(*units[i])
                        if i >= 2:
                            pe.wait_ge(biased_ready, i - 1)
                        nc.tensor.matmul(score_ps[:, i % 2, 0:keys.shape[1]], q_of(*units[i]), keys,
                                         start=True, stop=True).then_inc(scored, 1)
                    if 1 <= i <= n:
                        j = i - 1
                        pe.wait_ge(exp_ready, j + 1)
                        if j >= 2:
                            pe.wait_ge(turn_taken, j - 1)
                        for c in range(k_of(*units[j]).shape[1] // P):
                            last = nc.tensor.transpose(turn_ps[:, j % 2, c, :],
                                                       expd[:, j % 2, c * P:(c + 1) * P], ident[:])
                        last.then_inc(turned, 1)
                    if i >= 2:
                        j = i - 2
                        pe.wait_ge(turn_taken, j + 1)
                        if j >= 2:
                            pe.wait_ge(out_taken, j - 1)
                        values = v_of(*units[j])
                        for c, v in enumerate(values):
                            last = nc.tensor.matmul(out_ps[:, j % 2, 0:DH], expd_t[:, j % 2, c, :], v,
                                                    start=(c == 0), stop=(c == len(values) - 1))
                        last.then_inc(weighed, 1)

            @block.scalar
            def _(act):
                for i in range(n + 1):
                    if i < n:
                        kw = k_of(*units[i]).shape[1]
                        act.wait_ge(minus_ready, i + 1)
                        if i >= 2:
                            act.wait_ge(turned, i - 1)
                        nc.scalar.activation(expd[:, i % 2, 0:kw], biased[:, i % 2, 0:kw], ACT.Exp,
                                             bias=minus_top[:, i:i + 1],
                                             accum_out=total[:, i:i + 1]).then_inc(exp_ready, 1)
                        if sinks is not None:
                            nc.scalar.activation(sink_exp[:, i:i + 1], sinks(*units[i]), ACT.Exp,
                                                 bias=minus_top[:, i:i + 1]).then_inc(sink_ready, 1)
                    if i >= 1:
                        j = i - 1
                        nch = k_of(*units[j]).shape[1] // P
                        act.wait_ge(turned, j + 1)
                        if j >= 2:
                            act.wait_ge(weighed, j - 1)
                        nc.scalar.copy(expd_t[:, j % 2, 0:nch, :],
                                       turn_ps[:, j % 2, 0:nch, :]).then_inc(turn_taken, 1)

            @block.vector
            def _(dve):
                step = Steps(dve, dve_step)
                for i in range(n + 2):
                    if i < n:
                        kw = k_of(*units[i]).shape[1]
                        dve.wait_ge(scored, i + 1)
                        if i >= 2:
                            dve.wait_ge(exp_ready, i - 1)
                        nc.vector.scalar_tensor_tensor(
                            out=biased[:, i % 2, 0:kw], in0=score_ps[:, i % 2, 0:kw], scalar=DH ** -0.5,
                            in1=bias_of(*units[i]), op0=ALU.mult, op1=ALU.add).then_inc(biased_ready, 1)
                        dve.wait_ge(biased_ready, i + 1)
                        step(nc.vector.reduce_max(top[:, i:i + 1], biased[:, i % 2, 0:kw], AX.X))
                        if sinks is not None:
                            step(nc.vector.tensor_tensor(top[:, i:i + 1], top[:, i:i + 1],
                                                         sinks(*units[i]), ALU.max))
                        nc.vector.tensor_scalar(minus_top[:, i:i + 1], top[:, i:i + 1], -1.0, None,
                                                ALU.mult).then_inc(minus_ready, 1)
                    if i >= 2:
                        j = i - 2
                        dve.wait_ge(exp_ready, j + 1)
                        if sinks is not None:
                            dve.wait_ge(sink_ready, j + 1)
                            step(nc.vector.tensor_tensor(total[:, j:j + 1], total[:, j:j + 1],
                                                         sink_exp[:, j:j + 1], ALU.add))
                        step(nc.vector.reciprocal(total_inv[:, j:j + 1], total[:, j:j + 1]))
                        dve.wait_ge(weighed, j + 1)
                        nc.vector.tensor_scalar(o_of(*units[j]), out_ps[:, j % 2, 0:DH],
                                                total_inv[:, j:j + 1], None,
                                                ALU.mult).then_inc(out_taken, 1)



def column_norm_phase(nc, name, jobs, ones_of, width, to_t):
    with Scope(nc, name) as s:
        n = len(jobs)
        most = max(len(j) for j in jobs)
        square = s.sb("square", [P, n, most, T])
        mean = s.sb("mean", [P, n, T])
        root = s.sb("root", [P, n, T])
        rstd = s.sb("rstd", [P, n, T])
        sum_ps = s.ps("sum_ps", [P, n, BANK])
        normed = s.sb("normed", [P, n * most, T])
        flat = [(j, *entry) for j, job in enumerate(jobs) for entry in job]
        squared, summed, mean_ready, root_ready, dve_step, normed_ready, hi_ready = (s.sem(x) for x in (
            "squared", "summed", "mean_ready", "root_ready", "dve_step", "normed_ready", "hi_ready"))
        with nc.Block() as block:
            @block.scalar
            def _(act):
                for j, job in enumerate(jobs):
                    for m, (tile, _, _) in enumerate(job):
                        nc.scalar.activation(square[:, j, m, :], tile, ACT.Square).then_inc(squared, 1)
                for j in range(n):
                    act.wait_ge(mean_ready, j + 1)
                    nc.scalar.activation(root[:, j, :], mean[:, j, :], ACT.Sqrt).then_inc(root_ready, 1)
                for m, (_, _, _, c) in enumerate(flat):
                    act.wait_ge(normed_ready, m + 1)
                    split_hi(nc.scalar, to_t[:, 0, c, :], normed[:, m, :]).then_inc(hi_ready, 1)

            @block.tensor
            def _(pe):
                done = 0
                for j, job in enumerate(jobs):
                    for m in range(len(job)):
                        done += 1
                        pe.wait_ge(squared, done)
                        last = nc.tensor.matmul(sum_ps[:, j, :], ones_of, square[:, j, m, :],
                                                start=(m == 0), stop=(m == len(job) - 1))
                    last.then_inc(summed, 1)

            @block.vector
            def _(dve):
                step = Steps(dve, dve_step)
                for j in range(n):
                    dve.wait_ge(summed, j + 1)
                    nc.vector.tensor_scalar(mean[:, j, :], sum_ps[:, j, :], 1.0 / width, EPS, ALU.mult,
                                            ALU.add).then_inc(mean_ready, 1)
                for j in range(n):
                    dve.wait_ge(root_ready, j + 1)
                    step(nc.vector.reciprocal(rstd[:, j, :], root[:, j, :]))
                    for m, (of, tile, gain, c) in enumerate(flat):
                        if of == j:
                            nc.vector.scalar_tensor_tensor(
                                out=normed[:, m, :], in0=tile, scalar=gain, in1=rstd[:, j, :],
                                op0=ALU.mult, op1=ALU.mult).then_inc(normed_ready, 1)
                for m, (_, _, _, c) in enumerate(flat):
                    dve.wait_ge(hi_ready, m + 1)
                    split_lo(nc.vector, to_t[:, 1, c, :], normed[:, m, :], to_t[:, 0, c, :])



def ada_phase(nc, A, ada, extra_loads, ones):
    flat = ada[:].rearrange("p i d -> p (i d)")
    w = weight_tiles(A["w_ada"])
    SLOTS = 4
    n_rounds = 6 * D // BANK // SLOTS
    with Scope(nc, "ada") as s:
        c_col = s.sb("c_col", [P, KD])
        silu_col = s.sb("silu_col", [P, KD])
        silu_wide = s.sb("silu_wide", [P, KD, P])
        slots = s.sb("slots", [P, SLOTS, KD, BANK])
        banks = s.ps("banks", [P, SLOTS, BANK])
        loaded = [s.sem(f"loaded{i}") for i in range(SLOTS)]
        c_loaded, b_loaded, extra_loaded, silu_ready, wide_ready, product_done, taken = (s.sem(n) for n in (
            "c_loaded", "b_loaded", "extra_loaded", "silu_ready", "wide_ready", "product_done", "taken"))
        with nc.Block() as block:
            @block.sync
            def _(sp):
                def load(i, j):
                    sp.dma_start(slots[:, j], w[:, :, bass.ds(i * (SLOTS * BANK) + j * BANK, BANK)]).then_inc(loaded[j], 16)

                sp.dma_start(c_col[:], A["c_col"]).then_inc(c_loaded, 16)
                for j in range(SLOTS):
                    load(0, j)
                    if j == 1:
                        sp.dma_start(flat, rows(A["b_ada"], P)).then_inc(b_loaded, 16)
                with sp.Fori(1, n_rounds) as i:
                    for j in range(SLOTS):
                        sp.wait_ge(taken, i * SLOTS + (j + 1 - SLOTS))
                        load(i, j)
                for to, src in extra_loads:
                    sp.dma_start(to, src).then_inc(extra_loaded, 16)
                sp.wait_ge(extra_loaded, 16 * len(extra_loads))

            @block.scalar
            def _(act):
                act.wait_ge(c_loaded, 16)
                nc.scalar.activation(silu_col[:], c_col[:], ACT.Silu).then_inc(silu_ready, 1)
                act.wait_ge(silu_ready, 1)
                nc.scalar.copy(silu_wide[:], silu_col[:].unsqueeze(2).to_broadcast([P, KD, P])).then_inc(wide_ready, 1)

            @block.tensor
            def _(pe):
                pe.wait_ge(wide_ready, 1)
                with pe.Fori(0, n_rounds) as i:
                    for j in range(SLOTS):
                        pe.wait_ge(loaded[j], i * 16 + 16)
                        for k in range(KD):
                            last = nc.tensor.matmul(banks[:, j, :], silu_wide[:, k, :], slots[:, j, k, :],
                                                    start=(k == 0), stop=(k == KD - 1))
                        last.then_inc(product_done, 1)

            @block.vector
            def _(dve):
                nc.vector.memset(ones[:], 1.0)
                dve.wait_ge(b_loaded, 16)
                with dve.Fori(0, n_rounds) as i:
                    for j in range(SLOTS):
                        dve.wait_ge(product_done, i * SLOTS + (j + 1))
                        part = flat[:, bass.ds(i * (SLOTS * BANK) + j * BANK, BANK)]
                        nc.vector.tensor_tensor(part, banks[:, j, :], part, ALU.add).then_inc(taken, 1)


def first_projection(nc, A, h_t, feat, values):
    w = weight_tiles(A["w_in"])
    b = A["b_in"]
    AW, KVW, CW = 512, 128, 512
    o_k, o_v, o_b, o_c, o_u = AW, AW + KVW, AW + 2 * KVW, AW + 2 * KVW + CW, AW + 2 * KVW + 2 * CW
    with Scope(nc, "in1b") as s:
        bias = s.sb("bias", [P, 18])
        v_bias = s.sb("v_bias", [P, P])

        def feature(col, f):
            return (P, T, lambda w_k, part, k: (w_k[:, col:col + P], h_t[:, part, k, :]), f % 2 == 0,
                    add_column_to(feat[:, f, :], bias[:, f:f + 1]))

        def token(t):
            return (P, P, lambda w_k, part, k: (h_t[:, part, k, t * P:(t + 1) * P], w_k[:, 256:384]), t % 2 == 0,
                    copy_to(values[:, t, :]))

        def plain(col):
            return lambda slot, tiles: [(slot[:, :, :], w[:, tiles, col:col + BANK])]

        def doubled_keys(slot, tiles):
            return [(slot[:, :, 64 * i:64 * i + 64], w[:, tiles, o_k + 64 * (i // 2):o_k + 64 * (i // 2) + 64])
                    for i in range(4)]

        def the_values(slot, tiles):
            return [(slot[:, :, 256:384], w[:, tiles, o_v:o_v + P])]

        whole = slice(0, BANK)
        chunks = [(plain(0), [feature(P * j, j) for j in range(4)], whole),
                  (doubled_keys, [feature(0, 4), feature(P, 5)], slice(0, 256)),
                  (the_values, [token(t) for t in range(NT)], slice(256, 384))]
        for n, col in enumerate((o_b, o_c, o_u)):
            chunks.append((plain(col), [feature(P * j, 6 + 4 * n + j) for j in range(4)], whole))
        loads = [(bias[:, 0:4], A["b_in_col"][:, 0:4])]
        for i in range(4):
            half = slice(64 * (i % 2), 64 * (i % 2) + 64)
            loads.append((bias[half, 4 + i // 2:5 + i // 2],
                          b[o_k + 64 * (i // 2):o_k + 64 * (i // 2) + 64].rearrange("(p a) -> p a", a=1)))
        loads += [(bias[:, 6:18], A["b_in_col"][:, 6:18]), (v_bias[:], rows(b[o_v:o_v + P], P))]
        product_phase(nc, "in1", chunks, BANK, loads)
        with nc.Block() as block:
            @block.vector
            def _(dve):
                nc.vector.tensor_tensor(values[:], values[:],
                                        v_bias[:].unsqueeze(1).to_broadcast([P, NT, P]), ALU.add)


def gated_conv_phase(nc, A, feat, conv_y):
    with Scope(nc, "conv") as s:
        z = s.sb("z", [P, 4, T + 2])
        taps = s.sb("taps", [P, 4, 3])
        acc = s.sb("acc", [P, 4, T])
        taps_loaded, dve_step = s.sem("taps_loaded"), s.sem("dve_step")
        with nc.Block() as block:
            @block.sync
            def _(sp):
                sp.dma_start(taps[:], A["conv_w_col"]).then_inc(taps_loaded, 16)

            @block.vector
            def _(dve):
                step = Steps(dve, dve_step)
                step(nc.vector.memset(z[:, :, 0:2], 0.0))
                step(nc.vector.tensor_tensor(z[:, :, 2:T + 2], feat[:, 10:14, :], feat[:, 14:18, :], ALU.mult))
                dve.wait_ge(taps_loaded, 16)
                for c in range(4):
                    step(nc.vector.tensor_scalar(acc[:, c, :], z[:, c, 0:T], taps[:, c, 0:1], None, ALU.mult))
                    for j in (1, 2):
                        step(nc.vector.scalar_tensor_tensor(
                            out=acc[:, c, :], in0=z[:, c, j:j + T], scalar=taps[:, c, j:j + 1],
                            in1=acc[:, c, :], op0=ALU.mult, op1=ALU.add))
                nc.vector.tensor_tensor(conv_y[:], acc[:], feat[:, 6:10, :], ALU.mult)


def out_projection(nc, name, w_dram, mix_t, x, bias_dram=None, gate=None):
    w = weight_tiles(w_dram)
    with Scope(nc, name + "b") as s:
        b_rows = s.sb("b_rows", [P, D])
        part = s.sb("part", [P, 2, BANK])

        def output(n, t):
            cols = slice(n * BANK, (n + 1) * BANK)

            def take(eng, bank, step):
                src = bank
                if gate is not None:
                    src = part[:, t % 2, :]
                    step(eng.tensor_tensor(src, bank, b_rows[:, cols], ALU.add))
                    step(eng.tensor_tensor(src, src, gate[:, cols], ALU.mult))
                return eng.tensor_tensor(x[:, t, cols], src, x[:, t, cols], ALU.add)

            return (P, BANK, lambda w_k, part_, k: (mix_t[:, part_, k, t * P:(t + 1) * P], w_k[:, :]), False, take)

        chunks = [((lambda slot, tiles, n=n: [(slot[:, :, :], w[:, tiles, n * BANK:(n + 1) * BANK])]),
                   [output(n, t) for t in range(NT)], slice(0, BANK)) for n in range(2)]
        product_phase(nc, name, chunks, BANK, [(b_rows[:], rows(bias_dram, P))] if bias_dram is not None else [])


def first_attention(nc, A, ident, feat, values, attn):
    with Scope(nc, "att1c") as s:
        mask = s.sb("mask", [P, 2 * P])
        sinks = s.sb("sinks", [P, NH])
        loaded = s.sem("loaded")
        with nc.Block() as block:
            @block.sync
            def _(sp):
                sp.dma_start(mask[:], A["window_mask"]).then_inc(loaded, 16)
                sp.dma_start(sinks[:], rows(A["attn_sinks"], P)).then_inc(loaded, 16)
                sp.wait_ge(loaded, 32)
        units = [(n, h) for n in range(NT) for h in range(NH)]

        def part(h):
            return slice(64 * (h % 2), 64 * (h % 2) + 64)

        attention_phase(
            nc, "att1", ident, units,
            q_of=lambda n, h: feat[part(h), h // 2, n * P:(n + 1) * P],
            k_of=lambda n, h: feat[part(h), 4 + h // 4, max(n - 1, 0) * P:(n + 1) * P],
            v_of=lambda n, h: [values[:, c, 64 * (h // 4):64 * (h // 4) + 64] for c in range(max(n - 1, 0), n + 1)],
            bias_of=lambda n, h: mask[:, P:2 * P] if n == 0 else mask[:],
            o_of=lambda n, h: attn[:, n, DH * h:DH * h + DH],
            keys_max=2 * P, sinks=lambda n, h: sinks[:, h:h + 1])



def query_projection(nc, A, h_t, query_t):
    w = weight_tiles(A["w_query"])

    def feature(col, f):
        return (P, T, lambda w_k, part, k: (w_k[:, col:col + P], h_t[:, part, k, :]), f % 2 == 0,
                copy_to(query_t[:, f, :]))

    chunks = [((lambda slot, tiles, n=n: [(slot[:, :, :], w[:, tiles, n * BANK:(n + 1) * BANK])]),
               [feature(P * j, 4 * n + j) for j in range(4)], slice(0, BANK)) for n in range(4)]
    product_phase(nc, "qp", chunks, BANK)


def peer_score_phase(nc, A, query_t, score):
    with Scope(nc, "score") as s:
        keys_t = s.sb("keys_t", [P, NC, NKEY])
        score_ps = s.ps("score_ps", [P, 8, 4, NKEY])
        loaded, scored, act_copied, dve_copied = (s.sem(x) for x in ("loaded", "scored", "act_copied", "dve_copied"))
        with nc.Block() as block:
            @block.sync
            def _(sp):
                for half in range(2):
                    sp.dma_start(keys_t[:, half::2, :], A[f"keys_t{half + 1}"]).then_inc(loaded, 16)

            @block.tensor
            def _(pe):
                pe.wait_ge(loaded, 32)
                for g in range(4 * NT):
                    t, b = g // 4, g % 4
                    if g >= 8:
                        pe.wait_ge(dve_copied if g % 2 else act_copied, (g - 8) // 2 + 1)
                    for j in range(4):
                        last = nc.tensor.matmul(score_ps[:, g % 8, j, :], query_t[:, 4 * b + j, t * P:(t + 1) * P],
                                                keys_t[:, 4 * b + j, :], start=True, stop=True)
                    last.then_inc(scored, 1)

            def copies(eng, copy, parity, copied):
                for g in range(parity, 4 * NT, 2):
                    eng.wait_ge(scored, g + 1)
                    copy(score[:, g // 4, 4 * (g % 4):4 * (g % 4) + 4, :], score_ps[:, g % 8, :, :]).then_inc(copied, 1)

            @block.scalar
            def _(act):
                copies(act, nc.scalar.copy, 0, act_copied)

            @block.vector
            def _(dve):
                copies(dve, nc.vector.tensor_copy, 1, dve_copied)


class ExpertDots:

    SLOTS = 2

    def __init__(self, nc, s, A, h_t, dots_dram):
        self.nc, self.A, self.h_t, self.dots_dram = nc, A, h_t, dots_dram
        n = self.SLOTS
        self.raw = s.sb("u_raw", [P, n, KD, P])
        self.split = s.sb("u_split", [P, n, 2, KD, P], F32R)
        self.gelu = s.sb("gelu", [P, n, T])
        self.banks = s.ps("dot_ps", [P, n, BANK])
        self.loaded = [s.sem(f"u_loaded{i}") for i in range(n)]
        self.stored = [s.sem(f"dots_stored{i}") for i in range(n)]
        self.hi_ready, self.lo_ready, self.dotted, self.gelu_ready = (s.sem(x) for x in (
            "u_hi_ready", "u_lo_ready", "dotted", "gelu_ready"))

    def credits(self, eng, name):
        if name == "scalar":
            eng.sem_inc(self.gelu_ready, self.SLOTS)
            for sem in self.stored:
                eng.sem_inc(sem, 16)
        if name == "gpsimd":
            eng.sem_inc(self.lo_ready, self.SLOTS)
        if name == "tensor":
            eng.sem_inc(self.dotted, self.SLOTS)

    def load(self, sp, tile, turn, j):
        sp.wait_ge(self.lo_ready, tile + 1)
        sp.dma_start(self.raw[:, j], self.A["u_tiles"][bass.ds(tile, 1)].rearrange(
            "a p k e -> p (a k) e")).then_inc(self.loaded[j], 16)

    def split_scalar(self, act, tile, turn, j):
        act.wait_ge(self.loaded[j], turn * 16 + 16)
        act.wait_ge(self.dotted, tile + 1)
        split_hi(self.nc.scalar, self.split[:, j, 0], self.raw[:, j]).then_inc(self.hi_ready, 1)

    def split_pool(self, pool, tile, turn, j):
        pool.wait_ge(self.hi_ready, tile + 1)
        split_lo(self.nc.gpsimd, self.split[:, j, 1], self.raw[:, j],
                 self.split[:, j, 0]).then_inc(self.lo_ready, 1)

    def dot(self, pe, tile, turn, j):
        pe.wait_ge(self.lo_ready, tile + 1 + self.SLOTS)
        pe.wait_ge(self.gelu_ready, tile + 1)
        for k in range(KD):
            for i, (u_part, h_part) in enumerate(((0, 0), (0, 1), (1, 0))):
                last = self.nc.tensor.matmul(self.banks[:, j, :], self.split[:, j, u_part, k], self.h_t[:, h_part, k],
                                             start=(k == 0 and i == 0), stop=(k == KD - 1 and i == 2))
        last.then_inc(self.dotted, 1)

    def activate(self, act, tile, turn, j):
        act.wait_ge(self.dotted, tile + 1 + self.SLOTS)
        act.wait_ge(self.stored[j], turn * 16 + 16)
        self.nc.scalar.activation(self.gelu[:, j], self.banks[:, j, :], ACT.Gelu).then_inc(self.gelu_ready, 1)
        act.wait_ge(self.gelu_ready, tile + 1 + self.SLOTS)
        act.dma_start(self.dots_dram[bass.ds(tile, 1)].rearrange("a e t -> e (a t)"),
                      self.gelu[:, j]).then_inc(self.stored[j], 16)


SPAN = 64
SPANS = T // SPAN
CHOICE_TURNS = 32


def peer_choice_phase(nc, A, dots, score, choice):
    with Scope(nc, "pick") as s:
        val = s.sb("val", [P, NC, PK])
        idx = s.sb("idx", [P, NC, PK], U32)
        idx_f = s.sb("idx_f", [P, NC, PK])
        cand = s.sb("cand", [P, PH, PK, PK])
        best = s.sb("best", [P, PH, PK])
        place = s.sb("place", [P, PH, PK], U32)
        place_part = s.sb("place_part", [P, PH, PK], U32)
        place_f = s.sb("place_f", [P, PH, PK])
        hot = s.sb("hot", [P, PH * PK, PK])
        iota16 = s.sb("iota16", [P, PK])
        shifted = s.sb("shifted", [P, NT, PH, PK])
        expd = s.sb("expd", [P, NT * PH, PK])
        total = s.sb("total", [P, NT * PH])
        total_inv = s.sb("total_inv", [P, NT * PH])
        iota_loaded, dve_step, shift_ready, exp_ready = (s.sem(x) for x in (
            "iota_loaded", "dve_step", "shift_ready", "exp_ready"))
        with nc.Block() as block:
            @block.sync
            def _(sp):
                sp.dma_start(iota16[:], rows(A["iota"][0:PK], P)).then_inc(iota_loaded, 16)
                with sp.Fori(0, CHOICE_TURNS) as i:
                    for j in range(2):
                        dots.load(sp, i * 2 + j, i, j)

            @block.gpsimd
            def _(pool):
                dots.credits(pool, "gpsimd")
                with pool.Fori(0, CHOICE_TURNS) as i:
                    for j in range(2):
                        dots.split_pool(pool, i * 2 + j, i, j)

            @block.tensor
            def _(pe):
                dots.credits(pe, "tensor")
                with pe.Fori(0, CHOICE_TURNS) as i:
                    for j in range(2):
                        dots.dot(pe, i * 2 + j, i, j)

            @block.scalar
            def _(act):
                dots.credits(act, "scalar")
                nc.scalar.preload_act_table(ACT.Gelu)
                dots.split_scalar(act, 0, 0, 0)
                dots.split_scalar(act, 1, 0, 1)
                dots.activate(act, 0, 0, 0)
                with act.Fori(1, CHOICE_TURNS) as i:
                    dots.split_scalar(act, i * 2, i, 0)
                    dots.activate(act, i * 2 - 1, i - 1, 1)
                    dots.split_scalar(act, i * 2 + 1, i, 1)
                    dots.activate(act, i * 2, i, 0)
                act.wait_ge(shift_ready, 1)
                nc.scalar.activation(expd[:], shifted[:].rearrange("p t h k -> p (t h) k"), ACT.Exp).then_inc(exp_ready, 1)

            @block.vector
            def _(dve):
                step = Steps(dve, dve_step)
                dve.wait_ge(iota_loaded, 16)

                def best16(v, i, data):
                    step(nc.vector.max(v[:, 0:8], data))
                    step(nc.vector.max_index(i[:, 0:8], v[:, 0:8], data))
                    step(nc.vector.match_replace(data, v[:, 0:8], data, LOWEST))
                    step(nc.vector.max(v[:, 8:16], data))
                    step(nc.vector.max_index(i[:, 8:16], v[:, 8:16], data))

                for t in range(NT):
                    for c in range(NC):
                        best16(val[:, c, :], idx[:, c, :], score[:, t, c, :])
                    step(nc.vector.tensor_copy(idx_f[:], idx[:]))
                    step(nc.vector.tensor_tensor(
                        cand[:], val[:, 0::2, :].unsqueeze(3).to_broadcast([P, PH, PK, PK]),
                        val[:, 1::2, :].unsqueeze(2).to_broadcast([P, PH, PK, PK]), ALU.add))
                    for h in range(PH):
                        best16(best[:, h, :], place[:, h, :], cand[:, h, :, :].rearrange("p i j -> p (i j)"))
                    for i, (op, by) in enumerate(((ALU.logical_shift_right, 4), (ALU.bitwise_and, 15))):
                        step(nc.vector.tensor_scalar(place_part[:], place[:], by, None, op))
                        step(nc.vector.tensor_copy(place_f[:], place_part[:]))
                        step(nc.vector.tensor_tensor(
                            hot[:], place_f[:].rearrange("p h k -> p (h k)").unsqueeze(2).to_broadcast([P, PH * PK, PK]),
                            iota16[:].unsqueeze(1).to_broadcast([P, PH * PK, PK]), ALU.is_equal))
                        hot4 = hot[:].rearrange("p (h k) i -> p h k i", h=PH)
                        step(nc.vector.tensor_tensor(
                            hot4, hot4, idx_f[:, i::2, :].unsqueeze(2).to_broadcast([P, PH, PK, PK]), ALU.mult))
                        step(nc.vector.tensor_reduce(choice[:, i, t, :], hot[:], AX.X, ALU.add))
                    last = nc.vector.tensor_tensor(shifted[:, t], best[:], best[:, :, 0:1].to_broadcast([P, PH, PK]),
                                                   ALU.subtract)
                    if t < NT - 1:
                        step(last)
                last.then_inc(shift_ready, 1)
                dve.wait_ge(exp_ready, 1)
                step(nc.vector.tensor_reduce(total[:], expd[:], AX.X, ALU.add))
                step(nc.vector.reciprocal(total_inv[:], total[:]))
                nc.vector.tensor_tensor(
                    choice[:, 2].rearrange("p t (h k) -> p (t h) k", h=PH), expd[:],
                    total_inv[:].unsqueeze(2).to_broadcast([P, NT * PH, PK]), ALU.mult)


def peer_weight_phase(nc, A, ident, dots, choice, weight_dram):
    SET = 8
    TURNS = SPAN // (2 * SET)
    PART = NKEY // (2 * TURNS)
    assert CHOICE_TURNS + SPANS * TURNS == ETILES // 2
    with Scope(nc, "wt") as s:
        choice_t = s.sb("choice_t", [P, 3, T])
        iota = s.sb("iota", [P, NKEY])
        iota_loaded, turned = s.sem("iota_loaded"), s.sem("turned")
        with ExitStack() as inner:
            turn_ps = inner.enter_context(nc.psum_tensor("wt_turn_ps", [P, 3, NT, P], F32))
            with nc.Block() as block:
                @block.sync
                def _(sp):
                    sp.dma_start(iota[:], rows(A["iota"], P)).then_inc(iota_loaded, 16)
                    sp.wait_ge(iota_loaded, 16)

                @block.tensor
                def _(pe):
                    for i in range(3):
                        for t in range(NT):
                            last = nc.tensor.transpose(turn_ps[:, i, t, :], choice[:, i, t, :], ident[:])
                        last.then_inc(turned, 1)

                @block.vector
                def _(dve):
                    for i in range(3):
                        dve.wait_ge(turned, i + 1)
                        nc.vector.tensor_copy(choice_t[:, i, :], turn_ps[:, i, :, :].rearrange("p t q -> p (t q)"))

        now = s.sb("now", [P, 2, SET])
        hot1 = s.sb("hot1", [P, SET, NKEY])
        hot2 = s.sb("hot2", [P, SET, NKEY])
        stage = s.sb("stage", [P, 2, NKEY, SPAN])
        banks = s.ps("banks", [P, 2, 4, NKEY])
        now_ready, hot_ready, product_done, staged = (s.sem(x) for x in (
            "now_ready", "hot_ready", "product_done", "staged"))
        stored = [s.sem(f"stored{b}") for b in range(2)]

        def turns(eng, body):
            with eng.Fori(0, SPANS // 2) as pair:
                for b in range(2):
                    with eng.Fori(0, TURNS) as i:
                        body(pair * (2 * TURNS) + i + b * TURNS, pair * (2 * SPAN) + i * (2 * SET) + b * SPAN,
                             i * (2 * SET), b, pair)

        with nc.Block() as block:
            @block.vector
            def _(dve):
                def build(turn, token, at, b, pair):
                    dve.wait_ge(stored[b], pair * (32 * TURNS) + 32 * TURNS)
                    for j in range(2):
                        n = turn * 2 + j
                        nc.vector.tensor_copy(now[:, 0, :], choice_t[:, 0, bass.ds(token + j * SET, SET)]).then_inc(now_ready, 1)
                        nc.vector.tensor_copy(now[:, 1, :], choice_t[:, 2, bass.ds(token + j * SET, SET)]).then_inc(now_ready, 1)
                        nc.vector.tensor_tensor(
                            hot2[:], iota[:].unsqueeze(1).to_broadcast([P, SET, NKEY]),
                            choice_t[:, 1, bass.ds(token + j * SET, SET)].unsqueeze(2).to_broadcast([P, SET, NKEY]),
                            ALU.is_equal).then_inc(hot_ready, 1)
                        dve.wait_ge(now_ready, n * 2 + 2)
                        for q in range(SET):
                            last = nc.vector.tensor_scalar(hot1[:, q, :], iota[:], now[:, 0, q:q + 1],
                                                           now[:, 1, q:q + 1], ALU.is_equal, ALU.mult)
                        last.then_inc(hot_ready, 1)
                        for q in range(2):
                            dve.wait_ge(product_done, n * 2 + (q + 1))
                            nc.vector.tensor_copy(stage[:, b, :, bass.ds(at + (j * SET + 4 * q), 4)],
                                                  banks[:, q].rearrange("p t e -> p e t")).then_inc(staged, 1)

                turns(dve, build)

            @block.gpsimd
            def _(pool):
                with pool.Fori(CHOICE_TURNS, ETILES // 2) as i:
                    for j in range(2):
                        dots.split_pool(pool, i * 2 + j, i, j)

            @block.tensor
            def _(pe):
                def body(turn, token, at, b, pair):
                    for j in range(2):
                        dots.dot(pe, turn * 2 + (2 * CHOICE_TURNS + j), turn + CHOICE_TURNS, j)
                        n = turn * 2 + j
                        pe.wait_ge(hot_ready, n * 2 + 2)
                        for q in range(SET):
                            last = nc.tensor.matmul(banks[:, q // 4, q % 4, :], hot2[:, q, :], hot1[:, q, :],
                                                    start=True, stop=True)
                            if q % 4 == 3:
                                last.then_inc(product_done, 1)

                turns(pe, body)

            @block.scalar
            def _(act):
                nc.scalar.preload_act_table(ACT.Gelu)
                with act.Fori(CHOICE_TURNS, ETILES // 2) as i:
                    dots.split_scalar(act, i * 2, i, 0)
                    dots.activate(act, i * 2 - 1, i - 1, 1)
                    dots.split_scalar(act, i * 2 + 1, i, 1)
                    dots.activate(act, i * 2, i, 0)
                dots.activate(act, ETILES - 1, ETILES // 2 - 1, 1)

            @block.sync
            def _(sp):
                for b in range(2):
                    sp.sem_inc(stored[b], 16 * 2 * TURNS)

                def store_part(span, part):
                    sp.dma_start(weight_dram[span, :, bass.ds(part * PART, PART), :],
                                 stage[:, span % 2, bass.ds(part * PART, PART), :]).then_inc(stored[span % 2], 16)

                for span in range(SPANS):
                    first = CHOICE_TURNS + span * TURNS
                    for j in range(2):
                        dots.load(sp, 2 * first + j, first, j)
                    if span >= 1:
                        sp.wait_ge(staged, span * TURNS * 4)
                        for j in range(2):
                            store_part(span - 1, j)
                    with sp.Fori(1, TURNS) as i:
                        for j in range(2):
                            dots.load(sp, i * 2 + (2 * first + j), i + first, j)
                        if span >= 1:
                            for j in range(2):
                                store_part(span - 1, i * 2 + j)
                sp.wait_ge(staged, SPANS * TURNS * 4)
                for part in range(2 * TURNS):
                    store_part(SPANS - 1, part)
                for b in range(2):
                    sp.wait_ge(stored[b], 16 * 2 * TURNS * (1 + SPANS // 2))
                    sp.wait_ge(dots.stored[b], 16 + 16 * ETILES // 2)


def peer_value_phase(nc, A, dots_dram, weight_dram, x, gate):
    with Scope(nc, "val") as s:
        v_raw = s.sb("v_raw", [P, 2, 2, D])
        v = s.sb("v", [P, 2, 2, 2, D], F32R)
        dot = s.sb("dot", [P, 2, 2, T])
        weight = s.sb("weight", [P, 2, SPANS, 2, SPAN])
        coef = s.sb("coef", [P, 2, 2, T])
        coef_split = s.sb("coef_split", [P, 2, 2, 2, T], F32R)
        part = s.sb("part", [P, 2, BANK])
        banks = s.ps("banks", [P, 8, BANK])
        v_loaded = [s.sem(f"v_loaded{i}") for i in range(2)]
        c_loaded = [s.sem(f"c_loaded{i}") for i in range(2)]
        v_hi, v_lo, coef_ready, coef_hi, coef_lo, summed, dve_step = (s.sem(x_) for x_ in (
            "v_hi", "v_lo", "coef_ready", "coef_hi", "coef_lo", "summed", "dve_step"))
        n_turns = ETILES // 2

        def turns(eng, body):
            with eng.Fori(0, n_turns // 2) as i:
                for b in range(2):
                    body(i * 2 + b, b, i)

        with nc.Block() as block:
            @block.sync
            def _(sp):
                def load(turn, b, i):
                    sp.wait_ge(v_lo, turn + 1)
                    sp.dma_start(v_raw[:, b], A["peer_v"][bass.ds(turn * (2 * P), 2 * P), :].rearrange(
                        "(a e) d -> e a d", e=P)).then_inc(v_loaded[b], 16)
                    sp.wait_ge(coef_ready, turn * 2 + 2)
                    sp.dma_start(dot[:, b], dots_dram[bass.ds(turn * 2, 2)].rearrange(
                        "a e t -> e a t")).then_inc(c_loaded[b], 16)
                    sp.dma_start(weight[:, b].rearrange("p s a t -> p s (a t)"),
                                 weight_dram[:, :, bass.ds(turn * 2, 2), :].rearrange(
                                     "s b a t -> b s (a t)")).then_inc(c_loaded[b], 16)

                turns(sp, load)

            @block.scalar
            def _(act):
                def split(turn, b, i):
                    act.wait_ge(v_loaded[b], i * 16 + 16)
                    act.wait_ge(summed, turn + 1)
                    split_hi(nc.scalar, v[:, b, 0], v_raw[:, b]).then_inc(v_hi, 1)
                    act.wait_ge(coef_ready, turn * 2 + 6)
                    split_hi(nc.scalar, coef_split[:, b, 0], coef[:, b]).then_inc(coef_hi, 1)

                turns(act, split)

            @block.gpsimd
            def _(pool):
                def split(turn, b, i):
                    pool.wait_ge(v_hi, turn + 1)
                    split_lo(nc.gpsimd, v[:, b, 1], v_raw[:, b], v[:, b, 0]).then_inc(v_lo, 1)

                pool.sem_inc(v_lo, 2)
                turns(pool, split)

            @block.vector
            def _(dve):
                def coefficients(turn, b, i):
                    dve.wait_ge(c_loaded[b], i * 32 + 32)
                    dve.wait_ge(coef_lo, turn + 1)
                    for a in range(2):
                        nc.vector.tensor_tensor(
                            coef[:, b, a].rearrange("p (s t) -> p s t", s=SPANS),
                            dot[:, b, a].rearrange("p (s t) -> p s t", s=SPANS),
                            weight[:, b, :, a, :], ALU.mult).then_inc(coef_ready, 1)
                    dve.wait_ge(coef_hi, turn + 1)
                    split_lo(nc.vector, coef_split[:, b, 1], coef[:, b], coef_split[:, b, 0]).then_inc(coef_lo, 1)

                dve.sem_inc(coef_ready, 4)
                dve.sem_inc(coef_lo, 2)
                turns(dve, coefficients)
                step = Steps(dve, dve_step)
                dve.wait_ge(summed, 2 + n_turns)
                for o in range(8):
                    t, half = o // 2, o % 2
                    cols = slice(half * BANK, (half + 1) * BANK)
                    step(nc.vector.tensor_tensor(part[:, o % 2, :], banks[:, o, :], gate[:, cols], ALU.mult))
                    nc.vector.tensor_tensor(x[:, t, cols], part[:, o % 2, :], x[:, t, cols], ALU.add)

            @block.tensor
            def _(pe):
                def multiply(turn, b, first=False, final=False):
                    pe.wait_ge(v_lo, turn + 3)
                    pe.wait_ge(coef_lo, turn + 3)
                    for a in range(2):
                        for t in range(NT):
                            for c_part, v_part in ((0, 0), (0, 1), (1, 0)):
                                for half in range(2):
                                    last = nc.tensor.matmul(
                                        banks[:, 2 * t + half, :], coef_split[:, b, c_part, a, t * P:(t + 1) * P],
                                        v[:, b, v_part, a, half * BANK:(half + 1) * BANK],
                                        start=(first and a == 0 and c_part == 0 and v_part == 0),
                                        stop=(final and a == 1 and c_part == 1), skip_group_check=True)
                    last.then_inc(summed, 1)

                pe.sem_inc(summed, 2)
                multiply(0, 0, first=True)
                multiply(1, 1)
                with pe.Fori(1, n_turns // 2 - 1) as i:
                    for b in range(2):
                        multiply(i * 2 + b, b)
                multiply(n_turns - 2, 0)
                multiply(n_turns - 1, 1, final=True)



HY, NA, PW = 256, 512, 256
FH = 64
FE = 33
TWO_PI = 2.0 * np.pi
ROUND = 1.5 * 2.0 ** 23
PI_1 = 6.28125
PI_2 = float((np.array([TWO_PI - PI_1], np.float32).view(np.uint32) & np.uint32(0xFFFFF000)).view(np.float32)[0])
PI_3 = float(np.float32(TWO_PI - PI_1 - PI_2))
PI_LOW = 3.1415925


def second_projection(nc, A, h_t, feat, values):
    w = weight_tiles(A["w_in_2"][0])

    def feature(col, f):
        return (P, T, lambda w_k, part, k: (w_k[:, col:col + P], h_t[:, part, k, :]), f % 2 == 0,
                copy_to(feat[:, f, :]))

    def token(t):
        return (P, NA, lambda w_k, part, k: (h_t[:, part, k, t * P:(t + 1) * P], w_k[:, :]), t % 2 == 0,
                copy_to(values[:, t, :]))

    def cols(at, width):
        return lambda slot, tiles: [(slot[:, :, 0:width], w[:, tiles, at:at + width])]

    chunks, at, f = [], 0, 0
    for width in (512, 256, 512, 512):
        chunks.append((cols(at, width), [feature(P * j, f + j) for j in range(width // P)], slice(0, width)))
        at, f = at + width, f + width // P
    chunks.append((cols(at, NA), [token(t) for t in range(NT)], slice(0, NA)))
    chunks.append((cols(at + NA, PW), [feature(P * j, f + j) for j in range(PW // P)], slice(0, PW)))
    product_phase(nc, "in2", chunks, BANK)


def filter_phase(nc, A, even, odd):
    with Scope(nc, "filt") as s:
        pos_t = s.sb("pos_t", [FE, T])
        w1 = s.sb("w1", [FE, FH])
        w2 = s.sb("w2", [FH, FH])
        w_out = s.sb("w_out", [FH, 2 * HY])
        cols = s.sb("cols", [FH, 3])
        decay = s.sb("decay", [P, NT, 2 * HY])
        arg = s.sb("arg", [FH, T])
        turns = s.sb("turns", [FH, T])
        hid = s.sb("hid", [FH, 2, T])
        taps = s.sb("taps", [P, NT, 2 * HY])
        hid_ps = s.ps("hid_ps", [FH, 2, BANK])
        tap_ps = s.ps("tap_ps", [P, NT, BANK])
        loaded, hid_done, arg_ready, sine_ready, taps_done, dve_step = (s.sem(x) for x in (
            "loaded", "hid_done", "arg_ready", "sine_ready", "taps_done", "dve_step"))
        with nc.Block() as block:
            @block.sync
            def _(sp):
                for to, src in ((pos_t[:], A["pos_t"]), (w1[:], A["hy_f_w1_2"][0]), (w2[:], A["hy_f_w2_2"][0]),
                                (w_out[:], A["hy_f_wout_2"][0]),
                                (cols[:, 0:1], A["hy_f_b1_2"].rearrange("a n -> n a")),
                                (cols[:, 1:2], A["hy_f_b2_2"].rearrange("a n -> n a")),
                                (cols[:, 2:3], A["hy_f_freq_2"].rearrange("a n -> n a")),
                                (decay[:], A["decay"].rearrange("(t p) c -> p t c", p=P))):
                    sp.dma_start(to, src).then_inc(loaded, 16)

            @block.tensor
            def _(pe):
                pe.wait_ge(loaded, 16 * 8)
                nc.tensor.matmul(hid_ps[:, 0, :], w1[:], pos_t[:], start=True, stop=True).then_inc(hid_done, 1)
                pe.wait_ge(sine_ready, 1)
                nc.tensor.matmul(hid_ps[:, 1, :], w2[:], hid[:, 0, :], start=True, stop=True).then_inc(hid_done, 1)
                pe.wait_ge(sine_ready, 2)
                for t in range(NT):
                    nc.tensor.matmul(tap_ps[:, t, :], hid[:, 1, t * P:(t + 1) * P], w_out[:],
                                     start=True, stop=True).then_inc(taps_done, 1)

            @block.scalar
            def _(act):
                for i in range(2):
                    act.wait_ge(arg_ready, i + 1)
                    nc.scalar.activation(hid[:, i, :], arg[:], ACT.Sin).then_inc(sine_ready, 1)

            @block.vector
            def _(dve):
                step = Steps(dve, dve_step)
                dve.wait_ge(loaded, 16 * 8)
                for i in range(2):
                    dve.wait_ge(hid_done, i + 1)
                    step(nc.vector.tensor_scalar(arg[:], hid_ps[:, i, :], cols[:, i:i + 1], cols[:, 2:3],
                                                 ALU.add, ALU.mult))
                    step(nc.vector.tensor_scalar(turns[:], arg[:], 1.0 / TWO_PI, ROUND, ALU.mult, ALU.add))
                    step(nc.vector.tensor_scalar(turns[:], turns[:], ROUND, None, ALU.subtract))
                    for part in (PI_1, PI_2, PI_3):
                        step(nc.vector.scalar_tensor_tensor(out=arg[:], in0=turns[:], scalar=-part, in1=arg[:],
                                                            op0=ALU.mult, op1=ALU.add))
                    nc.vector.tensor_scalar(arg[:], arg[:], PI_LOW, -PI_LOW, ALU.min, ALU.max).then_inc(arg_ready, 1)
                    dve.wait_ge(sine_ready, i + 1)
                for t in range(NT):
                    dve.wait_ge(taps_done, t + 1)
                    step(nc.vector.tensor_tensor(taps[:, t, :], tap_ps[:, t, :], decay[:, t, :], ALU.mult))
                nc.vector.tensor_tensor(even[:], taps[:, :, 0:HY], taps[:, :, HY:], ALU.add)
                nc.vector.tensor_tensor(odd[:], taps[:, :, 0:HY], taps[:, :, HY:], ALU.subtract)


def hyena_phase(nc, A, ident, feat, even, odd, hy_y):
    with Scope(nc, "hyen") as s:
        short = s.sb("short", [P, 6, T])
        taps = s.sb("taps", [P, 6, 3])
        short_bias = s.sb("short_bias", [P, 6])
        skip = s.sb("skip", [P, 2])
        z = s.sb("z", [P, 2, T])
        with_cos = s.sb("with_cos", [P, NT, 2 * HY])
        with_sin = s.sb("with_sin", [P, NT, 2 * HY])
        cos = s.sb("cos", [P, NT, T])
        sin = s.sb("sin", [P, NT, T])
        cos_t = s.sb("cos_t", [P, NT, T])
        sin_t = s.sb("sin_t", [P, NT, T])
        spec_cos = s.sb("spec_cos", [P, NT, 2 * HY])
        spec_sin = s.sb("spec_sin", [P, NT, 2 * HY])
        out_cos = s.sb("out_cos", [P, NT, HY])
        out_sin = s.sb("out_sin", [P, NT, HY])
        part = s.sb("part", [P, NT, HY])
        banks = s.ps("banks", [P, 8, BANK])
        taps_loaded, dft_loaded, z_ready, turned, input_ready, spec_done, spec_taken, out_ready, y_done, dve_step = (
            s.sem(x) for x in ("taps_loaded", "dft_loaded", "z_ready", "turned", "input_ready", "spec_done",
                               "spec_taken", "out_ready", "y_done", "dve_step"))
        with nc.Block() as block:
            @block.sync
            def _(sp):
                sp.dma_start(taps[:], A["hy_short_w_col"]).then_inc(taps_loaded, 16)
                sp.dma_start(short_bias[:], A["hy_short_b_col"]).then_inc(taps_loaded, 16)
                sp.dma_start(skip[:], A["hy_skip_col"]).then_inc(taps_loaded, 16)
                for to, name in ((cos, "dft_cos"), (sin, "dft_sin"), (cos_t, "dft_cos_t"), (sin_t, "dft_sin_t")):
                    sp.dma_start(to[:], A[name].rearrange("(t p) f -> p t f", p=P)).then_inc(dft_loaded, 16)

            @block.tensor
            def _(pe):
                pe.wait_ge(z_ready, 1)
                for c in range(2):
                    for t in range(NT):
                        last = nc.tensor.transpose(banks[:, c, t * P:(t + 1) * P], z[:, c, t * P:(t + 1) * P], ident[:])
                    last.then_inc(turned, 1)
                pe.wait_ge(dft_loaded, 64)
                pe.wait_ge(input_ready, 3)
                for f in range(NT):
                    for i, (table, data) in enumerate(((cos, with_cos), (sin, with_sin))):
                        for t in range(NT):
                            last = nc.tensor.matmul(banks[:, 2 * f + i, :], table[:, t, f * P:(f + 1) * P],
                                                    data[:, t, :], start=(t == 0), stop=(t == NT - 1))
                        last.then_inc(spec_done, 1)
                pe.wait_ge(out_ready, 1)
                for c in range(2):
                    for i, (table, data) in enumerate(((cos_t, out_cos), (sin_t, out_sin))):
                        for f in range(NT):
                            last = nc.tensor.matmul(banks[:, c, :], data[:, f, c * P:(c + 1) * P], table[:, f, :],
                                                    start=(i == 0 and f == 0), stop=(i == 1 and f == NT - 1))
                    last.then_inc(y_done, 1)

            @block.scalar
            def _(act):
                nc.scalar.copy(with_cos[:, :, HY:], even[:]).then_inc(input_ready, 1)
                nc.scalar.copy(with_sin[:, :, HY:], odd[:]).then_inc(input_ready, 1)
                for g in range(8):
                    act.wait_ge(spec_done, g + 1)
                    dst = (spec_cos, spec_sin)[g % 2]
                    nc.scalar.copy(dst[:, g // 2, :], banks[:, g, :]).then_inc(spec_taken, 1)

            @block.vector
            def _(dve):
                step = Steps(dve, dve_step)
                dve.wait_ge(taps_loaded, 48)
                for f in range(6):
                    step(nc.vector.tensor_scalar(short[:, f, :], feat[:, f, :], taps[:, f, 1:2], short_bias[:, f:f + 1],
                                                 ALU.mult, ALU.add))
                    step(nc.vector.scalar_tensor_tensor(out=short[:, f, 1:T], in0=feat[:, f, 0:T - 1],
                                                        scalar=taps[:, f, 0:1], in1=short[:, f, 1:T],
                                                        op0=ALU.mult, op1=ALU.add))
                    step(nc.vector.scalar_tensor_tensor(out=short[:, f, 0:T - 1], in0=feat[:, f, 1:T],
                                                        scalar=taps[:, f, 2:3], in1=short[:, f, 0:T - 1],
                                                        op0=ALU.mult, op1=ALU.add))
                nc.vector.tensor_tensor(z[:], short[:, 4:6, :], short[:, 2:4, :], ALU.mult).then_inc(z_ready, 1)
                dve.wait_ge(turned, 2)
                for to in (with_cos, with_sin):
                    for c in range(2):
                        last = nc.vector.tensor_copy(to[:, :, c * P:(c + 1) * P],
                                                     banks[:, c, :].rearrange("p (t q) -> p t q", q=P))
                        if c == 0 or to is with_cos:
                            step(last)
                last.then_inc(input_ready, 1)
                dve.wait_ge(z_ready, 1)
                for c in range(2):
                    step(nc.vector.tensor_scalar(z[:, c, :], z[:, c, :], skip[:, c:c + 1], None, ALU.mult))
                dve.wait_ge(spec_taken, 8)
                zc, ec = spec_cos[:, :, 0:HY], spec_cos[:, :, HY:]
                zs, es = spec_sin[:, :, 0:HY], spec_sin[:, :, HY:]
                step(nc.vector.tensor_tensor(out_cos[:], zc, ec, ALU.mult))
                step(nc.vector.tensor_tensor(part[:], zs, es, ALU.mult))
                step(nc.vector.tensor_tensor(out_cos[:], out_cos[:], part[:], ALU.subtract))
                step(nc.vector.tensor_tensor(out_sin[:], zc, es, ALU.mult))
                step(nc.vector.tensor_tensor(part[:], zs, ec, ALU.mult))
                nc.vector.tensor_tensor(out_sin[:], out_sin[:], part[:], ALU.add).then_inc(out_ready, 1)
                for c in range(2):
                    dve.wait_ge(y_done, c + 1)
                    step(nc.vector.scalar_tensor_tensor(out=hy_y[:, c, :], in0=banks[:, c, :], scalar=2.0 / (2 * T),
                                                        in1=z[:, c, :], op0=ALU.mult, op1=ALU.add))
                    nc.vector.tensor_tensor(hy_y[:, c, :], hy_y[:, c, :], short[:, c, :], ALU.mult)


def pool_phase(nc, A, feat, pool_y):
    PAD = 8
    W = T + 2 * PAD
    with Scope(nc, "pool") as s:
        sums = s.sb("sums", [P, 5, 2, W])
        inv = s.sb("inv", [P, 2, T])
        mat = s.sb("mat", [P, 2, P])
        scale = s.sb("scale", [P, 2])
        pooled = s.sb("pooled", [P, 2, T])
        banks = s.ps("banks", [P, 2, BANK])
        zeroed, loaded, pooled_ready, product_done, dve_step = (s.sem(x) for x in (
            "zeroed", "loaded", "pooled_ready", "product_done", "dve_step"))
        with nc.Block() as block:
            @block.sync
            def _(sp):
                for g in range(4):
                    half = slice(64 * (g % 2), 64 * (g % 2) + 64)
                    sp.dma_start(inv[half, g // 2, :], rows(A["pool_inv"][g], 64)).then_inc(loaded, 16)
                sp.dma_start(scale[:], A["pool_scale_col"]).then_inc(loaded, 16)
                sp.wait_ge(zeroed, 1)
                for g in range(4):
                    half = slice(64 * (g % 2), 64 * (g % 2) + 64)
                    sp.dma_start(mat[half, g // 2, half], A["pool_w_2"][0, g]).then_inc(loaded, 16)

            @block.vector
            def _(dve):
                step = Steps(dve, dve_step)
                nc.vector.memset(mat[:], 0.0).then_inc(zeroed, 1)
                step(nc.vector.memset(sums[:], 0.0))
                step(nc.vector.tensor_copy(sums[:, 0, :, PAD:PAD + T], feat[:, 14:16, :]))
                step(nc.vector.tensor_tensor(sums[:, 1, :, 1:W - 1], sums[:, 0, :, 0:W - 2], sums[:, 0, :, 1:W - 1], ALU.add))
                for i, (lo, by) in enumerate(((2, 1), (4, 2), (8, 4))):
                    step(nc.vector.tensor_tensor(sums[:, i + 2, :, lo:W - lo], sums[:, i + 1, :, lo - by:W - lo - by],
                                                 sums[:, i + 1, :, lo + by:W - lo + by], ALU.add))
                dve.wait_ge(loaded, 16 * 9)
                for g in range(4):
                    half = slice(64 * (g % 2), 64 * (g % 2) + 64)
                    step(nc.vector.tensor_tensor(pooled[half, g // 2, :], sums[half, g + 1, g // 2, PAD:PAD + T],
                                                 inv[half, g // 2, :], ALU.mult))
                nc.vector.tensor_tensor(pooled[:], pooled[:], feat[:, 14:16, :], ALU.subtract).then_inc(pooled_ready, 1)
                for c in range(2):
                    dve.wait_ge(product_done, c + 1)
                    nc.vector.tensor_scalar(pool_y[:, c, :], banks[:, c, :], scale[:, c:c + 1], None, ALU.mult)

            @block.tensor
            def _(pe):
                pe.wait_ge(loaded, 16 * 9)
                pe.wait_ge(pooled_ready, 1)
                for c in range(2):
                    nc.tensor.matmul(banks[:, c, :], mat[:, c, :], pooled[:, c, :],
                                     start=True, stop=True).then_inc(product_done, 1)


def bias_table_phase(nc, A, table):
    DR, DC, GW = 15, 31, 64
    with Scope(nc, "bias") as s:
        pick = s.sb("pick", [DC + 1, GW, P])
        bias = s.sb("bias", [DC + 1, NH * DR])
        banks = s.ps("banks", [P, 4, BANK])
        one, loaded, product_done, act_taken, dve_taken = (s.sem(x) for x in (
            "one", "loaded", "product_done", "act_taken", "dve_taken"))
        n = GW // 4
        with nc.Block() as block:
            @block.sync
            def _(sp):
                sp.dma_start(pick[:], A["bias_pick"]).then_inc(loaded, 16)
                sp.wait_ge(one, 1)
                sp.dma_start(bias[0:DC, :], A["rpb_t"]).then_inc(loaded, 16)

            @block.tensor
            def _(pe):
                pe.wait_ge(loaded, 32)
                for g in range(n):
                    if g >= 4:
                        pe.wait_ge(act_taken, g - 3)
                        pe.wait_ge(dve_taken, g - 3)
                    for j in range(4):
                        last = nc.tensor.matmul(banks[:, g % 4, j * NH * DR:(j + 1) * NH * DR],
                                                pick[:, 4 * g + j, :], bias[:], start=True, stop=True)
                    last.then_inc(product_done, 1)

            def move(copy, half, row, g):
                src = banks[half, g % 4, 0:4 * NH * DR].rearrange("p (j h r) -> p h r j", j=4, h=NH)
                dst = table[half, :, :].rearrange("p h (r j) -> p h r j", j=GW)
                return copy(dst[:, :, row:row + DR, 4 * g:4 * g + 4], src)

            @block.scalar
            def _(act):
                for g in range(n):
                    act.wait_ge(product_done, g + 1)
                    move(nc.scalar.copy, slice(0, 64), 0, g).then_inc(act_taken, 1)

            @block.vector
            def _(dve):
                nc.vector.memset(bias[:], 1.0).then_inc(one, 1)
                for g in range(n):
                    dve.wait_ge(product_done, g + 1)
                    move(nc.vector.tensor_copy, slice(64, 128), 1, g).then_inc(dve_taken, 1)


def second_attention(nc, A, ident, feat, values, table, attn):
    units = [(t, h) for t in range(NT) for h in range(NH)]

    def part(h):
        return slice(64 * (h % 2), 64 * (h % 2) + 64)

    attention_phase(
        nc, "att2", ident, units,
        q_of=lambda t, h: feat[part(h), 6 + h // 2, t * P:(t + 1) * P],
        k_of=lambda t, h: feat[part(h), 10 + h // 2, :],
        v_of=lambda t, h: [values[:, c, DH * h:DH * h + DH] for c in range(NT)],
        bias_of=lambda t, h: table[:, h, (7 - 2 * t) * 64:(7 - 2 * t) * 64 + T],
        o_of=lambda t, h: attn[:, t, DH * h:DH * h + DH], keys_max=T)



class ExpertPieces:
    RAW = 6
    NCH = FF // BANK
    HK = KD // 2
    UP_PIECES = 4 * NCH
    DK = 2
    PIECES = UP_PIECES + FF // P // DK

    def __init__(self, nc, s, A):
        self.A = A
        self.raw = s.sb("raw_pieces", [P, self.RAW, self.HK * BANK])
        self.loaded = [s.sem(f"piece_loaded{i}") for i in range(self.RAW)]

    def load(self, sp, i, e, c):
        if c < self.UP_PIECES:
            n, m, half = c // 4, ("gate", "up")[c % 4 // 2], c % 2
            src = self.A[f"w_{m}_2"][0, bass.ds(i * 2 + e, 1)].rearrange("a (k p) n -> p (a k) n", p=P)
            src = src[:, half * self.HK:(half + 1) * self.HK, n * BANK:(n + 1) * BANK]
        else:
            at = (c - self.UP_PIECES) * self.DK * P
            src = self.A["w_down_2"][0, bass.ds(i * 2 + e, 1), at:at + self.DK * P, :].rearrange(
                "a (k p) n -> p (a k) n", p=P)
        sp.dma_start(self.raw[:, c % self.RAW].rearrange("p (k n) -> p k n", n=src.shape[2]),
                     src).then_inc(self.loaded[c % self.RAW], 16)


def router_phase(nc, A, ident, h_t, h_dram, gate_dram, token_dram, xs_t, token_f, gate, pieces):
    with Scope(nc, "rout") as s:
        w = s.sb("w", [P, KD, NE])
        w_split = s.sb("w_split", [P, 2, KD, NE], F32R)
        top = s.sb("top", [P, NT])
        logit = s.sb("logit", [P, NT, NE])
        expd = s.sb("expd", [P, NT, NE])
        total = s.sb("total", [P, NT])
        total_inv = s.sb("total_inv", [P, NT])
        aff = s.sb("aff", [P, NT, NE])
        aff_t = s.sb("aff_t", [NE, T])
        val = s.sb("val", [NE, CAP])
        idx = s.sb("idx", [NE, CAP], U32)
        idx_f = s.sb("idx_f", [NE, CAP])
        token_u = s.sb("token_u", [P, NPAIR], U32)
        xs = s.sb("xs", [P, NPAIR, D])
        logit_ps = s.ps("logit_ps", [P, NT, NE])
        aff_ps = s.ps("aff_ps", [NE, T])
        turn_ps = s.ps("turn_ps", [P, 4, 4, P])
        (w_loaded, logits_done, shift_ready, exp_ready, aff_ready, turned, best_ready, listed, relisted,
         token_ready, xs_turned, xs_taken, dve_step, w_hi, w_lo) = (s.sem(x) for x in (
             "w_loaded", "logits_done", "shift_ready", "exp_ready", "aff_ready", "turned", "best_ready", "listed",
             "relisted", "token_ready", "xs_turned", "xs_taken", "dve_step", "w_hi", "w_lo"))
        gathered = [s.sem(f"gathered{i}") for i in range(NPAIR)]
        with nc.Block() as block:
            @block.sync
            def _(sp):
                sp.dma_start(w[:], weight_tiles(A["w_router_2"][0])).then_inc(w_loaded, 16)
                for c in range(pieces.RAW):
                    pieces.load(sp, 0, 0, c)
                sp.wait_ge(best_ready, 1)
                sp.dma_start(gate_dram, val[:]).then_inc(listed, 16)
                sp.dma_start(token_dram, idx_f[:]).then_inc(listed, 16)
                sp.wait_ge(listed, 32)
                sp.dma_start(gate[:], gate_dram.rearrange("(i e) s -> (e s) i", e=2),
                             allow_slow_non_contiguous=True).then_inc(relisted, 16)
                sp.dma_start(token_f[:], token_dram.rearrange("(i e) s -> (e s) i", e=2),
                             allow_slow_non_contiguous=True).then_inc(relisted, 16)
                sp.wait_ge(relisted, 32)

            @block.tensor
            def _(pe):
                pe.wait_ge(w_lo, 1)
                for t in range(NT):
                    for k in range(KD):
                        for i, (h_part, w_part) in enumerate(((0, 0), (0, 1), (1, 0))):
                            last = nc.tensor.matmul(logit_ps[:, t, :], h_t[:, h_part, k, t * P:(t + 1) * P],
                                                    w_split[:, w_part, k, :], start=(k == 0 and i == 0),
                                                    stop=(k == KD - 1 and i == 2))
                last.then_inc(logits_done, 1)
                pe.wait_ge(aff_ready, 1)
                for t in range(NT):
                    last = nc.tensor.transpose(aff_ps[:, t * P:(t + 1) * P], aff[:, t, :], ident[:])
                last.then_inc(turned, 1)
                for g in range(2 * NPAIR):
                    i, half = g // 2, g % 2
                    pe.wait_ge(gathered[i], 16)
                    if g >= 4:
                        pe.wait_ge(xs_taken, g - 3)
                    for j in range(4):
                        c = 4 * half + j
                        last = nc.tensor.transpose(turn_ps[:, g % 4, j, :], xs[:, i, c * P:(c + 1) * P], ident[:])
                    last.then_inc(xs_turned, 1)

            @block.scalar
            def _(act):
                act.wait_ge(w_loaded, 16)
                split_hi(nc.scalar, w_split[:, 0], w[:]).then_inc(w_hi, 1)
                act.wait_ge(shift_ready, 1)
                nc.scalar.activation(expd[:], logit[:], ACT.Exp).then_inc(exp_ready, 1)
                for g in range(2 * NPAIR):
                    act.wait_ge(xs_turned, g + 1)
                    nc.scalar.copy(xs_t[:, g // 2, 4 * (g % 2):4 * (g % 2) + 4, :],
                                   turn_ps[:, g % 4, :, :]).then_inc(xs_taken, 1)

            @block.gpsimd
            def _(pool):
                pool.wait_ge(token_ready, 1)
                for i in range(NPAIR):
                    nc.gpsimd.indirect_dma_start(
                        out=xs[:, i, :], out_offset=None, in_=h_dram,
                        in_offset=bass.IndirectOffsetOnAxis(ap=token_u[:, i:i + 1], axis=0)).then_inc(gathered[i], 16)

            @block.vector
            def _(dve):
                step = Steps(dve, dve_step)
                dve.wait_ge(w_hi, 1)
                split_lo(nc.vector, w_split[:, 1], w[:], w_split[:, 0]).then_inc(w_lo, 1)
                dve.wait_ge(logits_done, 1)
                step(nc.vector.tensor_reduce(top[:], logit_ps[:], AX.X, ALU.max))
                nc.vector.tensor_tensor(logit[:], logit_ps[:], top[:].unsqueeze(2).to_broadcast([P, NT, NE]),
                                        ALU.subtract).then_inc(shift_ready, 1)
                dve.wait_ge(exp_ready, 1)
                step(nc.vector.tensor_reduce(total[:], expd[:], AX.X, ALU.add))
                step(nc.vector.reciprocal(total_inv[:], total[:]))
                nc.vector.tensor_tensor(aff[:], expd[:], total_inv[:].unsqueeze(2).to_broadcast([P, NT, NE]),
                                        ALU.mult).then_inc(aff_ready, 1)
                dve.wait_ge(turned, 1)
                step(nc.vector.tensor_copy(aff_t[:], aff_ps[:]))
                for r in range(CAP // 8):
                    eight = slice(8 * r, 8 * r + 8)
                    step(nc.vector.max(val[:, eight], aff_t[:]))
                    step(nc.vector.max_index(idx[:, eight], val[:, eight], aff_t[:]))
                    if r < CAP // 8 - 1:
                        step(nc.vector.match_replace(aff_t[:], val[:, eight], aff_t[:], -1.0))
                nc.vector.tensor_copy(idx_f[:], idx[:]).then_inc(best_ready, 1)
                dve.wait_ge(relisted, 32)
                nc.vector.tensor_copy(token_u[:], token_f[:]).then_inc(token_ready, 1)


def moe_phase(nc, A, ident, xs_t, token_f, gate, x, pieces):
    SPLIT = 4
    KF = FF // P
    RAW, NCH, HK, DK, UP_PIECES, PIECES = (
        pieces.RAW, pieces.NCH, pieces.HK, pieces.DK, pieces.UP_PIECES, pieces.PIECES)
    raw, loaded = pieces.raw, pieces.loaded
    PER_CHUNK = 4 // DK
    assert PIECES % RAW == 0 and PIECES % SPLIT == 0
    SILU = {4 * n + 4: n for n in range(NCH)}
    HID = {4 * n + 6: n for n in range(NCH)}
    TURN = {4 * n + 6: n for n in range(NCH)}
    HID_SPLIT = {4 * n + 9: n for n in range(NCH)}
    Y_COPY, SPREAD, XS_SPLIT = 2, 3, 19
    SPREAD_DO = {4 + o: o for o in range(8)}
    SPREAD_ADD = {7 + o: o for o in range(8)}
    with Scope(nc, "moe") as s:
        split = s.sb("split", [P, SPLIT, 2, HK * BANK], F32R)
        xs = s.sb("xs", [P, 2, 2, KD, CAP], F32R)
        silu = s.sb("silu", [CAP, 2, BANK])
        hid = s.sb("hid", [P, 2, BANK])
        hid_t = s.sb("hid_t", [P, 2, KF, CAP], F32R)
        y = s.sb("y", [P, D])
        spread = s.sb("spread", [P, T])
        iota = s.sb("iota", [P, T])
        up_ps = s.ps("up_ps", [CAP, 2, 2, BANK])
        turn_ps = s.ps("turn_ps", [P, 2, 4, P])
        y_ps = s.ps("y_ps", [P, 2, BANK])
        (iota_loaded, hi_ready, lo_ready, used, xs_hi, xs_lo, silu_ready, hid_ready, turned, hid_hi, hid_lo,
         y_taken, spread_ready, spread_done, added) = (s.sem(n) for n in (
             "iota_loaded", "hi_ready", "lo_ready", "used", "xs_hi", "xs_lo", "silu_ready", "hid_ready", "turned",
             "hid_hi", "hid_lo", "y_taken", "spread_ready", "spread_done", "added"))

        def pairs(eng, body):
            body(0, True, False)
            with eng.Fori(1, NPAIR - 1) as i:
                body(i, False, False)
            body(NPAIR - 1, False, True)

        def piece_no(i, e, c):
            return i * (2 * PIECES) + (e * PIECES + c)

        def chunk_no(i, e, n):
            return i * (2 * NCH) + (e * NCH + n)

        with nc.Block() as block:
            @block.sync
            def _(sp):
                sp.dma_start(iota[:], rows(A["iota512"], P)).then_inc(iota_loaded, 16)

                def pair(i, first):
                    for e in range(2):
                        for c in range(PIECES):
                            if first and e == 0 and c < RAW:
                                continue
                            sp.wait_ge(lo_ready, piece_no(i, e, c) + 1)
                            pieces.load(sp, i, e, c)

                pair(0, True)
                with sp.Fori(1, NPAIR) as i:
                    pair(i, False)

            @block.tensor
            def _(pe):
                pe.sem_inc(used, SPLIT)
                pe.sem_inc(turned, 2)

                def spread_step(i, o):
                    t, half = o // 2, o % 2
                    if o == 0:
                        pe.wait_ge(spread_ready, i)
                        pe.wait_ge(y_taken, i * 2 + 1)
                    if o >= 2:
                        pe.wait_ge(added, i * 8 + (o - 9))
                    nc.tensor.matmul(y_ps[:, half, :], spread[:, t * P:(t + 1) * P],
                                     y[:, half * BANK:(half + 1) * BANK], start=True,
                                     stop=True).then_inc(spread_done, 1)

                def expert(i, e, first):
                    for c in range(PIECES):
                        q = piece_no(i, e, c)
                        w = split[:, c % SPLIT]
                        if c == 0:
                            pe.wait_ge(xs_lo, i * 2 + (e + 1))
                        if c < UP_PIECES:
                            n, g, half = c // 4, c % 4 // 2, c % 2
                            if c % 4 == 0:
                                pe.wait_ge(hid_ready, chunk_no(i, e, n) + 1)
                            pe.wait_ge(lo_ready, q + (RAW + 1))
                            for k in range(HK):
                                for p, (w_part, x_part) in enumerate(((0, 0), (0, 1), (1, 0))):
                                    last = nc.tensor.matmul(
                                        up_ps[:, n % 2, g, :], xs[:, e, x_part, half * HK + k, :],
                                        w[:, w_part, k * BANK:(k + 1) * BANK],
                                        start=(half == 0 and k == 0 and p == 0),
                                        stop=(half == 1 and k == HK - 1 and p == 2))
                        else:
                            j = c - UP_PIECES
                            if j == 0:
                                pe.wait_ge(y_taken, i * 2 + (e + 1))
                                if e == 0 and not first:
                                    pe.wait_ge(added, i * 8)
                            pe.wait_ge(hid_lo, chunk_no(i, e, j // PER_CHUNK) + 3)
                            pe.wait_ge(lo_ready, q + (RAW + 1))
                            for k in range(DK):
                                for p, (w_part, h_part) in enumerate(((0, 0), (0, 1), (1, 0))):
                                    for half in range(2):
                                        last = nc.tensor.matmul(
                                            y_ps[0:CAP, half, :], hid_t[:, h_part, DK * j + k, :],
                                            w[:, w_part, k * D + half * BANK:k * D + (half + 1) * BANK],
                                            start=(j == 0 and k == 0 and p == 0),
                                            stop=(c == PIECES - 1 and k == DK - 1 and p == 2))
                        last.then_inc(used, 1)
                        if c in TURN:
                            n = TURN[c]
                            pe.wait_ge(hid_ready, chunk_no(i, e, n) + 3)
                            pe.wait_ge(hid_lo, chunk_no(i, e, n) + 1)
                            for j in range(4):
                                last = nc.tensor.transpose(turn_ps[:, n % 2, j, :],
                                                           hid[:, n % 2, j * P:(j + 1) * P], ident[:])
                            last.then_inc(turned, 1)
                        if e == 0 and not first and c in SPREAD_DO:
                            spread_step(i, SPREAD_DO[c])

                def pair(i, first, last):
                    for e in range(2):
                        expert(i, e, first)

                pairs(pe, pair)
                for o in range(8):
                    spread_step(NPAIR, o)

            @block.scalar
            def _(act):
                def copy_y(i, e, first=False):
                    act.wait_ge(used, piece_no(i, e, PIECES - 1) + (SPLIT + 1))
                    if e == 0 and not first:
                        act.wait_ge(spread_done, i * 8)
                    nc.scalar.copy(y[CAP * e:CAP * e + CAP, :],
                                   y_ps[0:CAP].rearrange("p a n -> p (a n)")).then_inc(y_taken, 1)

                def split_xs(i, e):
                    split_hi(nc.scalar, xs[:, e, 0], xs_t[:, bass.ds(i, 1), :, CAP * e:CAP * e + CAP].rearrange(
                        "p a k s -> p (a k) s")).then_inc(xs_hi, 1)

                def pair(i, first, last):
                    for e in range(2):
                        for c in range(PIECES):
                            act.wait_ge(loaded[c % RAW], i * (2 * PIECES // RAW * 16) + ((e * PIECES + c) // RAW + 1) * 16)
                            act.wait_ge(used, piece_no(i, e, c) + 1)
                            split_hi(nc.scalar, split[:, c % SPLIT, 0], raw[:, c % RAW]).then_inc(hi_ready, 1)
                            if c == Y_COPY:
                                if e == 1:
                                    copy_y(i, 0, first)
                                elif not first:
                                    copy_y(i - 1, 1)
                            if c in SILU:
                                n = SILU[c]
                                act.wait_ge(used, piece_no(i, e, 4 * n + 1) + (SPLIT + 1))
                                act.wait_ge(hid_ready, chunk_no(i, e, n) + 1)
                                nc.scalar.activation(silu[:, n % 2, :], up_ps[:, n % 2, 0, :],
                                                     ACT.Silu).then_inc(silu_ready, 1)
                            if c in HID_SPLIT:
                                n = HID_SPLIT[c]
                                act.wait_ge(turned, chunk_no(i, e, n) + 3)
                                split_hi(nc.scalar, hid_t[:, 0, 4 * n:4 * n + 4, :],
                                         turn_ps[:, n % 2, :, 0:CAP]).then_inc(hid_hi, 1)
                            if c == XS_SPLIT and not (last and e == 1):
                                split_xs(i + e, 1 - e)

                act.sem_inc(y_taken, 1)
                split_xs(0, 0)
                pairs(act, pair)
                copy_y(NPAIR - 1, 1)

            @block.vector
            def _(dve):
                def add_part(i, o):
                    part = x[:, o // 2, (o % 2) * BANK:(o % 2 + 1) * BANK]
                    dve.wait_ge(spread_done, i * 8 + (o - 7))
                    nc.vector.tensor_tensor(part, y_ps[:, o % 2, :], part, ALU.add).then_inc(added, 1)

                def build_spread(i):
                    nc.vector.tensor_scalar(spread[:], iota[:], token_f[:, bass.ds(i, 1)], gate[:, bass.ds(i, 1)],
                                            ALU.is_equal, ALU.mult).then_inc(spread_ready, 1)

                def split_xs(i, e, n):
                    dve.wait_ge(xs_hi, n)
                    split_lo(nc.vector, xs[:, e, 1], xs_t[:, bass.ds(i, 1), :, CAP * e:CAP * e + CAP].rearrange(
                        "p a k s -> p (a k) s"), xs[:, e, 0]).then_inc(xs_lo, 1)

                def pair(i, first, last):
                    for e in range(2):
                        for c in range(PIECES):
                            dve.wait_ge(hi_ready, piece_no(i, e, c) + 1)
                            split_lo(nc.vector, split[:, c % SPLIT, 1], raw[:, c % RAW],
                                     split[:, c % SPLIT, 0]).then_inc(lo_ready, 1)
                            if e == 0 and not first:
                                if c == SPREAD:
                                    build_spread(i - 1)
                                if c in SPREAD_ADD:
                                    add_part(i, SPREAD_ADD[c])
                            if c in HID:
                                n = HID[c]
                                dve.wait_ge(silu_ready, chunk_no(i, e, n) + 1)
                                dve.wait_ge(used, piece_no(i, e, 4 * n + 3) + (SPLIT + 1))
                                dve.wait_ge(turned, chunk_no(i, e, n) + 1)
                                nc.vector.tensor_tensor(hid[0:CAP, n % 2, :], silu[:, n % 2, :], up_ps[:, n % 2, 1, :],
                                                        ALU.mult).then_inc(hid_ready, 1)
                            if c in HID_SPLIT:
                                n = HID_SPLIT[c]
                                dve.wait_ge(hid_hi, chunk_no(i, e, n) + 1)
                                split_lo(nc.vector, hid_t[:, 1, 4 * n:4 * n + 4, :], turn_ps[:, n % 2, :, 0:CAP],
                                         hid_t[:, 0, 4 * n:4 * n + 4, :]).then_inc(hid_lo, 1)
                            if c == XS_SPLIT and not (last and e == 1):
                                split_xs(i + e, 1 - e, i * 2 + (e + 2))

                dve.sem_inc(lo_ready, RAW)
                dve.sem_inc(hid_ready, 2)
                dve.sem_inc(hid_lo, 2)
                nc.vector.memset(hid[CAP:P], 0.0)
                split_xs(0, 0, 1)
                dve.wait_ge(iota_loaded, 16)
                pairs(dve, pair)
                build_spread(NPAIR - 1)
                for o in range(8):
                    add_part(NPAIR, o)



def program(nc, A, out, taps=None):
    taps = taps or {}

    def tap(name, buf):
        if name in taps:
            with Scope(nc, "tap" + name) as s:
                done = s.sem("done")
                with nc.Block() as block:
                    @block.sync
                    def _(sp):
                        sp.dma_start(taps[name], buf[:].bitcast(F32)).then_inc(done, 16)
                        sp.wait_ge(done, 16)

    h_dram = nc.dram_tensor("h_rows", (T, D), F32, kind="Internal").ap()
    dots_dram = nc.dram_tensor("expert_dots", (ETILES, P, T), F32, kind="Internal").ap()
    weight_dram = nc.dram_tensor("expert_weights", (SPANS, NKEY, NKEY, SPAN), F32, kind="Internal").ap()
    gate_dram = nc.dram_tensor("gate_list", (NE, CAP), F32, kind="Internal").ap()
    token_dram = nc.dram_tensor("token_list", (NE, CAP), F32, kind="Internal").ap()

    with Scope(nc, "all") as g:
        x = g.sb("x", [P, NT, D])
        ident = g.sb("ident", [P, P])
        halves = g.sb("halves", [P, P])
        ones = g.sb("ones", [P, P])
        with Scope(nc, "one") as b1:
            gate2 = b1.sb("gate2", [P, D])
            acts = b1.sb("acts", [P, 2, KD, T], F32R)
            with Scope(nc, "adas") as b0:
                ada = b0.sb("ada", [P, 6, D])
                shift1, scale1, gate1, shift2, scale2 = (ada[:, i, :] for i in range(5))
                ada_phase(nc, A, ada, ((ident[:], A["ident"]), (halves[:], A["halves"]),
                                       (x[:], A["x"][0].rearrange("(t p) d -> p t d", p=P))), ones)
                tap("ada", ada)
                with nc.Block() as block:
                    @block.scalar
                    def _(act):
                        nc.scalar.copy(gate2[:], ada[:, 5, :])
                norm_phase(nc, "n1", ident, x, A["norm1_g"], scale=scale1, shift=shift1, to_t=acts)
                tap("h_t", acts)
                with Scope(nc, "mixin") as mi:
                    feat = mi.sb("feat", [P, 18, T])
                    values = mi.sb("values", [P, NT, P])
                    first_projection(nc, A, acts, feat, values)
                    tap("feat", feat)
                    with Scope(nc, "cv") as c:
                        conv_y = c.sb("conv_y", [P, 4, T])
                        gain = c.sb("gain", [P, 4])
                        load_columns(nc, "cg", gain, A["conv_out_g_col"])
                        gated_conv_phase(nc, A, feat, conv_y)
                        column_norm_phase(nc, "cn", [[(conv_y[:, i, :], gain[:, i:i + 1], 4 + i)] for i in range(4)],
                                          halves[:], DH, acts)
                    with Scope(nc, "a1") as a:
                        attn = a.sb("attn", [P, NT, NH * DH])
                        first_attention(nc, A, ident, feat, values, attn)
                        tap("attn", attn)
                        norm_phase(nc, "an", ident, attn, A["attn_out_g"], width=NH * DH, groups=NH, to_t=acts)
                tap("mix_t", acts)
                out_projection(nc, "out1", A["w_out"], acts, x, A["b_out"], gate1)
                tap("x1", x)
                norm_phase(nc, "n2", ident, x, A["norm2_g"], scale=scale2, shift=shift2, to_t=acts)
            with Scope(nc, "pe") as p:
                choice = p.sb("choice", [P, 3, NT, P])
                score = p.sb("score", [P, NT, NC, NKEY])
                with Scope(nc, "q") as q:
                    query_t = q.sb("query_t", [P, NC, T])
                    query_projection(nc, A, acts, query_t)
                    peer_score_phase(nc, A, query_t, score)
                with Scope(nc, "dots") as d:
                    dots = ExpertDots(nc, d, A, acts, dots_dram)
                    peer_choice_phase(nc, A, dots, score, choice)
                    tap("choice", choice)
                    peer_weight_phase(nc, A, ident, dots, choice, weight_dram)
            peer_value_phase(nc, A, dots_dram, weight_dram, x, gate2[:])
            norm_phase(nc, "nf", ident, x, A["final_g"], keep=x)
            tap("x2", x)

        with Scope(nc, "two") as b2:
            acts = b2.sb("acts", [P, 2, KD, T], F32R)
            norm_phase(nc, "n3", ident, x, A["norm1_g_2"][0], to_t=acts)
            gain = b2.sb("gain", [P, KD])
            load_columns(nc, "mg", gain, A["mix_norm_g_col"])
            feat = b2.sb("feat", [P, 16, T])
            values = b2.sb("values", [P, NT, NA])
            second_projection(nc, A, acts, feat, values)
            tap("feat2", feat)
            with Scope(nc, "hy") as hy:
                hy_y = hy.sb("hy_y", [P, 2, T])
                pool_y = hy.sb("pool_y", [P, 2, T])
                pool_phase(nc, A, feat, pool_y)
                tap("pool_y", pool_y)
                with Scope(nc, "ev") as ev:
                    even, odd = ev.sb("even", [P, NT, HY]), ev.sb("odd", [P, NT, HY])
                    filter_phase(nc, A, even, odd)
                    tap("even", even)
                    hyena_phase(nc, A, ident, feat, even, odd, hy_y)
                    tap("hy_y", hy_y)
                column_norm_phase(nc, "hn", [
                    [(y[:, i, :], gain[:, c + i:c + i + 1], c + i) for i in range(2)]
                    for y, c in ((hy_y, 0), (pool_y, 6))], ones[:], HY, acts)
            with Scope(nc, "a2") as a:
                attn = a.sb("attn", [P, NT, NA])
                with Scope(nc, "bt") as bt:
                    table = bt.sb("table", [P, NH, 16 * 64])
                    bias_table_phase(nc, A, table)
                    second_attention(nc, A, ident, feat, values, table, attn)
                tap("attn2", attn)
                norm_phase(nc, "an2", ident, attn, A["mix_norm_g_2"][0, HY:HY + NA], width=NA, to_t=acts, t_chunk0=2)
            tap("mix_t2", acts)
            out_projection(nc, "out2", A["w_out_2"][0], acts, x)
        tap("x3", x)
        xs_t = g.sb("xs_t", [P, NPAIR, KD, P])
        token_f, gate = g.sb("token_f", [P, NPAIR]), g.sb("gate", [P, NPAIR])
        pieces = ExpertPieces(nc, g, A)
        with Scope(nc, "ro") as r:
            acts = r.sb("acts", [P, 2, KD, T], F32R)
            norm_phase(nc, "n4", ident, x, A["norm2_g_2"][0], to_t=acts, out_dram=h_dram)
            router_phase(nc, A, ident, acts, h_dram, gate_dram, token_dram, xs_t, token_f, gate, pieces)
        tap("token_f", token_f)
        tap("gate", gate)
        moe_phase(nc, A, ident, xs_t, token_f, gate, x, pieces)
        tap("x4", x)
        norm_phase(nc, "no", ident, x, A["final_g_2"], out_dram=out[0])


def load_columns(nc, name, dst, columns_dram):
    with Scope(nc, name) as s:
        loaded = s.sem("loaded")
        with nc.Block() as block:
            @block.sync
            def _(sp):
                sp.dma_start(dst[:], columns_dram).then_inc(loaded, 16)
                sp.wait_ge(loaded, 16)



def shape_tables():
    f = np.float32
    c = {}
    c["ident"] = np.eye(P, dtype=f)
    half = np.arange(P) // 64
    c["halves"] = (half[:, None] == half[None, :]).astype(f)
    c["iota"] = np.arange(NKEY).astype(f)
    c["iota512"] = np.arange(T).astype(f)
    q, k = np.arange(P)[:, None], np.arange(2 * P)[None, :]
    diff = q + P - k
    c["window_mask"] = np.where((diff >= 0) & (diff < P), 0.0, NEG).astype(f)
    bands = (FE - 1) // 2
    t = np.linspace(0.0, 1.0, T, dtype=f)[:, None].astype(np.float64)
    ang = (f(TWO_PI) * np.arange(T, dtype=f)[:, None] / f(T)).astype(f)
    band = np.linspace(1e-4, bands - 1, bands, dtype=f)[None, :]
    turn = (band * ang).astype(f).astype(np.float64)
    c["pos_t"] = np.ascontiguousarray(np.concatenate([t, np.cos(turn), -np.sin(turn)], -1).T.astype(f))
    lo, hi = np.log(1e-2) / 0.3, np.log(1e-2) / 1.5
    decay = np.exp(-t * np.abs(np.linspace(lo, hi, HY, dtype=f)).astype(np.float64))
    back = decay.copy()
    back[0] = 0.0
    c["decay"] = np.concatenate([decay, back], -1).astype(f)
    turn = np.pi * ((2 * np.arange(T)[None, :] + 1) * np.arange(T)[:, None] % (4 * T)) / (2 * T)
    c["dft_cos"], c["dft_sin"] = np.cos(turn).astype(f), np.sin(turn).astype(f)
    c["dft_cos_t"] = np.ascontiguousarray(c["dft_cos"].T)
    c["dft_sin_t"] = np.ascontiguousarray(c["dft_sin"].T)
    at = np.arange(T)
    c["pool_inv"] = np.stack([1.0 / (np.clip(at + w // 2, 0, T) - np.clip(at - w // 2, 0, T))
                              for w in (2, 4, 8, 16)]).astype(f)
    j, col = np.arange(64)[:, None], (np.arange(P) % 64)[None, :]
    start = np.clip(col - 8, 0, 48)
    inside = (j >= start) & (j < start + 16)
    pick = np.zeros((32, 64, P), f)
    for dc in range(31):
        pick[dc] = inside & (j - col + 15 == dc)
    pick[31] = np.where(inside, 0.0, NEG)
    c["bias_pick"] = pick
    return c


PLAIN = ["x", "w_ada", "b_ada", "norm1_g", "w_in", "b_in", "attn_sinks", "attn_out_g", "w_out",
         "b_out", "norm2_g", "w_query", "peer_v", "final_g", "norm1_g_2", "w_in_2", "hy_f_w1_2",
         "hy_f_b1_2", "hy_f_w2_2", "hy_f_b2_2", "hy_f_wout_2", "hy_f_freq_2", "pool_w_2",
         "mix_norm_g_2", "w_out_2", "norm2_g_2", "w_router_2", "w_gate_2", "w_up_2", "w_down_2",
         "final_g_2"]


def laid_out(inputs):
    a = {n: np.ascontiguousarray(inputs[n]) for n in PLAIN}
    u = np.asarray(inputs["peer_u"]).reshape(ETILES, P, KD, P)
    a["u_tiles"] = np.ascontiguousarray(u.transpose(0, 3, 2, 1))
    for i in (1, 2):
        a[f"keys_t{i}"] = np.ascontiguousarray(np.asarray(inputs[f"peer_keys{i}"]).transpose(2, 0, 1))
    a["rpb_t"] = np.ascontiguousarray(np.asarray(inputs["na_rpb_2"])[0].transpose(2, 0, 1).reshape(31, NH * 15))
    for n, name in (("c", "c"), ("b_in", "b_in"), ("conv_w", "conv_w"), ("conv_out_g", "conv_out_g"),
                    ("hy_short_w", "hy_short_w_2"), ("hy_short_b", "hy_short_b_2"), ("hy_skip", "hy_skip_2"),
                    ("pool_scale", "pool_scale_2"), ("mix_norm_g", "mix_norm_g_2")):
        v = np.asarray(inputs[name])
        v = v.reshape(v.shape[-2:] if n in ("conv_w", "hy_short_w") else (1, -1))
        v = v.reshape(v.shape[0], -1, P).transpose(2, 1, 0)
        a[f"{n}_col"] = np.ascontiguousarray(v if v.shape[2] > 1 else v[:, :, 0])
    a.update(shape_tables())
    return a


def kernel(**inputs):
    import concourse.bacc as bacc
    from concourse.bass_utils import run_bass_kernel_spmd

    nc = bacc.Bacc("TRN2", target_bir_lowering=False, num_devices=1)
    arrays = {f"in_{n}": a for n, a in laid_out(inputs).items()}
    aps = {n[3:]: nc.dram_tensor(n, a.shape, mybir.dt.from_np(a.dtype), kind="ExternalInput").ap()
           for n, a in arrays.items()}
    out = nc.dram_tensor("out", (1, T, D), F32, kind="ExternalOutput").ap()
    program(nc, aps, out)
    r = run_bass_kernel_spmd(nc, [arrays], core_ids=[0])
    return r.results[0]["out"]
```
